# Optimizing a Trainium2 kernel written in Bass

```python
import jax, jax.numpy as jnp
from jax import lax
import numpy as np

D_MODEL = 1024
BATCH = 1
SEQ = 512
DEPTH = 1

HG_HEADS = 8
HG_DK = 128
HG_DV = 128
HG_CHUNK = 64
RET_HEADS = 4
RET_DK = 256
RET_DV = 512
RET_CHUNK = 128
ROPE_BASE = 10000.0
PEER_HEADS = 8
PEER_NKEYS = 128
PEER_N_EXPERTS = PEER_NKEYS * PEER_NKEYS
PEER_QDIM = 256
PEER_HALF = PEER_QDIM // 2
PEER_TOPK = 16
PEER_BLOCK = 128
NORM_EPS = 1e-6

IN_SIZES = (HG_HEADS * HG_DK, HG_HEADS * HG_DK, HG_HEADS * HG_DV, HG_HEADS * HG_DV,
            RET_HEADS * RET_DK, RET_HEADS * RET_DK, RET_HEADS * RET_DV, RET_HEADS * RET_DV,
            D_MODEL, D_MODEL)
IN_WIDTH = (2 * HG_HEADS * HG_DK + 2 * HG_HEADS * HG_DV + 2 * RET_HEADS * RET_DK
            + 2 * RET_HEADS * RET_DV + 2 * D_MODEL)


def rmsnorm(x, w):
    xf = x.astype(jnp.float32)
    y = xf * lax.rsqrt(jnp.mean(xf * xf, axis=-1, keepdims=True) + NORM_EPS)
    return (y * w.astype(jnp.float32)).astype(x.dtype)

def head_rms(x):
    return x * lax.rsqrt(jnp.mean(x * x, axis=-1, keepdims=True) + NORM_EPS)

def split_cols(t, sizes):
    outs, start = [], 0
    for n in sizes:
        outs.append(t[..., start:start + n])
        start += n
    return outs

def to_chunks(t, chunk):
    B, S, H, d = t.shape
    return t.reshape(B, S // chunk, chunk, H, d).transpose(1, 0, 3, 2, 4)

def from_chunks(t):
    nc, B, H, C, d = t.shape
    return t.transpose(1, 0, 3, 2, 4).reshape(B, nc * C, H, d)

def hgrn2_mix(q, f_logit, i, lb):
    B, S, _ = q.shape
    f = lb + (1.0 - lb) * jax.nn.sigmoid(f_logit)
    k = 1.0 - f
    logf = jnp.log(f)
    qc = to_chunks((q * HG_DK ** -0.5).reshape(B, S, HG_HEADS, HG_DK), HG_CHUNK)
    kc = to_chunks(k.reshape(B, S, HG_HEADS, HG_DK), HG_CHUNK)
    gc = to_chunks(logf.reshape(B, S, HG_HEADS, HG_DK), HG_CHUNK)
    vc = to_chunks(i.reshape(B, S, HG_HEADS, HG_DV), HG_CHUNK)
    causal = jnp.tril(jnp.ones((HG_CHUNK, HG_CHUNK), dtype=bool))

    def step(state, inp):
        qb, kb, gb, vb = inp
        b = jnp.cumsum(gb, axis=2)
        diff = b[:, :, :, None, :] - b[:, :, None, :, :]
        decay = jnp.exp(jnp.where(causal[:, :, None], diff, -jnp.inf))
        a = jnp.einsum('bhtd,bhsd,bhtsd->bhts', qb, kb, decay)
        o = (jnp.einsum('bhts,bhsv->bhtv', a, vb)
             + jnp.einsum('bhtd,bhdv->bhtv', qb * jnp.exp(b), state))
        b_last = b[:, :, -1:, :]
        state = (jnp.exp(b_last[:, :, 0, :])[..., None] * state
                 + jnp.einsum('bhsd,bhsv->bhdv', kb * jnp.exp(b_last - b), vb))
        return state, o

    s0 = jnp.zeros((B, HG_HEADS, HG_DK, HG_DV), jnp.float32)
    _, o = lax.scan(step, s0, (qc, kc, gc, vc))
    return from_chunks(o)

def rotary(x, pos):
    half = x.shape[-1] // 2
    inv = ROPE_BASE ** (-jnp.arange(half, dtype=jnp.float32) / half)
    ang = pos[:, None] * inv[None, :]
    cos = jnp.cos(ang)[None, :, None, :]
    sin = jnp.sin(ang)[None, :, None, :]
    x1, x2 = x[..., :half], x[..., half:]
    return jnp.concatenate([x1 * cos - x2 * sin, x1 * sin + x2 * cos], axis=-1)

def retention_mix(q, k, v):
    C = RET_CHUNK
    log_g = jnp.log(1.0 - jnp.exp2(-5.0 - jnp.arange(RET_HEADS, dtype=jnp.float32)))
    idx = jnp.arange(C, dtype=jnp.float32)
    rel = idx[:, None] - idx[None, :]
    dmask = jnp.where(rel >= 0, jnp.exp(log_g[:, None, None] * jnp.maximum(rel, 0.0)), 0.0)
    q_decay = jnp.exp(log_g[:, None] * (idx + 1.0))[None, :, :, None]
    k_decay = jnp.exp(log_g[:, None] * (C - 1.0 - idx))[None, :, :, None]
    chunk_decay = jnp.exp(log_g * C)[None, :, None, None]
    qc, kc, vc = to_chunks(q, C), to_chunks(k, C), to_chunks(v, C)

    def step(state, inp):
        qb, kb, vb = inp
        a = jnp.einsum('bhtd,bhsd->bhts', qb, kb) * dmask[None]
        o = (jnp.einsum('bhts,bhsv->bhtv', a, vb)
             + jnp.einsum('bhtd,bhdv->bhtv', qb * q_decay, state))
        state = chunk_decay * state + jnp.einsum('bhsd,bhsv->bhdv', kb * k_decay, vb)
        return state, o

    B = q.shape[0]
    s0 = jnp.zeros((B, RET_HEADS, RET_DK, RET_DV), jnp.float32)
    _, o = lax.scan(step, s0, (qc, kc, vc))
    return from_chunks(o)

def peer_ffn(h, w_q, sub_keys, expert_u, expert_v):
    B, S, D = h.shape
    T = B * S
    ht = h.reshape(T, D)
    q = (ht @ w_q).astype(jnp.float32).reshape(T, PEER_HEADS, 2, PEER_HALF)
    s = jnp.einsum('thpd,hpkd->thpk', q, sub_keys.astype(jnp.float32))
    top_s, top_i = lax.top_k(s, PEER_TOPK)
    cand = top_s[:, :, 0, :, None] + top_s[:, :, 1, None, :]
    cand_idx = top_i[:, :, 0, :, None] * PEER_NKEYS + top_i[:, :, 1, None, :]
    best_s, best_c = lax.top_k(cand.reshape(T, PEER_HEADS, PEER_TOPK * PEER_TOPK), PEER_TOPK)
    expert_idx = jnp.take_along_axis(
        cand_idx.reshape(T, PEER_HEADS, PEER_TOPK * PEER_TOPK), best_c, axis=-1)
    gates = jax.nn.softmax(best_s, axis=-1)
    nb = T // PEER_BLOCK

    def block_fn(args):
        xb, ib, gb = args
        u = jnp.take(expert_u, ib, axis=0)
        act = jax.nn.gelu(jnp.einsum('td,thkd->thk', xb, u).astype(jnp.float32))
        w = (gb * act).astype(xb.dtype)
        v = jnp.take(expert_v, ib, axis=0)
        return jnp.einsum('thk,thkd->td', w, v)

    out = lax.map(block_fn, (ht.reshape(nb, PEER_BLOCK, D),
                             expert_idx.reshape(nb, PEER_BLOCK, PEER_HEADS, PEER_TOPK),
                             gates.reshape(nb, PEER_BLOCK, PEER_HEADS, PEER_TOPK)))
    return out.reshape(B, S, D)

def first_inputs(seed: int = 0) -> dict:
    key = jax.random.key(seed)
    ks = jax.random.split(key, 14)
    f32 = jnp.float32

    def nrm(k, shape, scale):
        return jax.random.normal(k, shape, f32) * scale

    return {
        "x": nrm(ks[0], (BATCH, SEQ, D_MODEL), 1.0),
        "norm_mix_w": 1.0 + nrm(ks[1], (DEPTH, D_MODEL), 0.02),
        "w_in": nrm(ks[2], (DEPTH, D_MODEL, IN_WIDTH), D_MODEL ** -0.5),
        "hg_lower_bounds": nrm(ks[3], (DEPTH + 1, HG_HEADS * HG_DK), 0.1),
        "hg_norm_w": 1.0 + nrm(ks[4], (DEPTH, HG_HEADS * HG_DV), 0.02),
        "w_branch_hg": nrm(ks[5], (DEPTH, HG_HEADS * HG_DV, D_MODEL), (HG_HEADS * HG_DV) ** -0.5),
        "w_branch_ret": nrm(ks[6], (DEPTH, RET_HEADS * RET_DV, D_MODEL), (RET_HEADS * RET_DV) ** -0.5),
        "w_out": nrm(ks[7], (DEPTH, D_MODEL, D_MODEL), D_MODEL ** -0.5),
        "norm_ffn_w": 1.0 + nrm(ks[8], (DEPTH, D_MODEL), 0.02),
        "peer_w_q": nrm(ks[9], (DEPTH, D_MODEL, PEER_HEADS * PEER_QDIM), D_MODEL ** -0.5),
        "peer_sub_keys": nrm(ks[10], (DEPTH, PEER_HEADS, 2, PEER_NKEYS, PEER_HALF), PEER_HALF ** -0.5),
        "expert_u": nrm(ks[11], (DEPTH, PEER_N_EXPERTS, D_MODEL), D_MODEL ** -0.5),
        "expert_v": nrm(ks[12], (DEPTH, PEER_N_EXPERTS, D_MODEL), PEER_HEADS ** -0.5),
        "final_norm_w": 1.0 + nrm(ks[13], (D_MODEL,), 0.02),
    }

def first_block(x, norm_mix_w, w_in, hg_lower_bounds, hg_norm_w, w_branch_hg, w_branch_ret,
              w_out, norm_ffn_w, peer_w_q, peer_sub_keys, expert_u, expert_v, final_norm_w):
    B, S, _ = x.shape
    f32 = jnp.float32
    lbs = jnp.cumsum(jax.nn.softmax(hg_lower_bounds.astype(f32), axis=0), axis=0)
    pos = jnp.arange(S, dtype=f32)
    for l in range(DEPTH):
        h = rmsnorm(x, norm_mix_w[l])
        proj = h @ w_in[l]
        hq, hf, hi, hg, rq, rk, rv, rg, gate_a, gate_b = split_cols(proj, IN_SIZES)

        o_hg = hgrn2_mix(hq.astype(f32), hf.astype(f32), hi.astype(f32), lbs[l])
        o_hg = (head_rms(o_hg).reshape(B, S, HG_HEADS * HG_DV) * hg_norm_w[l].astype(f32)
                * jax.nn.silu(hg.astype(f32)))

        q = rotary(rq.astype(f32).reshape(B, S, RET_HEADS, RET_DK), pos)
        k = rotary(rk.astype(f32).reshape(B, S, RET_HEADS, RET_DK), pos) * RET_DK ** -0.5
        v = rv.astype(f32).reshape(B, S, RET_HEADS, RET_DV)
        o_ret = retention_mix(q, k, v)
        o_ret = head_rms(o_ret).reshape(B, S, RET_HEADS * RET_DV) * jax.nn.silu(rg.astype(f32))

        y_hg = o_hg.astype(x.dtype) @ w_branch_hg[l]
        y_ret = o_ret.astype(x.dtype) @ w_branch_ret[l]
        merged = jax.nn.sigmoid(gate_a) * y_hg + jax.nn.sigmoid(gate_b) * y_ret
        x = x + merged @ w_out[l]

        h = rmsnorm(x, norm_ffn_w[l])
        x = x + peer_ffn(h, peer_w_q[l], peer_sub_keys[l], expert_u[l], expert_v[l])
    return rmsnorm(x, final_norm_w)


CHUNK = 64
Q_BLOCK = 128
MIX = D_MODEL
W_LRU = MIX // 2
LRU_BLOCKS = 8
LRU_BW = W_LRU // LRU_BLOCKS
LRU_C = 8.0
CONV_A = 4
SB_HEADS = 4
SB_DH = MIX // 4 // SB_HEADS
SB_W = SB_HEADS * SB_DH
DF_HEADS = 4
DF_DV = MIX // 4 // DF_HEADS
DF_DQK = DF_DV // 2
DF_W = DF_HEADS * DF_DV
D_FF = ((8 * D_MODEL // 3 + 255) // 256) * 256
CONV_FF = 3
EPS = 1e-6
IN_SIZES_2 = [W_LRU, W_LRU, SB_W, SB_W, SB_W, DF_W, DF_W, DF_W]
P_IN = sum(IN_SIZES_2)


def rmsnorm_2(x, g):
    xf = x.astype(jnp.float32)
    y = xf * lax.rsqrt(jnp.mean(xf * xf, axis=-1, keepdims=True) + EPS)
    return (y * g.astype(jnp.float32)).astype(x.dtype)

def causal_dwconv(x, w, b):
    k = w.shape[0]
    y = lax.conv_general_dilated(
        x, w[:, None, :], window_strides=(1,), padding=[(k - 1, 0)],
        dimension_numbers=('NWC', 'WIO', 'NWC'), feature_group_count=x.shape[-1])
    return y + b

def rg_lru(xa, w_r, b_r, w_i, b_i, lam):
    bn, s, c = xa.shape
    xb = xa.reshape(bn, s, LRU_BLOCKS, LRU_BW)
    r = jax.nn.sigmoid((jnp.einsum('bsnc,ncd->bsnd', xb, w_r).reshape(bn, s, c) + b_r).astype(jnp.float32))
    i = jax.nn.sigmoid((jnp.einsum('bsnc,ncd->bsnd', xb, w_i).reshape(bn, s, c) + b_i).astype(jnp.float32))
    log_a = -LRU_C * r * jax.nn.softplus(-lam.astype(jnp.float32))
    a = jnp.exp(log_a)
    u = jnp.sqrt(-jnp.expm1(2.0 * log_a)) * (i * xa.astype(jnp.float32))

    def combine(left, right):
        a1, b1 = left
        a2, b2 = right
        return a1 * a2, a2 * b1 + b2

    _, h = lax.associative_scan(combine, (a, u), axis=1)
    return h.astype(xa.dtype)

def to_heads(t, n_heads):
    bn, s, w = t.shape
    return t.reshape(bn, s, n_heads, w // n_heads).transpose(0, 2, 1, 3)

def from_blocks(o):
    nb, bn, h, qb, dh = o.shape
    return o.transpose(1, 0, 3, 2, 4).reshape(bn, nb * qb, h, dh)

def stick_breaking(q, k, v):
    s_len = q.shape[2]
    scale = SB_DH ** -0.5
    spos = jnp.arange(s_len)

    def block(start):
        qb = lax.dynamic_slice_in_dim(q, start, Q_BLOCK, axis=2)
        tpos = start + jnp.arange(Q_BLOCK)
        earlier = spos[None, :] < tpos[:, None]
        z = jnp.einsum('bhqd,bhkd->bhqk', qb, k).astype(jnp.float32) * scale
        log_1m = jnp.where(earlier, jax.nn.log_sigmoid(-z), 0.0)
        tail = lax.cumsum(log_1m, axis=3, reverse=True) - log_1m
        wts = jnp.where(earlier, jnp.exp(jax.nn.log_sigmoid(z) + tail), 0.0)
        return jnp.einsum('bhqk,bhkd->bhqd', wts.astype(v.dtype), v)

    starts = jnp.arange(s_len // Q_BLOCK, dtype=jnp.int32) * Q_BLOCK
    o = from_blocks(lax.map(block, starts))
    return o.reshape(o.shape[0], s_len, SB_W)

def diff_attention(q, k, v, lam, lam_init, g_sub):
    s_len = q.shape[2]
    scale = DF_DQK ** -0.5
    q1, q2 = q[..., :DF_DQK], q[..., DF_DQK:]
    k1, k2 = k[..., :DF_DQK], k[..., DF_DQK:]
    slopes = 2.0 ** (-8.0 * (jnp.arange(DF_HEADS, dtype=jnp.float32) + 1.0) / DF_HEADS)
    spos = jnp.arange(s_len)

    def block(start):
        qb1 = lax.dynamic_slice_in_dim(q1, start, Q_BLOCK, axis=2)
        qb2 = lax.dynamic_slice_in_dim(q2, start, Q_BLOCK, axis=2)
        tpos = start + jnp.arange(Q_BLOCK)
        allowed = (spos[None, :] // CHUNK) <= (tpos[:, None] // CHUNK)
        dist = jnp.abs(tpos[:, None] - spos[None, :]).astype(jnp.float32)
        bias = -slopes[:, None, None] * dist

        def probs(qb, kk):
            sc = jnp.einsum('bhqd,bhkd->bhqk', qb, kk).astype(jnp.float32) * scale + bias
            return jax.nn.softmax(jnp.where(allowed, sc, -jnp.inf), axis=-1)

        p = probs(qb1, k1) - lam * probs(qb2, k2)
        return jnp.einsum('bhqk,bhkd->bhqd', p.astype(v.dtype), v)

    starts = jnp.arange(s_len // Q_BLOCK, dtype=jnp.int32) * Q_BLOCK
    o = from_blocks(lax.map(block, starts))
    o = rmsnorm_2(o, g_sub) * (1.0 - lam_init)
    return o.reshape(o.shape[0], s_len, DF_W)

def second_inputs(seed: int = 0) -> dict:
    key = jax.random.key(seed)
    ks = jax.random.split(key, 24)
    f32 = jnp.float32

    def nrm(k, shape, fan_in):
        return jax.random.normal(k, shape, f32) * (fan_in ** -0.5)

    def gain(k, shape):
        return 1.0 + 0.02 * jax.random.normal(k, shape, f32)

    def small(k, shape):
        return 0.01 * jax.random.normal(k, shape, f32)

    a_c = jax.random.uniform(ks[8], (DEPTH, W_LRU), f32, minval=0.9, maxval=0.999)
    a_base = a_c ** (1.0 / LRU_C)
    return {
        'x': jax.random.normal(ks[0], (BATCH, SEQ, D_MODEL), f32),
        'norm1_g': gain(ks[1], (DEPTH, D_MODEL)),
        'w_in': nrm(ks[2], (DEPTH, D_MODEL, P_IN), D_MODEL),
        'conv_a_w': nrm(ks[3], (DEPTH, CONV_A, W_LRU), CONV_A),
        'conv_a_b': small(ks[4], (DEPTH, W_LRU)),
        'w_rgate': nrm(ks[5], (DEPTH, LRU_BLOCKS, LRU_BW, LRU_BW), LRU_BW),
        'b_rgate': small(ks[6], (DEPTH, W_LRU)),
        'w_igate': nrm(ks[7], (DEPTH, LRU_BLOCKS, LRU_BW, LRU_BW), LRU_BW),
        'b_igate': small(ks[9], (DEPTH, W_LRU)),
        'lru_lambda': jnp.log(a_base) - jnp.log1p(-a_base),
        'lam_q1': 0.1 * jax.random.normal(ks[10], (DEPTH, DF_DQK), f32),
        'lam_k1': 0.1 * jax.random.normal(ks[11], (DEPTH, DF_DQK), f32),
        'lam_q2': 0.1 * jax.random.normal(ks[12], (DEPTH, DF_DQK), f32),
        'lam_k2': 0.1 * jax.random.normal(ks[13], (DEPTH, DF_DQK), f32),
        'subln_g': gain(ks[14], (DEPTH, DF_DV)),
        'w_out': nrm(ks[15], (DEPTH, MIX, D_MODEL), MIX),
        'norm2_g': gain(ks[16], (DEPTH, D_MODEL)),
        'w_ff_up': nrm(ks[17], (DEPTH, D_MODEL, 2 * D_FF), D_MODEL),
        'conv_ff_w': nrm(ks[18], (DEPTH, CONV_FF, 2 * D_FF), CONV_FF),
        'conv_ff_b': small(ks[19], (DEPTH, 2 * D_FF)),
        'w_ff_down': nrm(ks[20], (DEPTH, D_FF, D_MODEL), D_FF),
        'final_g': gain(ks[21], (D_MODEL,)),
    }

def second_block(x, norm1_g, w_in, conv_a_w, conv_a_b, w_rgate, b_rgate, w_igate, b_igate,
              lru_lambda, lam_q1, lam_k1, lam_q2, lam_k2, subln_g, w_out, norm2_g,
              w_ff_up, conv_ff_w, conv_ff_b, w_ff_down, final_g):
    split_at = np.cumsum(IN_SIZES_2)[:-1].tolist()
    for l in range(DEPTH):
        h = rmsnorm_2(x, norm1_g[l])
        proj = h @ w_in[l]
        xa, ya, sq, sk, sv, dq, dk, dv = jnp.split(proj, split_at, axis=-1)

        xa = causal_dwconv(xa, conv_a_w[l], conv_a_b[l])
        out_a = rg_lru(xa, w_rgate[l], b_rgate[l], w_igate[l], b_igate[l], lru_lambda[l]) * jax.nn.gelu(ya)

        out_b = stick_breaking(to_heads(sq, SB_HEADS), to_heads(sk, SB_HEADS), to_heads(sv, SB_HEADS))

        lam_init = 0.8 - 0.6 * float(np.exp(-0.3 * l))
        lam = (jnp.exp(jnp.sum(lam_q1[l] * lam_k1[l]).astype(jnp.float32))
               - jnp.exp(jnp.sum(lam_q2[l] * lam_k2[l]).astype(jnp.float32)) + lam_init)
        out_c = diff_attention(to_heads(dq, DF_HEADS), to_heads(dk, DF_HEADS), to_heads(dv, DF_HEADS),
                               lam, lam_init, subln_g[l])

        mixed = jnp.concatenate([out_a, out_b.astype(out_a.dtype), out_c.astype(out_a.dtype)], axis=-1)
        x = x + mixed @ w_out[l]

        h2 = rmsnorm_2(x, norm2_g[l])
        u = causal_dwconv(h2 @ w_ff_up[l], conv_ff_w[l], conv_ff_b[l])
        gate, val = jnp.split(u, 2, axis=-1)
        x = x + (jax.nn.silu(gate) * val) @ w_ff_down[l]
    return rmsnorm_2(x, final_g)


def setup_inputs(seed=0):
    out = dict(first_inputs(seed))
    for name, value in second_inputs(seed + 1).items():
        if name != "x":
            out[name + "_2"] = value
    return out


def reference(
    x, norm_mix_w, w_in, hg_lower_bounds, hg_norm_w, w_branch_hg, w_branch_ret, w_out,
    norm_ffn_w, peer_w_q, peer_sub_keys, expert_u, expert_v, final_norm_w, norm1_g_2, w_in_2,
    conv_a_w_2, conv_a_b_2, w_rgate_2, b_rgate_2, w_igate_2, b_igate_2, lru_lambda_2, lam_q1_2,
    lam_k1_2, lam_q2_2, lam_k2_2, subln_g_2, w_out_2, norm2_g_2, w_ff_up_2, conv_ff_w_2,
    conv_ff_b_2, w_ff_down_2, final_g_2,
):
    x = first_block(
        x, norm_mix_w, w_in, hg_lower_bounds, hg_norm_w, w_branch_hg, w_branch_ret, w_out,
        norm_ffn_w, peer_w_q, peer_sub_keys, expert_u, expert_v, final_norm_w,
    )
    return second_block(
        x, norm1_g_2, w_in_2, conv_a_w_2, conv_a_b_2, w_rgate_2, b_rgate_2, w_igate_2,
        b_igate_2, lru_lambda_2, lam_q1_2, lam_k1_2, lam_q2_2, lam_k2_2, subln_g_2, w_out_2,
        norm2_g_2, w_ff_up_2, conv_ff_w_2, conv_ff_b_2, w_ff_down_2, final_g_2,
    )


_drawn_inputs = setup_inputs


def setup_inputs(seed=0):
    import zlib

    import numpy as np

    out = dict(_drawn_inputs(seed))
    spreads = {}
    factors = {'hg_norm_w': 3.133,
     'norm1_g_2': 3.236,
     'conv_a_b_2': 8.264,
     'b_rgate_2': 35.489,
     'b_igate_2': 33.208,
     'lam_k1_2': 8.0,
     'subln_g_2': 28.252,
     'norm2_g_2': 11.278,
     'conv_ff_b_2': 23.251,
     'final_g_2': 22.973}
    for name, (base, spread) in spreads.items():
        noise = np.random.default_rng([zlib.crc32(name.encode()), seed]).standard_normal(out[name].shape)
        drawn = base * np.exp(spread * noise) if base else spread * noise
        out[name] = __import__('jax').numpy.asarray(drawn.astype(out[name].dtype))
    for name, factor in factors.items():
        out[name] = (out[name] * factor).astype(out[name].dtype)
    return out
```

```python
import numpy as np
import concourse.bass as bass
from concourse import mybir

F32 = mybir.dt.float32
F32R = mybir.dt.float32r
U32 = mybir.dt.uint32
ACT = mybir.ActivationFunctionType
ALU = mybir.AluOpType
AX = mybir.AxisListType

P = 128
D = 1024
T = 512
KT = D // P
TT = T // P
EPS = 1e-6
HG_HEADS, HG_DK = 8, 128
RET_HEADS, RET_DK, RET_DV = 4, 256, 512
PEER_HEADS, TOPK, NKEYS = 8, 16, 128
CHOICES = PEER_HEADS * TOPK
GROUP = 32
TOKENS_PER_BATCH = 8
STAGED_TOKENS = 64
LRU_TILES = 4
SB_HEADS, SB_DH = 4, 64
DF_HEADS, DF_DV, DF_DQK = 4, 64, 32
FF = 2816
FF_TILES = FF // P
LAM_INIT = 0.8 - 0.6 * float(np.exp(-0.3 * 0))
LEVELS = [0, 64, 32, 16, 8, 4, 2, 1]

VEC = {}
_at = 0
for _name, _n in (("norm_mix", 8), ("bounds", 16), ("hg_norm", 8), ("norm_ffn", 8), ("final", 8),
                  ("norm1", 8), ("conv_a_w", 16), ("conv_a_b", 4), ("b_r", 4), ("b_i", 4), ("lam", 4),
                  ("subln", 1), ("norm2", 8), ("conv_ff_w", 3 * 2 * FF_TILES), ("conv_ff_b", 2 * FF_TILES),
                  ("final2", 8), ("lam_qk", 128)):
    VEC[_name] = (_at, _n)
    _at += _n
N_VEC = _at

TAB = {}
_at = 0
for _name, _n in (("identity", 128), ("later", 128), ("earlier", 128), ("halves", 128), ("iota16", 16), ("iota128", 128),
                  ("cos", 512), ("sin", 512), ("decay", RET_HEADS * 512), ("scan_keep", 512), ("distance", 512), ("levels", 8 * 128)):
    TAB[_name] = (_at, _n)
    _at += _n
N_TAB = _at

STREAM = (("hf", 8), ("hq", 8), ("hi", 8), ("rqk", 16), ("rv", 16), ("hg", 8), ("gate_a", 8), ("w_hg", 8),
          ("gate_b", 8), ("rg", 16), ("w_ret", 16), ("w_out", 8), ("peer_q", 16), ("experts", 256),
          ("in_2", 16), ("values_2", 4), ("out_2", 8), ("up", 44), ("down", 22))
N_STREAM = sum(n for _, n in STREAM)
RAW = 4


class Count:

    def __init__(self, eng, passed):
        self.eng, self.passed, self.base, self.loops = eng, passed, {}, []

    def alone(self):
        if self.loops:
            self.eng.sem_inc(self.passed, 1)

    def due(self, sem, n=1, back=0):
        self.base[sem.name] = self.base.get(sem.name, 0) + n
        value = least = self.base[sem.name] - back
        for reg, deltas, first in self.loops:
            step = deltas.get(sem.name, 0)
            if step:
                value = value + reg * step
                least += step * first
        assert least >= 0 or isinstance(value, int), sem.name
        return max(value, 0) if isinstance(value, int) else value

    def once(self, body, *args):
        before = dict(self.base)
        body(*args)
        self.delta = {s: v - before.get(s, 0) for s, v in self.base.items() if v != before.get(s, 0)}

    def loop(self, first, end, body):
        start, delta = dict(self.base), self.delta
        self.alone()
        self.base = {s: v - first * delta.get(s, 0) for s, v in start.items()}
        with self.eng.Fori(first, end) as i:
            self.loops.append((i, delta, first))
            body(i)
            self.loops.pop()
        self.base = {s: v + (end - first) * delta.get(s, 0) for s, v in start.items()}

    def repeat(self, n, body):
        self.once(body, 0)
        if n > 1:
            self.loop(1, n, body)


def build(nc, x, weights, vectors, tables, keys, lru_gates, out):
    top = nc.sbuf_base + (-nc.sbuf_base) % 64
    limit = nc.sbuf_usable_end

    def place(name, shape, at, dtype=F32):
        size = int(np.prod(shape[1:])) * 4
        assert top + at + size <= limit, (name, top + at + size, limit)
        return nc.alloc_sbuf_tensor_at(name, shape, dtype, offset=top + at)

    KB = 1024
    w_raw = place("w_raw", [P, RAW, 1024], 0)
    w_hi = place("w_hi", [P, 2, 1024], 16 * KB, F32R)
    w_lo = place("w_lo", [P, 2, 1024], 24 * KB, F32R)
    h_hi = place("h_hi", [P, KT, T], 32 * KB, F32R)
    h_lo = place("h_lo", [P, KT, T], 48 * KB, F32R)
    X0 = 64 * KB
    resid = place("resid", [P, KT, T], X0)
    SMALL = 80 * KB
    rstd = place("rstd", [P, T], SMALL)
    sq = place("sq", [P, 2, T], SMALL + 2 * KB)
    tmp = place("tmp", [P, 2, T], SMALL + 6 * KB)
    ones = place("ones", [P, P], SMALL + 10 * KB)
    eps = place("eps", [P, 1], SMALL + 10 * KB + 512)
    tiny = place("tiny", [P, 64], SMALL + 10 * KB + 576)
    vec = place("vec", [P, N_VEC], SMALL + 10 * KB + 832)
    TAB0 = SMALL + 10 * KB + 832 + 4 * N_VEC + (-4 * N_VEC) % 64
    tab = place("tab", [P, TAB["cos"][0]], TAB0)
    A0 = TAB0 + 4 * TAB["cos"][0]
    A0 += -A0 % 32

    def v(name, i=0, n=1):
        return vec[:, VEC[name][0] + i:VEC[name][0] + i + n]

    def t_(name):
        return tab[:, TAB[name][0]:TAB[name][0] + TAB[name][1]]

    hq_ = place("hg_q_then_o", [P, HG_HEADS, T], A0)
    rq = place("ret_q", [P, 8, T], A0 + 16 * KB)
    rk = place("ret_k", [P, 8, T], A0 + 32 * KB)
    hb = place("hg_log_decay", [P, HG_HEADS, T], A0 + 48 * KB)
    hk = place("hg_k", [P, HG_HEADS, T], A0 + 64 * KB)
    hv = place("hg_v", [P, TT, HG_HEADS * 128], X0)
    W0 = A0 + 80 * KB
    att = place("hg_att", [P, TT * 640], W0)
    head_b = place("head_b", [P, T], W0 + 10 * KB)
    head_k = place("head_k", [P, T], W0 + 12 * KB)
    head_q = place("head_q", [P, T], W0 + 14 * KB)
    head_v = place("head_v", [P, TT, 128], W0 + 16 * KB)
    far_k = place("far_k", [P, 3, 128], W0 + 18 * KB)
    far_q = place("far_q", [P, 768], W0 + 20 * KB)
    masks = place("masks", [P, len(LEVELS), P], W0 + 23 * KB)
    skip = place("skip", [P, 1], W0 + 27 * KB)
    scan_keep = place("scan_keep", [P, T], W0 + 16 * KB)
    far_e = place("far_e", [P, 3, 128], W0 + 28 * KB)
    lev_e, lev_z = tmp, sq
    rv = place("ret_v_then_o", [P, TT, RET_HEADS * RET_DV], A0 + 48 * KB)
    rot_q = place("rot_q", [P, 2, T], W0)
    rot_k = place("rot_k", [P, 2, T], W0 + 4 * KB)
    ratt = place("ret_att", [P, TT * 512], W0 + 8 * KB)
    cos_sin = place("cos_sin", [P, 2, T], W0 + 16 * KB)
    rtmp = place("ret_tmp", [P, 2, T], W0 + 20 * KB)
    rvh = place("ret_head_v", [P, TT, RET_DV], X0)
    decay = place("decay", [P, RET_HEADS, T], X0 + 8 * KB)
    oh_hi = place("o_hg_hi", [P, 8, T], W0, F32R)
    oh_lo = place("o_hg_lo", [P, 8, T], X0, F32R)
    ga = place("gate_a", [P, 8, T], A0 + 16 * KB)
    gb = place("gate_b", [P, 8, T], A0 + 32 * KB)
    or_hi = place("o_ret_hi", [P, 16, T], W0, F32R)
    or_lo = [place("o_ret_lo0", [P, 8, T], X0, F32R), place("o_ret_lo1", [P, 8, T], A0, F32R)]
    scores = place("scores", [P, TT, 16 * NKEYS], A0)
    peer_q = place("peer_q", [P, 16, T], A0 + 32 * KB)
    stage = place("gate_stage", [P, NKEYS, STAGED_TOKENS], A0 + 32 * KB)
    sub_keys = place("sub_keys", [P, 16, NKEYS], A0 + 64 * KB)
    cand = place("cand", [P, PEER_HEADS, TOPK * TOPK], A0 + 64 * KB)
    pick = place("pick", [P, CHOICES, TOPK], A0 + 72 * KB)
    S1 = A0 + 80 * KB
    top_s = place("top_s", [P, 16, TOPK], S1)
    top_u = place("top_u", [P, 16, TOPK], S1 + KB, U32)
    top_f = place("top_f", [P, 16, TOPK], S1 + 2 * KB)
    best_s = place("best_s", [P, PEER_HEADS, TOPK], S1 + 3 * KB)
    best_u = place("best_u", [P, CHOICES], S1 + 3 * KB + 512, U32)
    row_u = place("row_u", [P, CHOICES], S1 + 4 * KB, U32)
    row_f = place("row_f", [P, 2, CHOICES], S1 + 4 * KB + 512)
    chosen = place("chosen", [P, 3, CHOICES], S1 + 5 * KB + 512)
    denom = place("denom", [P, 2, PEER_HEADS], S1 + 7 * KB)
    chosen_t = place("chosen_t", [P, 3, P], S1 + 7 * KB + 128)
    hot1 = place("hot1", [P, 2, TOKENS_PER_BATCH, NKEYS], S1 + 9 * KB)
    hot2 = place("hot2", [P, 2, TOKENS_PER_BATCH, NKEYS], S1 + 17 * KB)
    tile_scores = place("tile_scores", [P, 16, NKEYS], SMALL + 2 * KB)
    g_in = place("gates_in", [P, 4, T], A0)
    expert_w = place("expert_w", [P, GROUP, T], A0 + 8 * KB)
    ew_hi = place("ew_hi", [P, 2, T], A0 + 72 * KB, F32R)
    ew_lo = place("ew_lo", [P, 2, T], A0 + 76 * KB, F32R)
    in2 = place("in2", [P, 16, T], A0)
    val2 = place("val2", [P, TT, 512], A0 + 32 * KB)
    mix_hi = place("mix_hi", [P, 8, T], A0 + 40 * KB, F32R)
    mix_lo = place("mix_lo", [P, 8, T], A0 + 56 * KB, F32R)
    B0 = A0 + 72 * KB
    lru_w = place("lru_w", [P, 8, P], B0)
    lru = [place(f"lru{n}", [P, T], B0 + (4 + 2 * n) * KB) for n in range(6)]
    sbw = place("sb_w", [P, TT, T], B0 + 4 * KB)
    sbz = place("sb_z", [P, TT, T], B0 + 12 * KB)
    sbt = place("sb_t", [P, 2, T], B0 + 20 * KB)
    distance = place("distance", [P, T], B0 + 28 * KB)
    dfs = place("df_s", [P, 2, T], B0 + 4 * KB)
    dfe = place("df_e", [P, 2, T], B0 + 8 * KB)
    dfp = place("df_p", [P, T], B0 + 12 * KB)
    dfpt = place("df_pt", [P, TT, T], B0 + 14 * KB)
    df_stat = place("df_stat", [P, 16], B0 + 22 * KB)
    dfo = place("df_o", [P, 2, T], B0 + 24 * KB)
    ff_hi = place("ff_hi", [P, FF_TILES, T], A0, F32R)
    ff_lo = place("ff_lo", [P, FF_TILES, T], A0 + 44 * KB, F32R)
    conv = place("conv", [P, 2, T], A0 + 88 * KB)
    act_g = place("act_g", [P, 2, T], A0 + 92 * KB)
    final = place("final", [P, KT, T], A0)

    bank = [nc.alloc_psum_tensor(f"bank{n}", [P, T], F32) for n in range(8)]

    gates = nc.dram_tensor("gates", (T // STAGED_TOKENS, NKEYS, NKEYS, STAGED_TOKENS), F32, kind="Internal").ap()

    def sem(name):
        return nc.alloc_semaphore(name)

    raw_loaded = [sem(f"raw_loaded{n}") for n in range(RAW)]
    gate_in = [sem(f"gate_in{n}") for n in range(4)]
    sp_passed, pool_passed, pe_passed, act_passed, dve_passed = (sem(n) for n in (
        "sp_passed", "pool_passed", "pe_passed", "act_passed", "dve_passed"))
    consts_in, x_in, masks_in, cs_in, keys_in, lru_in = (sem(n) for n in (
        "consts_in", "x_in", "masks_in", "cs_in", "keys_in", "lru_in"))
    distance_in, gates_out, out_done = (sem(n) for n in (
        "distance_in", "gates_out", "out_done"))
    hi_split, split_done, hot_gated = (sem(n) for n in (
        "hi_split", "split_done", "hot_gated"))
    tile_done, pair_used, sq_used, lev_done, far_done, o_done = (sem(n) for n in (
        "tile_done", "pair_used", "sq_used", "lev_done", "far_done", "o_done"))
    ret_s_done, ret_o_done, score_done, turned, batch_done, lru_gate_done = (sem(n) for n in (
        "ret_s_done", "ret_o_done", "score_done", "turned", "batch_done", "lru_gate_done"))
    sb_z_done, sb_tail_done, sb_o_done, df_s_done, df_pt_done, df_o_done = (sem(n) for n in (
        "sb_z_done", "sb_tail_done", "sb_o_done", "df_s_done", "df_pt_done", "df_o_done"))
    acc_read_act, acc_read_dve, tok_read = (sem(n) for n in (
        "acc_read_act", "acc_read_dve", "tok_read"))
    act_step, sq_done, root_done, bounds_exp, logf_done, head_ready = (sem(n) for n in (
        "act_step", "sq_done", "root_done", "bounds_exp", "logf_done", "head_ready"))
    far_q_exp, lev_exp, att_far, o_read, rvh_ready, ret_o_read = (sem(n) for n in (
        "far_q_exp", "lev_exp", "att_far", "o_read", "rvh_ready", "ret_o_read"))
    score_read, scores_copied, best_exp, gate_read, ew_hi_ready, lam_exp = (sem(n) for n in (
        "score_read", "scores_copied", "best_exp", "gate_read", "ew_hi_ready", "lam_exp"))
    lam_ready, lru_gate_read, lru_decays, lru_root, lru_gelu, sb_ln = (sem(n) for n in (
        "lam_ready", "lru_gate_read", "lru_decays", "lru_root", "lru_gelu", "sb_ln"))
    sb_exp, df_exp, df_pt_read, df_o_read = (sem(n) for n in (
        "sb_exp", "df_exp", "df_pt_read", "df_o_read"))
    dve_step, eps_set, ones_set, h_ready, bounds_shifted, f_done = (sem(n) for n in (
        "dve_step", "eps_set", "ones_set", "h_ready", "bounds_shifted", "f_done"))
    decay_done, far_e_ready, lev_diff, far_ready, lev_ready, lev_read = (sem(n) for n in (
        "decay_done", "far_e_ready", "lev_diff", "far_ready", "lev_ready", "lev_read"))
    rot_ready, ret_att, normed, gated, chosen_done, best_shifted = (sem(n) for n in (
        "rot_ready", "ret_att", "normed", "gated", "chosen_done", "best_shifted"))
    hot_ready, weighted, ew_ready, x_added, resid_ready, lam_abs = (sem(n) for n in (
        "hot_ready", "weighted", "ew_ready", "x_added", "resid_ready", "lam_abs"))
    softplus_done, conv_done, lru_var, mixed_ready, sb_z_read, sb_sp_ready = (sem(n) for n in (
        "softplus_done", "conv_done", "lru_var", "mixed_ready", "sb_z_read", "sb_sp_ready"))
    sb_tail_read, sb_w_ready, sb_o_read, df_s_read, df_max, df_p_ready = (sem(n) for n in (
        "sb_tail_read", "sb_w_ready", "sb_o_read", "df_s_read", "df_max", "df_p_ready"))
    ff_silu, ff_ready, down_read, final_done = (sem(n) for n in (
        "ff_silu", "ff_ready", "down_read", "final_done"))

    START, at = {}, 0
    for name, n in STREAM:
        START[name] = at
        at += n
    START["end"] = at

    ACT_READ, at = {}, 0
    for name, n in (("hf", 8), ("hq", 8), ("rqk", 16), ("hg", 8), ("gate_a", 8), ("gate_b", 8), ("rg", 16),
                    ("peer_q", 16), ("experts", NKEYS), ("in_2", 16)):
        ACT_READ[name] = at
        at += n

    def one(t, i):
        return t[:, bass.ds(i, 1), :].rearrange("p a n -> p (a n)")

    def f32(t):
        return t.bitcast(F32)

    block = nc.Block()
    block.__enter__()

    @block.sync
    def _(sp):
        c = Count(sp, sp_passed)
        sp.dma_start(vec[:], vectors).then_inc(consts_in, 16)
        sp.dma_start(tab[:], tables[:, 0:TAB["cos"][0]]).then_inc(consts_in, 16)
        sp.dma_start(resid[:], x).then_inc(x_in, 16)
        sp.dma_start(masks[:].rearrange("p l n -> p (l n)"), tables[:, TAB["levels"][0]:TAB["levels"][0] + len(LEVELS) * P]).then_inc(masks_in, 16)
        sp.dma_start(scan_keep[:], tables[:, TAB["scan_keep"][0]:TAB["scan_keep"][0] + T]).then_inc(masks_in, 16)

        def load(i, slot):
            sp.wait_ge(split_done, c.due(split_done, 1, back=RAW))
            sp.dma_start(w_raw[:, slot, :], weights[bass.ds(i, 1), :, :].rearrange("a p n -> (a p) n")).then_inc(raw_loaded[slot], 16)

        def load_run(first, n):
            def four(i):
                for s in range(RAW):
                    load(i * RAW + (first + s), s)
            c.repeat(n // RAW, four)

        load_run(0, START["experts"])
        sp.wait_ge(gates_out, c.due(gates_out, 16 * (T // STAGED_TOKENS)))

        def group(g):
            first = START["experts"] + g * (2 * GROUP)

            def four(i):
                for s in range(RAW):
                    load(first + i * RAW + s, s)
                    sp.wait_ge(weighted, c.due(weighted, 1, back=4))
                    e = g * GROUP + i * RAW + s
                    sp.dma_start(g_in[:, s, :].rearrange("p (b t) -> p b t", t=STAGED_TOKENS),
                                 gates[:, :, bass.ds(e, 1), :].rearrange("b k a t -> k b (a t)")).then_inc(gate_in[s], 16)
            c.repeat(GROUP // RAW, four)

            def four_values(i):
                for s in range(RAW):
                    load(first + GROUP + i * RAW + s, s)
            c.repeat(GROUP // RAW, four_values)
        c.repeat(NKEYS // GROUP, group)
        rest = N_STREAM - START["in_2"]
        load_run(START["in_2"], rest - rest % RAW)
        for s in range(rest % RAW):
            load(N_STREAM - rest % RAW + s, s)
        sp.wait_ge(final_done, c.due(final_done, KT))
        sp.dma_start(out, final[:]).then_inc(out_done, 16)
        sp.wait_ge(out_done, 16)

    @block.gpsimd
    def _(pool):
        c = Count(pool, pool_passed)

        one_col = ones[:, 0:1]
        pool.wait_ge(ones_set, c.due(ones_set))

        def split(slot):
            pair = slot % 2
            pool.wait_ge(raw_loaded[slot], c.due(raw_loaded[slot], 16))
            pool.wait_ge(tile_done, c.due(tile_done, 1, back=2))
            nc.gpsimd.tensor_tensor(w_hi[:, pair, :], w_raw[:, slot, :], one_col.to_broadcast((P, 1024)), ALU.mult).then_inc(hi_split, 1)
            pool.wait_ge(hi_split, c.due(hi_split))
            nc.gpsimd.tensor_tensor(w_lo[:, pair, :], w_raw[:, slot, :], f32(w_hi[:, pair, :]), ALU.subtract).then_inc(split_done, 1)
            pool.wait_ge(split_done, c.due(split_done))

        def four(i):
            for s in range(RAW):
                split(s)

        c.repeat(START["experts"] // RAW, four)

        def token_tile(tt):
            def two(i):
                for p in range(2):
                    pool.wait_ge(hot_ready, c.due(hot_ready))
                    gate = chosen_t[:, 2, bass.ds((i * 2 + p) * TOKENS_PER_BATCH, TOKENS_PER_BATCH)]
                    nc.gpsimd.tensor_tensor(hot1[:, p], hot1[:, p], gate.unsqueeze(2).to_broadcast((P, TOKENS_PER_BATCH, NKEYS)),
                                            ALU.mult).then_inc(hot_gated, 1)
                    pool.wait_ge(hot_gated, c.due(hot_gated))
            c.repeat(P // TOKENS_PER_BATCH // 2, two)
        c.repeat(TT, token_tile)
        rest = N_STREAM - START["experts"]
        c.repeat(rest // RAW, four)
        for s in range(rest % RAW):
            split(s)

    @block.tensor
    def _(pe):
        c = Count(pe, pe_passed)
        mm = nc.tensor.matmul

        def settle():
            pe.wait_ge(acc_read_act, c.due(acc_read_act, 0))
            pe.wait_ge(acc_read_dve, c.due(acc_read_dve, 0))
            pe.wait_ge(tok_read, c.due(tok_read, 0))

        def three(out_, hi, lo, rhs_hi, rhs_lo, first, last):
            mm(out_, hi, rhs_hi, start=first, stop=False)
            mm(out_, hi, rhs_lo, start=False, stop=False)
            return mm(out_, lo, rhs_hi, start=False, stop=last)

        def tile_fm(p, rhs_hi, rhs_lo, acc, first=True, last=True):
            pe.wait_ge(split_done, c.due(split_done))
            for k in range(KT):
                col = slice(k * P, (k + 1) * P)
                ins = three(acc, w_hi[:, p, col], w_lo[:, p, col], rhs_hi[:, k, :], rhs_lo[:, k, :],
                            first and k == 0, last and k == KT - 1)
            ins.then_inc(tile_done, 1)

        def dense_fm(n, rhs_hi, rhs_lo, read):
            settle()

            def two(i):
                for p in range(2):
                    pe.wait_ge(read, c.due(read, 1, back=2))
                    tile_fm(p, rhs_hi, rhs_lo, bank[p][:])
            c.repeat(n // 2, two)

        def dense_tm(groups):
            settle()

            def group(g):
                pe.wait_ge(tok_read, c.due(tok_read, TT, back=TT))
                for j in range(4):
                    pe.wait_ge(split_done, c.due(split_done))
                    for k2 in range(2):
                        k = 2 * j + k2
                        col = slice(k2 * 512, k2 * 512 + 512)
                        for tt in range(TT):
                            tok = slice(tt * P, tt * P + P)
                            o = bank[2 + tt][:]
                            mm(o, h_hi[:, k, tok], w_hi[:, j % 2, col], start=k == 0, stop=False)
                            mm(o, h_hi[:, k, tok], w_lo[:, j % 2, col], start=False, stop=False)
                            ins = mm(o, h_lo[:, k, tok], w_hi[:, j % 2, col], start=False, stop=k == KT - 1)
                    ins.then_inc(tile_done, 1)
            c.repeat(groups, group)

        def norm():
            for k in range(KT):
                pe.wait_ge(sq_done, c.due(sq_done))
                mm(bank[7][:], ones[:], sq[:, k % 2, :], start=k == 0, stop=k == KT - 1).then_inc(sq_used, 1)

        pe.wait_ge(ones_set, c.due(ones_set))
        norm()
        pe.wait_ge(h_ready, c.due(h_ready, KT))
        dense_fm(16, h_hi, h_lo, acc_read_act)
        dense_tm(2)
        settle()

        def hgrn_head(i):
            pe.wait_ge(head_ready, c.due(head_ready))

            def level(lhs, rhs, l):
                pe.wait_ge(lev_read, c.due(lev_read, 1, back=2))
                for j in range(TT):
                    tok = slice(j * P, j * P + P)
                    ins = mm(bank[2 + l % 2][:, tok], lhs[:, tok], rhs[:, tok], start=j == 0, stop=j == TT - 1)
                ins.then_inc(lev_done, 1)

            level(head_k, head_q, 0)
            pe.wait_ge(acc_read_act, c.due(acc_read_act, 1, back=2))
            tile_fm(0, h_hi, h_lo, bank[0][:])
            pe.wait_ge(far_ready, c.due(far_ready))
            pe.wait_ge(att_far, c.due(att_far, 3, back=3))
            mm(bank[4][:, 0:384], far_k[:, 0, :], far_q[:, 0:384], start=True, stop=True)
            mm(bank[5][:, 0:256], far_k[:, 1, :], far_q[:, 384:640], start=True, stop=False)
            mm(bank[5][:, 256:384], far_k[:, 2, :], far_q[:, 640:768], start=False, stop=True).then_inc(far_done, 1)
            for l in range(1, len(LEVELS)):
                pe.wait_ge(lev_ready, c.due(lev_ready))
                level(lev_z[:, l % 2, :], lev_z[:, l % 2, :], l)
                if l == 3:
                    pe.wait_ge(acc_read_act, c.due(acc_read_act, 1, back=2))
                    tile_fm(1, h_hi, h_lo, bank[1][:])
            pe.wait_ge(lev_read, c.due(lev_read, 0))
            pe.wait_ge(att_far, c.due(att_far, 0))
            pe.wait_ge(o_read, c.due(o_read, 1, back=1))
            for j in range(TT):
                ins = mm(bank[6][:, j * P:T], head_v[:, j, :], att[:, j * 640:j * 640 + T - j * P], start=j == 0, stop=j == TT - 1)
            ins.then_inc(o_done, 1)
        c.repeat(HG_HEADS, hgrn_head)

        dense_tm(4)
        settle()

        def ret_head(i):
            pe.wait_ge(rot_ready, c.due(rot_ready))
            for j in range(TT):
                pe.wait_ge(ret_att, c.due(ret_att, 1, back=2))
                for k in range(2):
                    ins = mm(bank[2 + j % 2][:, 0:T - j * P], rot_k[:, k, j * P:j * P + P], rot_q[:, k, j * P:T],
                             start=k == 0, stop=k == 1)
                ins.then_inc(ret_s_done, 1)
            pe.wait_ge(ret_att, c.due(ret_att, 0))
            pe.wait_ge(rvh_ready, c.due(rvh_ready))
            for m in range(4):
                pe.wait_ge(ret_o_read, c.due(ret_o_read, 1, back=2))
                for j in range(TT):
                    ins = mm(bank[4 + m % 2][:, j * P:T], rvh[:, j, m * P:m * P + P], ratt[:, j * 512:j * 512 + T - j * P],
                             start=j == 0, stop=j == TT - 1)
                ins.then_inc(ret_o_done, 1)
        c.repeat(RET_HEADS, ret_head)
        pe.wait_ge(ret_o_read, c.due(ret_o_read, 0))

        def hg_norm(i):
            for p in range(2):
                pe.wait_ge(sq_done, c.due(sq_done))
                mm(bank[2 + p][:], ones[:], sq[:, p, :], start=True, stop=True).then_inc(sq_used, 1)
        c.repeat(HG_HEADS // 2, hg_norm)

        def ret_norm(i):
            for m in range(4):
                pe.wait_ge(sq_done, c.due(sq_done))
                mm(bank[4][:], ones[:], sq[:, m % 2, :], start=m == 0, stop=m == 3).then_inc(sq_used, 1)
        c.repeat(RET_HEADS, ret_norm)

        dense_fm(8, h_hi, h_lo, acc_read_act)
        dense_fm(8, h_hi, h_lo, acc_read_act)
        pe.wait_ge(gated, c.due(gated, 8))
        dense_fm(8, oh_hi, oh_lo, acc_read_dve)
        dense_fm(8, h_hi, h_lo, acc_read_act)
        dense_fm(16, h_hi, h_lo, acc_read_act)
        pe.wait_ge(gated, c.due(gated, 16))
        settle()

        def two_deep(i):
            for n in range(2):
                pe.wait_ge(acc_read_dve, c.due(acc_read_dve, 1, back=2))
                tile_fm(0, or_hi[:, 0:8, :], or_lo[0], bank[n][:], last=False)
                tile_fm(1, or_hi[:, 8:16, :], or_lo[1], bank[n][:], first=False)
        c.repeat(4, two_deep)
        pe.wait_ge(h_ready, c.due(h_ready, KT))
        dense_fm(8, h_hi, h_lo, acc_read_dve)
        norm()

        pe.wait_ge(h_ready, c.due(h_ready, KT))
        dense_fm(16, h_hi, h_lo, acc_read_act)
        settle()
        pe.wait_ge(keys_in, c.due(keys_in, 16))
        for tt in range(TT):
            pe.wait_ge(score_read, c.due(score_read, 4, back=4))
            for n in range(16):
                ins = mm(bank[2 + n // 4][:, n % 4 * P:n % 4 * P + P], peer_q[:, n, tt * P:tt * P + P], sub_keys[:, n, :],
                         start=n % 4 == 0, stop=n % 4 == 3)
            ins.then_inc(score_done, 1)
        pe.wait_ge(score_read, c.due(score_read, 0))

        def token_tile(tt):
            pe.wait_ge(chosen_done, c.due(chosen_done))
            for n in range(3):
                ins = nc.tensor.transpose(bank[6][:, n * P:n * P + P], chosen[:, n, :], t_("identity"))
            ins.then_inc(turned, 1)

            def two(i):
                for p in range(2):
                    pe.wait_ge(hot_gated, c.due(hot_gated))
                    pe.wait_ge(gate_read, c.due(gate_read, 2, back=4))
                    for t in range(TOKENS_PER_BATCH):
                        ins = mm(bank[2 + 2 * p + t // 4][:, t % 4 * P:t % 4 * P + P], hot2[:, p, t, :], hot1[:, p, t, :],
                                 start=t % 4 == 0, stop=t % 4 == 3)
                    ins.then_inc(batch_done, 1)
            c.repeat(P // TOKENS_PER_BATCH // 2, two)
        c.repeat(TT, token_tile)
        pe.wait_ge(gate_read, c.due(gate_read, 0))

        def group(g):
            pe.wait_ge(x_added, c.due(x_added, 0))
            dense_fm(GROUP, h_hi, h_lo, acc_read_act)
            for half in range(2):
                banks = [bank[(2 + half * 4 + m) % 8] for m in range(4)]
                pe.wait_ge(x_added, c.due(x_added, 4, back=8))
                pe.wait_ge(acc_read_act, c.due(acc_read_act, 0))

                def values(i, first, last):
                    for p in range(2):
                        pe.wait_ge(split_done, c.due(split_done))
                        for e in range(2):
                            pe.wait_ge(ew_ready, c.due(ew_ready))
                            for m in range(4):
                                col = slice(e * 512 + m * P, e * 512 + m * P + P)
                                ins = three(banks[m][:], w_hi[:, p, col], w_lo[:, p, col], ew_hi[:, e, :], ew_lo[:, e, :],
                                            first and p == 0 and e == 0, last and p == 1 and e == 1)
                            ins.then_inc(pair_used if e == 0 else tile_done, 1)
                n = GROUP // 4
                c.once(values, 0, True, False)
                c.loop(1, n - 1, lambda i: values(i, False, False))
                c.once(values, n - 1, False, True)
        c.repeat(NKEYS // GROUP, group)
        pe.wait_ge(x_added, c.due(x_added, 0))
        norm()

        norm()
        pe.wait_ge(h_ready, c.due(h_ready, KT))
        dense_fm(16, h_hi, h_lo, acc_read_act)
        dense_tm(1)
        settle()
        pe.wait_ge(lru_in, c.due(lru_in, 16))
        for n in range(LRU_TILES):
            pe.wait_ge(conv_done, c.due(conv_done))
            pe.wait_ge(lru_gate_read, c.due(lru_gate_read, 2, back=2))
            mm(bank[2][:], lru_w[:, n, :], lru[0][:], start=True, stop=True)
            mm(bank[3][:], lru_w[:, 4 + n, :], lru[0][:], start=True, stop=True).then_inc(lru_gate_done, 1)
        pe.wait_ge(lru_gate_read, c.due(lru_gate_read, 0))
        for h in range(SB_HEADS):
            row = slice(64 * (h % 2), 64 * (h % 2) + 64)
            pe.wait_ge(sb_z_read, c.due(sb_z_read, TT, back=TT))
            for j in range(TT):
                mm(bank[2 + j][:, 0:T - j * P], in2[row, 10 + h // 2, j * P:j * P + P], in2[row, 8 + h // 2, j * P:T],
                   start=True, stop=True).then_inc(sb_z_done, 1)
            pe.wait_ge(sb_sp_ready, c.due(sb_sp_ready, TT))
            for j in range(TT):
                pe.wait_ge(sb_tail_read, c.due(sb_tail_read, 1, back=2))
                acc = bank[j % 2]
                for j2 in range(j, TT):
                    ins = mm(acc[:, (j2 - j) * P:T - j * P], t_("later") if j2 == j else ones[:], sbw[:, j2, 0:T - j2 * P],
                             start=j2 == j, stop=j2 == TT - 1)
                ins.then_inc(sb_tail_done, 1)
            pe.wait_ge(sb_w_ready, c.due(sb_w_ready, TT))
            pe.wait_ge(sb_o_read, c.due(sb_o_read, 1 if h % 2 == 0 else 0, back=1))
            for j in range(TT):
                ins = mm(bank[6][row, j * P:T], val2[:, j, h * 64:h * 64 + 64], sbw[:, j, 0:T - j * P],
                         start=j == 0, stop=j == TT - 1)
            ins.then_inc(sb_o_done, 1)
        pe.wait_ge(sb_o_read, c.due(sb_o_read, 0))
        for h in range(DF_HEADS):
            for i in range(TT):
                for q in range(2):
                    r0 = 64 * (h % 2) + 32 * q
                    pe.wait_ge(df_s_read, c.due(df_s_read, 1, back=2))
                    mm(bank[2 + q][:, 0:(i + 1) * P], in2[r0:r0 + 32, 12 + h // 2, i * P:i * P + P],
                       in2[r0:r0 + 32, 14 + h // 2, 0:(i + 1) * P], start=True, stop=True).then_inc(df_s_done, 1)
                pe.wait_ge(df_p_ready, c.due(df_p_ready))
                pe.wait_ge(df_pt_read, c.due(df_pt_read, 1, back=1))
                for j in range(i + 1):
                    ins = nc.tensor.transpose(bank[4][:, j * P:j * P + P], dfp[:, j * P:j * P + P], t_("identity"))
                ins.then_inc(df_pt_done, 1)
            pe.wait_ge(df_pt_read, c.due(df_pt_read, 0))
            row = slice(64 * (h % 2), 64 * (h % 2) + 64)
            pe.wait_ge(df_o_read, c.due(df_o_read, 1 if h % 2 == 0 else 0, back=1))
            for j in range(TT):
                ins = mm(bank[6][row, j * P:T], val2[:, j, 256 + h * 64:256 + h * 64 + 64], dfpt[:, j, j * P:T],
                         start=j == 0, stop=j == TT - 1)
            ins.then_inc(df_o_done, 1)
            if h % 2:
                pe.wait_ge(sq_done, c.due(sq_done))
                mm(bank[5][:], t_("halves"), sq[:, h // 2, :], start=True, stop=True).then_inc(sq_used, 1)
        pe.wait_ge(mixed_ready, c.due(mixed_ready, 6))
        dense_fm(8, mix_hi, mix_lo, acc_read_dve)
        norm()
        pe.wait_ge(h_ready, c.due(h_ready, KT))
        dense_fm(2 * FF_TILES, h_hi, h_lo, acc_read_dve)
        settle()
        pe.wait_ge(ff_ready, c.due(ff_ready, FF_TILES))

        def down(i, first, last):
            for p in range(2):
                pe.wait_ge(split_done, c.due(split_done))
                for n in range(KT):
                    col = slice(n * P, n * P + P)
                    ins = three(bank[n][:], w_hi[:, p, col], w_lo[:, p, col], one(ff_hi, i * 2 + p), one(ff_lo, i * 2 + p),
                                first and p == 0, last and p == 1)
                ins.then_inc(tile_done, 1)
        n = FF_TILES // 2
        c.once(down, 0, True, False)
        c.loop(1, n - 1, lambda i: down(i, False, False))
        c.once(down, n - 1, False, True)
        pe.wait_ge(down_read, c.due(down_read, KT))
        norm()

    @block.scalar
    def _(act):
        c = Count(act, act_passed)
        fn = nc.scalar.activation

        def fn_at(*args, **kw):
            c.alone()
            return fn(*args, **kw)

        def evac(n, where, func=ACT.Copy, scale=1.0):
            def two(i):
                for p in range(2):
                    act.wait_ge(tile_done, c.due(tile_done))
                    fn_at(one(where, i * 2 + p), bank[p][:], func, scale=scale).then_inc(acc_read_act, 1)
                    act.wait_ge(acc_read_act, c.due(acc_read_act))
            c.repeat(n // 2, two)

        def evac_tm(groups, where):
            def group(g):
                act.wait_ge(tile_done, c.due(tile_done, 4))
                for tt in range(TT):
                    fn_at(where[:, tt, bass.ds(g * 512, 512)], bank[2 + tt][:], ACT.Copy).then_inc(tok_read, 1)
                    act.wait_ge(tok_read, c.due(tok_read))
            c.repeat(groups, group)

        def norm(src, width=D):
            for k in range(KT):
                act.wait_ge(sq_used, c.due(sq_used, 1, back=2))
                fn(sq[:, k % 2, :], src[:, k, :], ACT.Square).then_inc(sq_done, 1)
                act.wait_ge(sq_done, c.due(sq_done))
            act.wait_ge(sq_used, c.due(sq_used, 0))
            fn(rstd[:], bank[7][:], ACT.Sqrt, scale=1.0 / D, bias=eps[:]).then_inc(root_done, 1)
            act.wait_ge(root_done, c.due(root_done))

        act.wait_ge(x_in, c.due(x_in, 16))
        act.wait_ge(eps_set, c.due(eps_set))
        norm(resid)
        act.wait_ge(bounds_shifted, c.due(bounds_shifted))
        fn(tiny[:, 0:16], tiny[:, 0:16], ACT.Exp).then_inc(bounds_exp, 1)
        act.wait_ge(bounds_exp, c.due(bounds_exp))
        evac(8, hk, ACT.Sigmoid)
        evac(8, hq_, ACT.Copy, HG_DK ** -0.5)
        evac_tm(2, hv)
        act.wait_ge(f_done, c.due(f_done))
        fn(hb[:], hb[:], ACT.Ln).then_inc(logf_done, 1)
        act.wait_ge(logf_done, c.due(logf_done))
        act.wait_ge(decay_done, c.due(decay_done, HG_HEADS))

        def hgrn_head(i):
            act.wait_ge(o_done, c.due(o_done, 1, back=1))
            fn_at(head_b[:], one(hb, i), ACT.Copy).then_inc(act_step, 1)
            act.wait_ge(act_step, c.due(act_step))
            fn_at(head_k[:], one(hk, i), ACT.Copy).then_inc(act_step, 1)
            act.wait_ge(act_step, c.due(act_step))
            fn_at(head_q[:], one(hq_, i), ACT.Copy).then_inc(act_step, 1)
            act.wait_ge(act_step, c.due(act_step))
            fn_at(head_v[:], hv[:, :, bass.ds(i * 128, 128)], ACT.Copy).then_inc(head_ready, 1)
            act.wait_ge(head_ready, c.due(head_ready))
            act.wait_ge(far_e_ready, c.due(far_e_ready))
            fn(far_e[:], far_e[:], ACT.Exp).then_inc(act_step, 1)
            act.wait_ge(act_step, c.due(act_step))
            tile = [head_b[:, j * P:j * P + P] for j in range(TT)]
            total = [head_b[:, j * P + P - 1:j * P + P] for j in range(TT)]
            for n, (j, bias) in enumerate(((1, None), (2, total[1]), (3, skip[:]), (2, None), (3, total[2]), (3, None))):
                extra = {} if bias is None else {"bias": bias}
                done = far_q_exp if n == 5 else act_step
                fn(far_q[:, n * P:n * P + P], tile[j], ACT.Exp, **extra).then_inc(done, 1)
                act.wait_ge(done, c.due(done))

            def products():
                act.wait_ge(far_done, c.due(far_done))
                fn(att[:, 128:512], bank[4][:, 0:384], ACT.Copy).then_inc(att_far, 1)
                act.wait_ge(att_far, c.due(att_far))
                fn(att[:, 768:1024], bank[5][:, 0:256], ACT.Copy).then_inc(att_far, 1)
                act.wait_ge(att_far, c.due(att_far))
                fn(att[:, 1408:1536], bank[5][:, 256:384], ACT.Copy).then_inc(att_far, 1)
                act.wait_ge(att_far, c.due(att_far))
            for l in range(1, len(LEVELS)):
                act.wait_ge(lev_diff, c.due(lev_diff))
                fn(lev_e[:, l % 2, :], lev_e[:, l % 2, :], ACT.Exp).then_inc(lev_exp, 1)
                act.wait_ge(lev_exp, c.due(lev_exp))
                if l == 2:
                    act.wait_ge(tile_done, c.due(tile_done))
                    fn_at(one(rq, i), bank[0][:], ACT.Copy).then_inc(acc_read_act, 1)
                    act.wait_ge(acc_read_act, c.due(acc_read_act))
                if l == 4:
                    products()
            act.wait_ge(tile_done, c.due(tile_done))
            fn_at(one(rk, i), bank[1][:], ACT.Copy, scale=RET_DK ** -0.5).then_inc(acc_read_act, 1)
            act.wait_ge(acc_read_act, c.due(acc_read_act))
            act.wait_ge(o_done, c.due(o_done, 0))
            fn_at(one(hq_, i), bank[6][:], ACT.Copy).then_inc(o_read, 1)
            act.wait_ge(o_read, c.due(o_read))
        c.repeat(HG_HEADS, hgrn_head)
        act.dma_start(cos_sin[:], tables[:, TAB["cos"][0]:TAB["cos"][0] + 1024].rearrange("p (a n) -> p a n", a=2)).then_inc(cs_in, 16)
        act.dma_start(decay[:], tables[:, TAB["decay"][0]:TAB["decay"][0] + RET_HEADS * T].rearrange("p (a n) -> p a n", a=RET_HEADS)).then_inc(cs_in, 16)
        evac_tm(4, rv)

        def ret_head(i):
            fn_at(rvh[:], rv[:, :, bass.ds(i * RET_DV, RET_DV)], ACT.Copy).then_inc(rvh_ready, 1)
            act.wait_ge(rvh_ready, c.due(rvh_ready))
            for m in range(4):
                act.wait_ge(ret_o_done, c.due(ret_o_done))
                fn_at(rv[:, m, bass.ds(i * RET_DV, T)], bank[4 + m % 2][:], ACT.Copy).then_inc(ret_o_read, 1)
                act.wait_ge(ret_o_read, c.due(ret_o_read))
        c.repeat(RET_HEADS, ret_head)

        def hg_norm(i):
            for p in range(2):
                fn_at(sq[:, p, :], one(hq_, i * 2 + p), ACT.Square).then_inc(sq_done, 1)
                act.wait_ge(sq_done, c.due(sq_done))
            for p in range(2):
                act.wait_ge(sq_used, c.due(sq_used))
                act.wait_ge(normed, c.due(normed, 1, back=2))
                fn(tmp[:, p, :], bank[2 + p][:], ACT.Sqrt, scale=1.0 / 128, bias=eps[:]).then_inc(root_done, 1)
                act.wait_ge(root_done, c.due(root_done))
        c.repeat(HG_HEADS // 2, hg_norm)

        def ret_norm(i):
            act.wait_ge(normed, c.due(normed, 0))
            for m in range(4):
                act.wait_ge(sq_used, c.due(sq_used, 1, back=2))
                fn_at(sq[:, m % 2, :], rv[:, m, bass.ds(i * RET_DV, T)], ACT.Square).then_inc(sq_done, 1)
                act.wait_ge(sq_done, c.due(sq_done))
            act.wait_ge(sq_used, c.due(sq_used, 0))
            fn(tmp[:, 0, :], bank[4][:], ACT.Sqrt, scale=1.0 / RET_DV, bias=eps[:]).then_inc(root_done, 1)
            act.wait_ge(root_done, c.due(root_done))
            act.wait_ge(normed, c.due(normed))
        c.repeat(RET_HEADS, ret_norm)

        def silu(n):
            def two(i):
                for p in range(2):
                    act.wait_ge(tile_done, c.due(tile_done))
                    act.wait_ge(gated, c.due(gated, 1, back=2))
                    fn(sq[:, p, :], bank[p][:], ACT.Silu).then_inc(acc_read_act, 1)
                    act.wait_ge(acc_read_act, c.due(acc_read_act))
            c.repeat(n // 2, two)
        silu(8)
        evac(8, ga, ACT.Sigmoid)
        act.wait_ge(tile_done, c.due(tile_done, 8))
        evac(8, gb, ACT.Sigmoid)
        silu(16)
        act.wait_ge(gated, c.due(gated, 0))
        act.dma_start(sub_keys[:], keys).then_inc(keys_in, 16)
        act.wait_ge(tile_done, c.due(tile_done, 16))
        act.dma_start(resid[:], x).then_inc(x_in, 16)
        act.wait_ge(tile_done, c.due(tile_done, 8))
        act.wait_ge(acc_read_dve, c.due(acc_read_dve, 24))
        norm(resid)
        evac(16, peer_q)
        for tt in range(TT):
            act.wait_ge(score_done, c.due(score_done))
            for n in range(4):
                fn(scores[:, tt, n * 512:n * 512 + 512], bank[2 + n][:], ACT.Copy).then_inc(score_read, 1)
                act.wait_ge(score_read, c.due(score_read))

        def token_tile(tt):
            act.wait_ge(chosen_done, c.due(chosen_done, 1, back=1))
            fn_at(tile_scores.rearrange("p a n -> p (a n)"), one(scores, tt), ACT.Copy).then_inc(scores_copied, 1)
            act.wait_ge(scores_copied, c.due(scores_copied))
            act.wait_ge(best_shifted, c.due(best_shifted))
            fn(best_s[:], best_s[:], ACT.Exp).then_inc(best_exp, 1)
            act.wait_ge(best_exp, c.due(best_exp))

            def staged(s):
                act.wait_ge(gates_out, c.due(gates_out, 16, back=16))

                def two(i):
                    for p in range(2):
                        act.wait_ge(batch_done, c.due(batch_done))
                        for b in range(2):
                            t0 = i * (2 * TOKENS_PER_BATCH) + p * TOKENS_PER_BATCH + 4 * b
                            fn_at(stage[:, :, bass.ds(t0, 4)].rearrange("p k t -> p t k"),
                               bank[2 + 2 * p + b][:].rearrange("p (t k) -> p t k", k=NKEYS), ACT.Copy).then_inc(gate_read, 1)
                            act.wait_ge(gate_read, c.due(gate_read))
                c.repeat(STAGED_TOKENS // TOKENS_PER_BATCH // 2, two)
                act.dma_start(gates[bass.ds(tt * (P // STAGED_TOKENS) + s, 1), :, :, :].rearrange("b k a t -> k (b a t)"),
                              stage[:].rearrange("p a t -> p (a t)")).then_inc(gates_out, 16)
            for s in range(P // STAGED_TOKENS):
                staged(s)
        c.repeat(TT, token_tile)
        act.wait_ge(gates_out, c.due(gates_out, 0))

        def group(g):
            evac(GROUP, expert_w, ACT.Gelu_apprx_tanh)
            act.wait_ge(weighted, c.due(weighted, GROUP))

            for half in range(2):
                def values(i):
                    for p in range(2):
                        for e in range(2):
                            if e == 0:
                                act.wait_ge(pair_used, c.due(pair_used, 1, back=1))
                            else:
                                act.wait_ge(tile_done, c.due(tile_done, 1, back=1))
                            fn_at(ew_hi[:, e, :], one(expert_w, i * 4 + p * 2 + e), ACT.Copy).then_inc(ew_hi_ready, 1)
                            act.wait_ge(ew_hi_ready, c.due(ew_hi_ready))
                c.repeat(GROUP // 4, values)
            act.wait_ge(ew_ready, c.due(ew_ready, 2 * GROUP))
        c.repeat(NKEYS // GROUP, group)
        act.wait_ge(tile_done, c.due(tile_done, 0))
        act.dma_start(lru_w[:], lru_gates).then_inc(lru_in, 16)
        act.dma_start(distance[:], tables[:, TAB["distance"][0]:TAB["distance"][0] + T]).then_inc(distance_in, 16)
        act.wait_ge(x_added, c.due(x_added, 8 * (NKEYS // GROUP)))
        norm(resid)

        act.wait_ge(resid_ready, c.due(resid_ready, KT))
        norm(resid)
        act.wait_ge(lam_abs, c.due(lam_abs))
        fn(tiny[:, 0:4], tiny[:, 4:8], ACT.Exp).then_inc(lam_exp, 1)
        act.wait_ge(lam_exp, c.due(lam_exp))
        act.wait_ge(softplus_done, c.due(softplus_done))
        fn(tiny[:, 58:60], tiny[:, 56:58], ACT.Exp).then_inc(lam_ready, 1)
        act.wait_ge(lam_ready, c.due(lam_ready))
        evac(16, in2)
        evac_tm(1, val2)
        for n in range(LRU_TILES):
            act.wait_ge(lru_gate_done, c.due(lru_gate_done))
            fn(lru[1][:], bank[2][:], ACT.Sigmoid, bias=v("b_r", n)).then_inc(lru_gate_read, 1)
            act.wait_ge(lru_gate_read, c.due(lru_gate_read))
            fn(lru[2][:], bank[3][:], ACT.Sigmoid, bias=v("b_i", n)).then_inc(lru_gate_read, 1)
            act.wait_ge(lru_gate_read, c.due(lru_gate_read))
            fn(lru[3][:], lru[1][:], ACT.Exp, scale=tiny[:, 52 + n:53 + n]).then_inc(act_step, 1)
            act.wait_ge(act_step, c.due(act_step))
            fn(lru[4][:], lru[1][:], ACT.Tanh, scale=tiny[:, 48 + n:49 + n]).then_inc(lru_decays, 1)
            act.wait_ge(lru_decays, c.due(lru_decays))
            act.wait_ge(lru_var, c.due(lru_var))
            fn(lru[4][:], lru[4][:], ACT.Sqrt).then_inc(lru_root, 1)
            act.wait_ge(lru_root, c.due(lru_root))
            fn(lru[5][:], in2[:, 4 + n, :], ACT.Gelu_apprx_tanh).then_inc(lru_gelu, 1)
            act.wait_ge(lru_gelu, c.due(lru_gelu))
            act.wait_ge(mixed_ready, c.due(mixed_ready))
        for h in range(SB_HEADS):
            act.wait_ge(sb_z_read, c.due(sb_z_read, TT))
            for j in range(TT):
                N = T - j * P
                act.wait_ge(sb_sp_ready, c.due(sb_sp_ready, 1, back=2))
                fn(sbt[:, j % 2, 0:N], sbz[:, j, 0:N], ACT.Abs).then_inc(act_step, 1)
                act.wait_ge(act_step, c.due(act_step))
                fn(sbt[:, j % 2, 0:N], sbt[:, j % 2, 0:N], ACT.Exp, scale=-1.0).then_inc(act_step, 1)
                act.wait_ge(act_step, c.due(act_step))
                fn(sbt[:, j % 2, 0:N], sbt[:, j % 2, 0:N], ACT.Ln, bias=1.0).then_inc(sb_ln, 1)
                act.wait_ge(sb_ln, c.due(sb_ln))
            act.wait_ge(sb_tail_read, c.due(sb_tail_read, TT))
            for j in range(TT):
                N = T - j * P
                fn(sbw[:, j, 0:N], sbz[:, j, 0:N], ACT.Exp).then_inc(sb_exp, 1)
                act.wait_ge(sb_exp, c.due(sb_exp))
            act.wait_ge(sb_w_ready, c.due(sb_w_ready, TT))
        for h in range(DF_HEADS):
            for i in range(TT):
                N = (i + 1) * P
                for q in range(2):
                    act.wait_ge(df_max, c.due(df_max))
                    fn(dfe[:, q, 0:N], dfs[:, q, 0:N], ACT.Exp, scale=DF_DQK ** -0.5, bias=df_stat[:, 2 + q:3 + q],
                       accum_out=df_stat[:, 4 + q:5 + q]).then_inc(df_exp, 1)
                    act.wait_ge(df_exp, c.due(df_exp))
                act.wait_ge(df_pt_done, c.due(df_pt_done))
                if i == 0:
                    act.wait_ge(df_o_done, c.due(df_o_done, 1, back=1))
                fn(dfpt[:, 0:i + 1, i * P:i * P + P], bank[4][:, 0:N].rearrange("p (j n) -> p j n", n=P), ACT.Copy).then_inc(df_pt_read, 1)
                act.wait_ge(df_pt_read, c.due(df_pt_read))
            if h % 2:
                act.wait_ge(df_o_done, c.due(df_o_done, 0))
                fn(dfo[:, h // 2, :], bank[6][:], ACT.Copy).then_inc(df_o_read, 1)
                act.wait_ge(df_o_read, c.due(df_o_read))
                fn(sq[:, h // 2, :], dfo[:, h // 2, :], ACT.Square).then_inc(sq_done, 1)
                act.wait_ge(sq_done, c.due(sq_done))
                act.wait_ge(sq_used, c.due(sq_used))
                fn(rstd[:], bank[5][:], ACT.Sqrt, scale=1.0 / DF_DV, bias=eps[:]).then_inc(root_done, 1)
                act.wait_ge(root_done, c.due(root_done))
        act.wait_ge(acc_read_dve, c.due(acc_read_dve, 8))
        norm(resid)

        def ff(i):
            act.wait_ge(acc_read_dve, c.due(acc_read_dve, 2))
            act.wait_ge(ff_ready, c.due(ff_ready, 1, back=1))
            fn(act_g[:, 0, :], conv[:, 0, :], ACT.Silu).then_inc(ff_silu, 1)
            act.wait_ge(ff_silu, c.due(ff_silu))
        c.repeat(FF_TILES, ff)
        act.wait_ge(down_read, c.due(down_read, KT))
        norm(resid)

    @block.vector
    def _(dve):
        c = Count(dve, dve_passed)
        ve = nc.vector
        tt_ = ve.tensor_tensor
        ts = ve.tensor_scalar
        stt = ve.scalar_tensor_tensor

        def pair(hi, lo, value, done):
            ve.tensor_copy(hi, value).then_inc(dve_step, 1)
            dve.wait_ge(dve_step, c.due(dve_step))
            tt_(lo, value, f32(hi), ALU.subtract).then_inc(done, 1)
            dve.wait_ge(done, c.due(done))

        def inverse_root():
            dve.wait_ge(root_done, c.due(root_done))
            ve.reciprocal(rstd[:], rstd[:]).then_inc(dve_step, 1)
            dve.wait_ge(dve_step, c.due(dve_step))

        def normed_pair(gain):
            inverse_root()
            for k in range(KT):
                stt(tmp[:, k % 2, :], resid[:, k, :], v(gain, k), rstd[:], ALU.mult, ALU.mult).then_inc(dve_step, 1)
                dve.wait_ge(dve_step, c.due(dve_step))
                pair(h_hi[:, k, :], h_lo[:, k, :], tmp[:, k % 2, :], h_ready)

        ve.memset(eps[:], EPS).then_inc(eps_set, 1)
        dve.wait_ge(eps_set, c.due(eps_set))
        ve.memset(ones[:], 1.0).then_inc(ones_set, 1)
        dve.wait_ge(ones_set, c.due(ones_set))
        dve.wait_ge(consts_in, c.due(consts_in, 32))
        b0, b1 = v("bounds", 0, 8), v("bounds", 8, 8)
        tt_(tiny[:, 16:24], b0, b1, ALU.max).then_inc(dve_step, 1)
        dve.wait_ge(dve_step, c.due(dve_step))
        tt_(tiny[:, 0:8], b0, tiny[:, 16:24], ALU.subtract).then_inc(dve_step, 1)
        dve.wait_ge(dve_step, c.due(dve_step))
        tt_(tiny[:, 8:16], b1, tiny[:, 16:24], ALU.subtract).then_inc(bounds_shifted, 1)
        dve.wait_ge(bounds_shifted, c.due(bounds_shifted))
        dve.wait_ge(x_in, c.due(x_in, 16))
        normed_pair("norm_mix")
        dve.wait_ge(bounds_exp, c.due(bounds_exp))
        tt_(tiny[:, 16:24], tiny[:, 0:8], tiny[:, 8:16], ALU.add).then_inc(dve_step, 1)
        dve.wait_ge(dve_step, c.due(dve_step))
        ve.reciprocal(tiny[:, 16:24], tiny[:, 16:24]).then_inc(dve_step, 1)
        dve.wait_ge(dve_step, c.due(dve_step))
        tt_(tiny[:, 24:32], tiny[:, 0:8], tiny[:, 16:24], ALU.mult).then_inc(dve_step, 1)
        dve.wait_ge(dve_step, c.due(dve_step))
        ts(tiny[:, 32:40], tiny[:, 24:32], -1.0, 1.0, ALU.mult, ALU.add).then_inc(dve_step, 1)
        dve.wait_ge(dve_step, c.due(dve_step))
        dve.wait_ge(acc_read_act, c.due(acc_read_act, 8))
        for h in range(HG_HEADS):
            ts(hb[:, h, :], hk[:, h, :], tiny[:, 32 + h:33 + h], tiny[:, 24 + h:25 + h], ALU.mult, ALU.add).then_inc(dve_step, 1)
            dve.wait_ge(dve_step, c.due(dve_step))
        ts(hk[:], hb[:], -1.0, 1.0, ALU.mult, ALU.add).then_inc(f_done, 1)
        dve.wait_ge(f_done, c.due(f_done))
        dve.wait_ge(logf_done, c.due(logf_done))
        dve.wait_ge(masks_in, c.due(masks_in, 32))

        def scan(h):
            ve.tensor_tensor_scan(one(hb, h), scan_keep[:], one(hb, h), 0.0, ALU.mult, ALU.add).then_inc(decay_done, 1)
            dve.wait_ge(decay_done, c.due(decay_done))
        c.repeat(HG_HEADS, scan)
        ve.memset(att[:], 0.0).then_inc(dve_step, 1)
        dve.wait_ge(dve_step, c.due(dve_step))

        def hgrn_head(i):
            dve.wait_ge(head_ready, c.due(head_ready))
            tiles = head_b[:].rearrange("p (j n) -> p j n", n=P)
            tt_(far_e[:], tiles[:, 0:3, P - 1:P].to_broadcast((P, 3, P)), tiles[:, 0:3, :], ALU.subtract).then_inc(dve_step, 1)
            dve.wait_ge(dve_step, c.due(dve_step))
            tt_(skip[:], tiles[:, 1, P - 1:P], tiles[:, 2, P - 1:P], ALU.add).then_inc(far_e_ready, 1)
            dve.wait_ge(far_e_ready, c.due(far_e_ready))

            def halves(t, w):
                both = t.rearrange("p (b n) -> p b n", n=2 * w)
                return both[:, :, 0:w], both[:, :, w:2 * w]

            def diff(l):
                w = LEVELS[l]
                left, right = halves(head_b[:], w)
                e_left, e_right = halves(lev_e[:, l % 2, :], w)
                last = left[:, :, w - 1:w].to_broadcast((P, T // (2 * w), w))
                tt_(e_right, right, last, ALU.subtract).then_inc(dve_step, 1)
                dve.wait_ge(dve_step, c.due(dve_step))
                tt_(e_left, last, left, ALU.subtract).then_inc(lev_diff, 1)
                dve.wait_ge(lev_diff, c.due(lev_diff))

            def scaled(l):
                w = LEVELS[l]
                dve.wait_ge(lev_exp, c.due(lev_exp))
                e_left, e_right = halves(lev_e[:, l % 2, :], w)
                z_left, z_right = halves(lev_z[:, l % 2, :], w)
                tt_(z_right, halves(head_q[:], w)[1], e_right, ALU.mult).then_inc(dve_step, 1)
                dve.wait_ge(dve_step, c.due(dve_step))
                tt_(z_left, halves(head_k[:], w)[0], e_left, ALU.mult).then_inc(lev_ready, 1)
                dve.wait_ge(lev_ready, c.due(lev_ready))

            def select(l):
                c.alone()
                ve.copy_predicated(att[:].rearrange("p (j n) -> p j n", n=640)[:, :, 0:P],
                                   masks[:, l, :].bitcast(U32).unsqueeze(1).to_broadcast((P, TT, P)),
                                   bank[2 + l % 2][:].rearrange("p (j n) -> p j n", n=P)).then_inc(lev_read, 1)
                dve.wait_ge(lev_read, c.due(lev_read))

            diff(1)
            diff(2)
            dve.wait_ge(far_q_exp, c.due(far_q_exp))
            tt_(far_k[:], head_k[:, 0:384].rearrange("p (j n) -> p j n", n=P), far_e[:], ALU.mult).then_inc(dve_step, 1)
            dve.wait_ge(dve_step, c.due(dve_step))
            tt_(far_q[:, 0:384], far_q[:, 0:384], head_q[:, 128:512], ALU.mult).then_inc(dve_step, 1)
            dve.wait_ge(dve_step, c.due(dve_step))
            tt_(far_q[:, 384:640], far_q[:, 384:640], head_q[:, 256:512], ALU.mult).then_inc(dve_step, 1)
            dve.wait_ge(dve_step, c.due(dve_step))
            tt_(far_q[:, 640:768], far_q[:, 640:768], head_q[:, 384:512], ALU.mult).then_inc(far_ready, 1)
            dve.wait_ge(far_ready, c.due(far_ready))
            dve.wait_ge(o_done, c.due(o_done, 1, back=1))
            dve.wait_ge(lev_done, c.due(lev_done))
            select(0)
            scaled(1)
            for l in range(2, len(LEVELS)):
                scaled(l)
                dve.wait_ge(lev_done, c.due(lev_done))
                select(l - 1)
                if l + 1 < len(LEVELS):
                    diff(l + 1)
            dve.wait_ge(lev_done, c.due(lev_done))
            select(len(LEVELS) - 1)
        c.repeat(HG_HEADS, hgrn_head)

        dve.wait_ge(cs_in, c.due(cs_in, 32))

        def ret_head(i):
            dve.wait_ge(ret_s_done, c.due(ret_s_done, 0))
            cos, sin = cos_sin[:, 0, :], cos_sin[:, 1, :]
            for n, (src, dst) in enumerate(((rq, rot_q), (rk, rot_k))):
                x1, x2 = one(src, i * 2), one(src, i * 2 + 1)
                for m, (f1, f2, op) in enumerate(((cos, sin, ALU.subtract), (sin, cos, ALU.add))):
                    tt_(rtmp[:, 0, :], x1, f1, ALU.mult).then_inc(dve_step, 1)
                    dve.wait_ge(dve_step, c.due(dve_step))
                    tt_(rtmp[:, 1, :], x2, f2, ALU.mult).then_inc(dve_step, 1)
                    dve.wait_ge(dve_step, c.due(dve_step))
                    done = rot_ready if n == m == 1 else dve_step
                    tt_(dst[:, m, :], rtmp[:, 0, :], rtmp[:, 1, :], op).then_inc(done, 1)
                    dve.wait_ge(done, c.due(done))
            dve.wait_ge(ret_o_done, c.due(ret_o_done, 4, back=4))
            for j in range(TT):
                N = T - j * P
                dve.wait_ge(ret_s_done, c.due(ret_s_done))
                tt_(ratt[:, j * 512:j * 512 + N], bank[2 + j % 2][:, 0:N], decay[:, bass.ds(i, 1), 0:N].rearrange("p a n -> p (a n)"),
                    ALU.mult).then_inc(ret_att, 1)
                dve.wait_ge(ret_att, c.due(ret_att))
        c.repeat(RET_HEADS, ret_head)

        def hg_norm(i):
            for p in range(2):
                n = i * 2 + p
                dve.wait_ge(root_done, c.due(root_done))
                ve.reciprocal(tmp[:, p, :], tmp[:, p, :]).then_inc(dve_step, 1)
                dve.wait_ge(dve_step, c.due(dve_step))
                gain = vec[:, bass.ds(n + VEC["hg_norm"][0], 1)]
                stt(one(hq_, n), one(hq_, n), gain, tmp[:, p, :], ALU.mult, ALU.mult).then_inc(normed, 1)
                dve.wait_ge(normed, c.due(normed))
        c.repeat(HG_HEADS // 2, hg_norm)

        def ret_norm(i):
            dve.wait_ge(root_done, c.due(root_done))
            ve.reciprocal(tmp[:, 0, :], tmp[:, 0, :]).then_inc(dve_step, 1)
            dve.wait_ge(dve_step, c.due(dve_step))
            for m in range(4):
                o = rv[:, m, bass.ds(i * RET_DV, T)]
                done = normed if m == 3 else dve_step
                tt_(o, o, tmp[:, 0, :], ALU.mult).then_inc(done, 1)
                dve.wait_ge(done, c.due(done))
        c.repeat(RET_HEADS, ret_norm)

        c.base[acc_read_act.name] = ACT_READ["hg"]

        def hg_gate(i):
            for p in range(2):
                n = i * 2 + p
                dve.wait_ge(acc_read_act, c.due(acc_read_act))
                tt_(tmp[:, p, :], one(hq_, n), sq[:, p, :], ALU.mult).then_inc(dve_step, 1)
                dve.wait_ge(dve_step, c.due(dve_step))
                pair(one(oh_hi, n), one(oh_lo, n), tmp[:, p, :], gated)
        c.repeat(4, hg_gate)
        dve.wait_ge(acc_read_act, c.due(acc_read_act, 8))
        c.base[tile_done.name] = START["w_hg"]

        def branch_hg(i):
            for p in range(2):
                dve.wait_ge(tile_done, c.due(tile_done))
                g = one(ga, i * 2 + p)
                tt_(g, g, bank[p][:], ALU.mult).then_inc(acc_read_dve, 1)
                dve.wait_ge(acc_read_dve, c.due(acc_read_dve))
        c.repeat(4, branch_hg)
        dve.wait_ge(acc_read_act, c.due(acc_read_act, 8))
        for half in range(2):
            def ret_gate(i):
                for m in range(4):
                    dve.wait_ge(acc_read_act, c.due(acc_read_act))
                    o = rv[:, m, bass.ds((i + half * 2) * RET_DV, T)]
                    tt_(tmp[:, m % 2, :], o, sq[:, m % 2, :], ALU.mult).then_inc(dve_step, 1)
                    dve.wait_ge(dve_step, c.due(dve_step))
                    pair(one(or_hi, (i + half * 2) * 4 + m), one(or_lo[half], i * 4 + m), tmp[:, m % 2, :], gated)
            c.repeat(2, ret_gate)
        c.base[tile_done.name] = START["w_ret"]

        def merge(i):
            for p in range(2):
                n = i * 2 + p
                dve.wait_ge(tile_done, c.due(tile_done, 2))
                tt_(one(gb, n), one(gb, n), bank[p][:], ALU.mult).then_inc(acc_read_dve, 1)
                dve.wait_ge(acc_read_dve, c.due(acc_read_dve))
                tt_(tmp[:, p, :], one(ga, n), one(gb, n), ALU.add).then_inc(dve_step, 1)
                dve.wait_ge(dve_step, c.due(dve_step))
                pair(one(h_hi, n), one(h_lo, n), tmp[:, p, :], h_ready)
        c.repeat(4, merge)
        dve.wait_ge(x_in, c.due(x_in, 16))

        def to_residual(n):
            def two(i):
                for p in range(2):
                    dve.wait_ge(tile_done, c.due(tile_done))
                    r = one(resid, i * 2 + p)
                    tt_(r, r, bank[p][:], ALU.add).then_inc(acc_read_dve, 1)
                    dve.wait_ge(acc_read_dve, c.due(acc_read_dve))
            c.repeat(n // 2, two)
        to_residual(8)
        normed_pair("norm_ffn")

        NEG = -3.0e38

        def best16(values, top, index):
            ve.max(top[:, 0:8], values).then_inc(dve_step, 1)
            dve.wait_ge(dve_step, c.due(dve_step))
            ve.max_index(index[:, 0:8], top[:, 0:8], values).then_inc(dve_step, 1)
            dve.wait_ge(dve_step, c.due(dve_step))
            ve.match_replace(values, top[:, 0:8], values, NEG).then_inc(dve_step, 1)
            dve.wait_ge(dve_step, c.due(dve_step))
            ve.max(top[:, 8:16], values).then_inc(dve_step, 1)
            dve.wait_ge(dve_step, c.due(dve_step))
            ve.max_index(index[:, 8:16], top[:, 8:16], values).then_inc(dve_step, 1)
            dve.wait_ge(dve_step, c.due(dve_step))

        def token_tile(tt):
            dve.wait_ge(scores_copied, c.due(scores_copied))
            for n in range(16):
                best16(tile_scores[:, n, :], top_s[:, n, :], top_u[:, n, :])
            ve.tensor_copy(top_f[:], top_u[:]).then_inc(dve_step, 1)
            dve.wait_ge(dve_step, c.due(dve_step))
            by_half = top_s[:].rearrange("p (h two) r -> p two h r", two=2)
            shape = (P, PEER_HEADS, TOPK, TOPK)
            tt_(cand[:].rearrange("p h (a b) -> p h a b", b=TOPK), by_half[:, 0].unsqueeze(3).to_broadcast(shape),
                by_half[:, 1].unsqueeze(2).to_broadcast(shape), ALU.add).then_inc(dve_step, 1)
            dve.wait_ge(dve_step, c.due(dve_step))
            for h in range(PEER_HEADS):
                best16(cand[:, h, :], best_s[:, h, :], best_u[:, h * TOPK:h * TOPK + TOPK])
            ve.tensor_copy(denom[:, 0, :], best_s[:, :, 0]).then_inc(dve_step, 1)
            dve.wait_ge(dve_step, c.due(dve_step))
            tt_(best_s[:], best_s[:], denom[:, 0, :].unsqueeze(2).to_broadcast((P, PEER_HEADS, TOPK)), ALU.subtract).then_inc(best_shifted, 1)
            dve.wait_ge(best_shifted, c.due(best_shifted))
            ts(row_u[:], best_u[:], 4, None, ALU.logical_shift_right).then_inc(dve_step, 1)
            dve.wait_ge(dve_step, c.due(dve_step))
            ve.tensor_copy(row_f[:, 0, :], row_u[:]).then_inc(dve_step, 1)
            dve.wait_ge(dve_step, c.due(dve_step))
            ts(row_u[:], best_u[:], 15, None, ALU.bitwise_and).then_inc(dve_step, 1)
            dve.wait_ge(dve_step, c.due(dve_step))
            ve.tensor_copy(row_f[:, 1, :], row_u[:]).then_inc(dve_step, 1)
            dve.wait_ge(dve_step, c.due(dve_step))
            keys_by_half = top_f[:].rearrange("p (h two) r -> p two h r", two=2)
            for n in range(2):
                tt_(pick[:], row_f[:, n, :].unsqueeze(2).to_broadcast((P, CHOICES, TOPK)),
                    t_("iota16").unsqueeze(1).to_broadcast((P, CHOICES, TOPK)), ALU.is_equal).then_inc(dve_step, 1)
                dve.wait_ge(dve_step, c.due(dve_step))
                tt_(pick[:].rearrange("p (h k) r -> p h k r", k=TOPK), pick[:].rearrange("p (h k) r -> p h k r", k=TOPK),
                    keys_by_half[:, n].unsqueeze(2).to_broadcast(shape), ALU.mult).then_inc(dve_step, 1)
                dve.wait_ge(dve_step, c.due(dve_step))
                ve.tensor_reduce(chosen[:, n, :], pick[:], AX.X, ALU.add).then_inc(dve_step, 1)
                dve.wait_ge(dve_step, c.due(dve_step))
            dve.wait_ge(best_exp, c.due(best_exp))
            ve.tensor_reduce(denom[:, 0, :], best_s[:], AX.X, ALU.add).then_inc(dve_step, 1)
            dve.wait_ge(dve_step, c.due(dve_step))
            ve.reciprocal(denom[:, 1, :], denom[:, 0, :]).then_inc(dve_step, 1)
            dve.wait_ge(dve_step, c.due(dve_step))
            tt_(chosen[:, 2, :].rearrange("p (h k) -> p h k", k=TOPK), best_s[:],
                denom[:, 1, :].unsqueeze(2).to_broadcast((P, PEER_HEADS, TOPK)), ALU.mult).then_inc(chosen_done, 1)
            dve.wait_ge(chosen_done, c.due(chosen_done))
            dve.wait_ge(turned, c.due(turned))
            dve.wait_ge(hot_gated, c.due(hot_gated, P // TOKENS_PER_BATCH, back=P // TOKENS_PER_BATCH))
            ve.tensor_copy(chosen_t[:], bank[6][:, 0:3 * P].rearrange("p (a n) -> p a n", n=P)).then_inc(dve_step, 1)
            dve.wait_ge(dve_step, c.due(dve_step))

            def two(i):
                for p in range(2):
                    dve.wait_ge(batch_done, c.due(batch_done, 1, back=2))
                    at = bass.ds((i * 2 + p) * TOKENS_PER_BATCH, TOKENS_PER_BATCH)
                    big = (P, TOKENS_PER_BATCH, NKEYS)
                    for key, hot, done in ((1, hot2, dve_step), (0, hot1, hot_ready)):
                        tt_(hot[:, p], chosen_t[:, key, at].unsqueeze(2).to_broadcast(big),
                            t_("iota128").unsqueeze(1).to_broadcast(big), ALU.is_equal).then_inc(done, 1)
                        dve.wait_ge(done, c.due(done))
            c.repeat(P // TOKENS_PER_BATCH // 2, two)
        for tt in range(TT):
            token_tile(tt)

        c.base[acc_read_act.name] = ACT_READ["experts"]
        c.base[tile_done.name] = START["experts"]

        def group(g):
            def four(i):
                for s in range(4):
                    dve.wait_ge(acc_read_act, c.due(acc_read_act))
                    dve.wait_ge(gate_in[s], c.due(gate_in[s], 16))
                    e = one(expert_w, i * 4 + s)
                    tt_(e, e, g_in[:, s, :], ALU.mult).then_inc(weighted, 1)
                    dve.wait_ge(weighted, c.due(weighted))
            c.repeat(GROUP // 4, four)
            dve.wait_ge(tile_done, c.due(tile_done, GROUP))
            for half in range(2):
                def values(i):
                    for e in range(4):
                        dve.wait_ge(ew_hi_ready, c.due(ew_hi_ready))
                        tt_(ew_lo[:, e % 2, :], one(expert_w, i * 4 + e), f32(ew_hi[:, e % 2, :]), ALU.subtract).then_inc(ew_ready, 1)
                        dve.wait_ge(ew_ready, c.due(ew_ready))
                c.repeat(GROUP // 4, values)
                dve.wait_ge(tile_done, c.due(tile_done, GROUP // 2))
                for m in range(4):
                    r = resid[:, half * 4 + m, :]
                    tt_(r, r, bank[(2 + half * 4 + m) % 8][:], ALU.add).then_inc(x_added, 1)
                    dve.wait_ge(x_added, c.due(x_added))
        c.repeat(NKEYS // GROUP, group)
        inverse_root()
        for k in range(KT):
            stt(resid[:, k, :], resid[:, k, :], v("final", k), rstd[:], ALU.mult, ALU.mult).then_inc(resid_ready, 1)
            dve.wait_ge(resid_ready, c.due(resid_ready))

        normed_pair("norm1")
        lam, u, z, z2, s = v("lam", 0, 4), tiny[:, 0:4], tiny[:, 4:8], tiny[:, 8:12], tiny[:, 12:16]
        ts(z, lam, -1.0, None, ALU.mult).then_inc(dve_step, 1)
        dve.wait_ge(dve_step, c.due(dve_step))
        tt_(z, z, lam, ALU.min).then_inc(lam_abs, 1)
        dve.wait_ge(lam_abs, c.due(lam_abs))
        dve.wait_ge(lam_exp, c.due(lam_exp))
        ts(z2, u, 2.0, None, ALU.add).then_inc(dve_step, 1)
        dve.wait_ge(dve_step, c.due(dve_step))
        ve.reciprocal(z2, z2).then_inc(dve_step, 1)
        dve.wait_ge(dve_step, c.due(dve_step))
        tt_(z, u, z2, ALU.mult).then_inc(dve_step, 1)
        dve.wait_ge(dve_step, c.due(dve_step))
        tt_(z2, z, z, ALU.mult).then_inc(dve_step, 1)
        dve.wait_ge(dve_step, c.due(dve_step))
        ts(s, z2, 1.0 / 17, 1.0 / 15, ALU.mult, ALU.add).then_inc(dve_step, 1)
        dve.wait_ge(dve_step, c.due(dve_step))
        for odd in (13, 11, 9, 7, 5, 3, 1):
            tt_(s, s, z2, ALU.mult).then_inc(dve_step, 1)
            dve.wait_ge(dve_step, c.due(dve_step))
            ts(s, s, 1.0 / odd, None, ALU.add).then_inc(dve_step, 1)
            dve.wait_ge(dve_step, c.due(dve_step))
        tt_(s, s, z, ALU.mult).then_inc(dve_step, 1)
        dve.wait_ge(dve_step, c.due(dve_step))
        ts(u, lam, -1.0, 0.0, ALU.mult, ALU.max).then_inc(dve_step, 1)
        dve.wait_ge(dve_step, c.due(dve_step))
        stt(s, s, 2.0, u, ALU.mult, ALU.add).then_inc(dve_step, 1)
        dve.wait_ge(dve_step, c.due(dve_step))
        ts(tiny[:, 48:52], s, 8.0, None, ALU.mult).then_inc(dve_step, 1)
        dve.wait_ge(dve_step, c.due(dve_step))
        qk = v("lam_qk", 0, 128).rearrange("p (a n) -> p a n", n=32)
        tt_(tmp[:, 0, 0:64].rearrange("p (a n) -> p a n", n=32), qk[:, 0::2, :], qk[:, 1::2, :], ALU.mult).then_inc(dve_step, 1)
        dve.wait_ge(dve_step, c.due(dve_step))
        ve.tensor_reduce(tiny[:, 56:58], tmp[:, 0, 0:64].rearrange("p (a n) -> p a n", n=32), AX.X, ALU.add).then_inc(dve_step, 1)
        dve.wait_ge(dve_step, c.due(dve_step))
        ts(tiny[:, 52:56], s, -8.0, None, ALU.mult).then_inc(softplus_done, 1)
        dve.wait_ge(softplus_done, c.due(softplus_done))
        c.base[acc_read_act.name] = ACT_READ["in_2"]
        dve.wait_ge(acc_read_act, c.due(acc_read_act, 16))
        for n in range(LRU_TILES):
            xa = in2[:, n, :]
            y = lru[0]
            ts(y[:], xa, v("conv_a_w", 12 + n), v("conv_a_b", n), ALU.mult, ALU.add).then_inc(dve_step, 1)
            dve.wait_ge(dve_step, c.due(dve_step))
            for back in (1, 2, 3):
                done = conv_done if back == 3 else dve_step
                stt(y[:, back:T], xa[:, 0:T - back], v("conv_a_w", (3 - back) * 4 + n), y[:, back:T], ALU.mult, ALU.add).then_inc(done, 1)
                dve.wait_ge(done, c.due(done))
            dve.wait_ge(lru_decays, c.due(lru_decays))
            tt_(lru[1][:], lru[3][:], lru[3][:], ALU.mult).then_inc(dve_step, 1)
            dve.wait_ge(dve_step, c.due(dve_step))
            stt(lru[4][:], lru[1][:], 1.0, lru[4][:], ALU.add, ALU.mult).then_inc(lru_var, 1)
            dve.wait_ge(lru_var, c.due(lru_var))
            tt_(lru[2][:], lru[2][:], y[:], ALU.mult).then_inc(dve_step, 1)
            dve.wait_ge(dve_step, c.due(dve_step))
            dve.wait_ge(lru_root, c.due(lru_root))
            tt_(lru[2][:], lru[2][:], lru[4][:], ALU.mult).then_inc(dve_step, 1)
            dve.wait_ge(dve_step, c.due(dve_step))
            ve.tensor_tensor_scan(lru[1][:], lru[3][:], lru[2][:], 0.0, ALU.mult, ALU.add).then_inc(dve_step, 1)
            dve.wait_ge(dve_step, c.due(dve_step))
            dve.wait_ge(lru_gelu, c.due(lru_gelu))
            tt_(lru[1][:], lru[1][:], lru[5][:], ALU.mult).then_inc(dve_step, 1)
            dve.wait_ge(dve_step, c.due(dve_step))
            pair(mix_hi[:, n, :], mix_lo[:, n, :], lru[1][:], mixed_ready)
        for h in range(SB_HEADS):
            for j in range(TT):
                N = T - j * P
                dve.wait_ge(sb_z_done, c.due(sb_z_done))
                ts(sbz[:, j, 0:N], bank[2 + j][:, 0:N], SB_DH ** -0.5, None, ALU.mult).then_inc(sb_z_read, 1)
                dve.wait_ge(sb_z_read, c.due(sb_z_read))
            dve.wait_ge(sb_o_done, c.due(sb_o_done, 1, back=1))
            for j in range(TT):
                N = T - j * P
                dve.wait_ge(sb_ln, c.due(sb_ln))
                stt(sbw[:, j, 0:N], sbz[:, j, 0:N], 0.0, sbt[:, j % 2, 0:N], ALU.max, ALU.add).then_inc(dve_step, 1)
                dve.wait_ge(dve_step, c.due(dve_step))
                tt_(sbz[:, j, 0:N], sbz[:, j, 0:N], sbw[:, j, 0:N], ALU.subtract).then_inc(dve_step, 1)
                dve.wait_ge(dve_step, c.due(dve_step))
                tt_(sbw[:, j, 0:P], sbw[:, j, 0:P], t_("earlier"), ALU.mult).then_inc(sb_sp_ready, 1)
                dve.wait_ge(sb_sp_ready, c.due(sb_sp_ready))
            for j in range(TT):
                N = T - j * P
                dve.wait_ge(sb_tail_done, c.due(sb_tail_done))
                tt_(sbz[:, j, 0:N], sbz[:, j, 0:N], bank[j % 2][:, 0:N], ALU.subtract).then_inc(sb_tail_read, 1)
                dve.wait_ge(sb_tail_read, c.due(sb_tail_read))
            for j in range(TT):
                dve.wait_ge(sb_exp, c.due(sb_exp))
                tt_(sbw[:, j, 0:P], sbw[:, j, 0:P], t_("earlier"), ALU.mult).then_inc(sb_w_ready, 1)
                dve.wait_ge(sb_w_ready, c.due(sb_w_ready))
            if h % 2:
                dve.wait_ge(sb_o_done, c.due(sb_o_done, 0))
                ve.tensor_copy(mix_hi[:, 4 + h // 2, :], bank[6][:]).then_inc(dve_step, 1)
                dve.wait_ge(dve_step, c.due(dve_step))
                tt_(mix_lo[:, 4 + h // 2, :], bank[6][:], f32(mix_hi[:, 4 + h // 2, :]), ALU.subtract).then_inc(sb_o_read, 1)
                dve.wait_ge(sb_o_read, c.due(sb_o_read))
        dve.wait_ge(lam_ready, c.due(lam_ready))
        dve.wait_ge(distance_in, c.due(distance_in, 16))
        tt_(tiny[:, 60:61], tiny[:, 58:59], tiny[:, 59:60], ALU.subtract).then_inc(dve_step, 1)
        dve.wait_ge(dve_step, c.due(dve_step))
        ts(tiny[:, 60:61], tiny[:, 60:61], LAM_INIT, -1.0, ALU.add, ALU.mult).then_inc(dve_step, 1)
        dve.wait_ge(dve_step, c.due(dve_step))
        for h in range(DF_HEADS):
            slope = 2.0 ** (-8.0 * (h + 1) / DF_HEADS) * DF_DQK ** 0.5
            for i in range(TT):
                N = (i + 1) * P
                st = [df_stat[:, k:k + 1] for k in range(16)]
                for q in range(2):
                    dve.wait_ge(df_s_done, c.due(df_s_done))
                    stt(dfs[:, q, 0:N], distance[:, T - N:T], -slope, bank[2 + q][:, 0:N], ALU.mult, ALU.add).then_inc(df_s_read, 1)
                    dve.wait_ge(df_s_read, c.due(df_s_read))
                    ve.reduce_max(st[q], dfs[:, q, 0:N], AX.X).then_inc(dve_step, 1)
                    dve.wait_ge(dve_step, c.due(dve_step))
                    ts(st[2 + q], st[q], -(DF_DQK ** -0.5), None, ALU.mult).then_inc(df_max, 1)
                    dve.wait_ge(df_max, c.due(df_max))
                dve.wait_ge(df_exp, c.due(df_exp, 2))
                ve.reciprocal(df_stat[:, 6:8], df_stat[:, 4:6]).then_inc(dve_step, 1)
                dve.wait_ge(dve_step, c.due(dve_step))
                tt_(st[8], st[7], tiny[:, 60:61], ALU.mult).then_inc(dve_step, 1)
                dve.wait_ge(dve_step, c.due(dve_step))
                dve.wait_ge(df_pt_done, c.due(df_pt_done, 1, back=1))
                ts(dfp[:, 0:N], dfe[:, 0, 0:N], st[6], None, ALU.mult).then_inc(dve_step, 1)
                dve.wait_ge(dve_step, c.due(dve_step))
                stt(dfp[:, 0:N], dfe[:, 1, 0:N], st[8], dfp[:, 0:N], ALU.mult, ALU.add).then_inc(df_p_ready, 1)
                dve.wait_ge(df_p_ready, c.due(df_p_ready))
            if h % 2:
                inverse_root()
                n = 6 + h // 2
                stt(tmp[:, 0, :], dfo[:, h // 2, :], v("subln"), rstd[:], ALU.mult, ALU.mult).then_inc(dve_step, 1)
                dve.wait_ge(dve_step, c.due(dve_step))
                ts(tmp[:, 0, :], tmp[:, 0, :], 1.0 - LAM_INIT, None, ALU.mult).then_inc(dve_step, 1)
                dve.wait_ge(dve_step, c.due(dve_step))
                pair(mix_hi[:, n, :], mix_lo[:, n, :], tmp[:, 0, :], mixed_ready)
        c.base[tile_done.name] = START["out_2"]
        to_residual(8)
        normed_pair("norm2")

        def ff(i):
            for p in range(2):
                dve.wait_ge(tile_done, c.due(tile_done))
                n = i * 2 + p
                w = [vec[:, bass.ds(n + VEC["conv_ff_w"][0] + k * 2 * FF_TILES, 1)] for k in range(3)]
                b = vec[:, bass.ds(n + VEC["conv_ff_b"][0], 1)]
                acc, y = bank[p], conv[:, p, :]
                if p == 0:
                    dve.wait_ge(ff_silu, c.due(ff_silu, 1, back=1))
                ts(y, acc[:], w[2], b, ALU.mult, ALU.add).then_inc(dve_step, 1)
                dve.wait_ge(dve_step, c.due(dve_step))
                stt(y[:, 1:T], acc[:, 0:T - 1], w[1], y[:, 1:T], ALU.mult, ALU.add).then_inc(dve_step, 1)
                dve.wait_ge(dve_step, c.due(dve_step))
                stt(y[:, 2:T], acc[:, 0:T - 2], w[0], y[:, 2:T], ALU.mult, ALU.add).then_inc(acc_read_dve, 1)
                dve.wait_ge(acc_read_dve, c.due(acc_read_dve))
            dve.wait_ge(ff_silu, c.due(ff_silu, 0))
            tt_(tmp[:, 0, :], act_g[:, 0, :], conv[:, 1, :], ALU.mult).then_inc(dve_step, 1)
            dve.wait_ge(dve_step, c.due(dve_step))
            pair(one(ff_hi, i), one(ff_lo, i), tmp[:, 0, :], ff_ready)
        c.repeat(FF_TILES, ff)
        dve.wait_ge(tile_done, c.due(tile_done, FF_TILES))
        for n in range(KT):
            tt_(resid[:, n, :], resid[:, n, :], bank[n][:], ALU.add).then_inc(down_read, 1)
            dve.wait_ge(down_read, c.due(down_read))
        inverse_root()
        for k in range(KT):
            stt(final[:, k, :], resid[:, k, :], v("final2", k), rstd[:], ALU.mult, ALU.mult).then_inc(final_done, 1)
            dve.wait_ge(final_done, c.due(final_done))

    block.__exit__(None, None, None)


def tables_of_shapes():
    f = np.float32
    tab = np.zeros((P, N_TAB), f)

    def put(name, value):
        tab[:, TAB[name][0]:TAB[name][0] + TAB[name][1]] = value
    p, q = np.arange(P)[:, None], np.arange(P)[None, :]
    put("identity", p == q)
    put("later", p > q)
    put("earlier", p < q)
    put("halves", p // 64 == q // 64)
    u = np.arange(T)[None, :] - (T - P)
    put("distance", np.where((u // 64) <= (p // 64), np.abs(p - u), 1e30))
    put("iota16", np.arange(16)[None, :])
    put("iota128", q)
    put("scan_keep", np.arange(T)[None, :] % P != 0)
    half = RET_DK // 2
    inv = f(10000.0) ** (-np.arange(half, dtype=f) / f(half))
    angle = inv[:, None] * np.arange(T, dtype=f)[None, :]
    put("cos", np.cos(angle))
    put("sin", np.sin(angle))
    log_g = np.log(f(1.0) - np.exp2(f(-5.0) - np.arange(RET_HEADS, dtype=f)))
    rel = np.arange(T, dtype=f)[None, :] - np.arange(P, dtype=f)[:, None]
    put("decay", np.concatenate([np.where(rel >= 0, np.exp(log_g[h] * np.maximum(rel, 0)), 0) for h in range(RET_HEADS)], axis=1))
    masks = np.zeros((P, len(LEVELS), P), f)
    for n, w in enumerate(LEVELS):
        if w == 0:
            masks[:, n] = p == q
        else:
            masks[:, n] = (p // (2 * w) == q // (2 * w)) & (p % (2 * w) < w) & (q % (2 * w) >= w)
    put("levels", masks.reshape(P, -1))
    return tab


def kernel(**inputs):
    import concourse.bacc as bacc
    from concourse.bass_utils import run_bass_kernel_spmd

    a = {k: np.asarray(v) for k, v in inputs.items()}

    def fm(w, n=None):
        k, n = w.shape
        t = w.reshape(k // P, P, n // P, P).transpose(2, 1, 0, 3)
        return t.reshape(n // P, P, k // 1024, 1024).transpose(0, 2, 1, 3).reshape(-1, P, 1024)

    def tm(w):
        k, n = w.shape
        return w.reshape(4, 2, P, n // 512, 512).transpose(3, 0, 2, 1, 4).reshape(-1, P, 1024)

    def cols(t):
        return t.reshape(-1, P).T

    w_in = a["w_in"][0]
    at = np.cumsum([0, 1024, 1024, 1024, 1024, 1024, 1024, 2048, 2048, 1024, 1024])
    hq, hf, hi, hg, rq, rk, rv, rg, gate_a, gate_b = (w_in[:, at[n]:at[n + 1]] for n in range(10))
    w2 = a["w_in_2"][0]
    at = np.cumsum([0, 512, 512, 256, 256, 256, 256, 256, 256])
    xa, ya, sq, sk, sv, dq, dk, dv = (w2[:, at[n]:at[n + 1]] for n in range(8))
    u_tiles = a["expert_u"][0].reshape(NKEYS, P, KT, P).transpose(0, 3, 2, 1).reshape(NKEYS // GROUP, GROUP, P, 1024)
    v_tiles = a["expert_v"][0].reshape(NKEYS // GROUP, GROUP // 2, 2, P, 2, 512).transpose(0, 4, 1, 3, 2, 5).reshape(
        NKEYS // GROUP, GROUP, P, 1024)
    experts = np.concatenate([u_tiles, v_tiles], axis=1).reshape(-1, P, 1024)
    up = fm(a["w_ff_up_2"][0]).reshape(2, FF_TILES, P, 1024).transpose(1, 0, 2, 3).reshape(-1, P, 1024)
    rqk = np.stack([fm(rq), fm(rk)], axis=1).reshape(-1, P, 1024)
    weights = np.concatenate([
        fm(hf), fm(hq), tm(hi), rqk, tm(rv), fm(hg), fm(gate_a), fm(a["w_branch_hg"][0]), fm(gate_b), fm(rg),
        fm(a["w_branch_ret"][0]), fm(a["w_out"][0]), fm(a["peer_w_q"][0]), experts,
        fm(np.concatenate([xa, ya, sq, sk, dq, dk], axis=1)), tm(np.concatenate([sv, dv], axis=1)), fm(a["w_out_2"][0]),
        up, a["w_ff_down_2"][0].reshape(FF_TILES, P, 1024)])
    conv_w = a["conv_ff_w_2"][0].reshape(3, 2, FF_TILES, P).transpose(3, 0, 2, 1).reshape(P, -1)
    conv_b = a["conv_ff_b_2"][0].reshape(2, FF_TILES, P).transpose(2, 1, 0).reshape(P, -1)
    lam_qk = np.concatenate([a[f"lam_{n}_2"][0] for n in ("q1", "k1", "q2", "k2")])
    vectors = np.concatenate([
        cols(a["norm_mix_w"]), cols(a["hg_lower_bounds"]), cols(a["hg_norm_w"]), cols(a["norm_ffn_w"]),
        cols(a["final_norm_w"]), cols(a["norm1_g_2"]), cols(a["conv_a_w_2"]), cols(a["conv_a_b_2"]),
        cols(a["b_rgate_2"]), cols(a["b_igate_2"]), cols(a["lru_lambda_2"]),
        np.tile(a["subln_g_2"][0], 2)[:, None], cols(a["norm2_g_2"]), conv_w, conv_b, cols(a["final_g_2"]),
        np.broadcast_to(lam_qk, (P, 128))], axis=1)
    gates_2 = np.zeros((P, 8, P), np.float32)
    for g, name in enumerate(("w_rgate_2", "w_igate_2")):
        for n in range(8):
            r = 64 * (n % 2)
            gates_2[r:r + 64, g * 4 + n // 2, r:r + 64] = a[name][0, n]
    tab = tables_of_shapes()
    arrays = {
        "x": a["x"][0].T.reshape(KT, P, T).transpose(1, 0, 2),
        "weights": weights,
        "vectors": vectors,
        "tables": tab,
        "keys": a["peer_sub_keys"][0].reshape(16, NKEYS, P).transpose(2, 0, 1),
        "lru_gates": gates_2,
    }
    nc = bacc.Bacc("TRN2", target_bir_lowering=False, num_devices=1)
    arrays = {k: np.ascontiguousarray(v) for k, v in arrays.items()}
    aps = {k: nc.dram_tensor(k, v.shape, mybir.dt.from_np(v.dtype), kind="ExternalInput").ap() for k, v in arrays.items()}
    out = nc.dram_tensor("out", (P, KT, T), F32, kind="ExternalOutput").ap()
    build(nc, **aps, out=out)
    got = run_bass_kernel_spmd(nc, [arrays], core_ids=[0]).results[0]["out"]
    return np.ascontiguousarray(got.transpose(2, 1, 0).reshape(1, T, D))
```

```python
import numpy as np
import concourse.bass as bass
from concourse import mybir

F32 = mybir.dt.float32
F32R = mybir.dt.float32r
U32 = mybir.dt.uint32
ACT = mybir.ActivationFunctionType
ALU = mybir.AluOpType
AX = mybir.AxisListType

P = 128
D = 1024
T = 512
KT = D // P
TT = T // P
EPS = 1e-6
HG_HEADS, HG_DK = 8, 128
RET_HEADS, RET_DK, RET_DV = 4, 256, 512
PEER_HEADS, TOPK, NKEYS = 8, 16, 128
CHOICES = PEER_HEADS * TOPK
FULL_ROWS, SHORT = 4, 4
CANDS = FULL_ROWS * TOPK + (TOPK - FULL_ROWS) * SHORT
GROUP = 32
FIRST_KEYS = (8, 4, 4, 2, 4, 2, 2, 2)
TOKENS_PER_BATCH = 4
HOTS = 4
STAGED_TOKENS = 64
LOTS = P // STAGED_TOKENS
LOT_BATCHES = STAGED_TOKENS // TOKENS_PER_BATCH
LRU_TILES = 4
SB_HEADS, SB_DH = 4, 64
DF_HEADS, DF_DV, DF_DQK = 4, 64, 32
FF = 2816
FF_TILES = FF // P
LAM_INIT = 0.8 - 0.6 * float(np.exp(-0.3 * 0))
LEVELS = [0, 64, 32, 16, 8, 4, 2, 1]

VEC = {}
_at = 0
for _name, _n in (("norm_mix", 8), ("bounds", 16), ("hg_norm", 8), ("norm_ffn", 8), ("final", 8),
                  ("norm1", 8), ("conv_a_w", 16), ("conv_a_b", 4), ("b_r", 4), ("b_i", 4), ("lam", 4),
                  ("subln", 1), ("norm2", 8), ("conv_ff_w", 3 * 2 * FF_TILES), ("conv_ff_b", 2 * FF_TILES),
                  ("final2", 8), ("lam_qk", 128)):
    VEC[_name] = (_at, _n)
    _at += _n
N_VEC = _at

TAB = {}
_at = 0
for _name, _n in (("identity", 128), ("later", 128), ("earlier", 128), ("halves", 128), ("iota16", 16), ("iota128", 128),
                  ("cos", 512), ("sin", 512), ("decay", RET_HEADS * 512), ("scan_keep", 512), ("distance", 512), ("levels", 8 * 128)):
    TAB[_name] = (_at, _n)
    _at += _n
N_TAB = _at

STREAM = (("hf", 8), ("hq", 8), ("hi", 8), ("rqk", 16), ("rv", 16), ("gates", 16), ("hg", 8), ("w_hg", 8),
          ("rg", 16), ("w_ret", 16), ("w_out", 8), ("peer_q", 16), ("experts", 256),
          ("in_2", 12), ("values_2", 4), ("late_2", 4), ("out_2", 8), ("up", 44), ("down", 22))
N_STREAM = sum(n for _, n in STREAM)
RAW = 4


class Count:

    def __init__(self, eng, passed):
        self.eng, self.passed, self.base, self.loops = eng, passed, {}, []

    def alone(self):
        if self.loops:
            self.eng.sem_inc(self.passed, 1)

    def due(self, sem, n=1, back=0):
        self.base[sem.name] = self.base.get(sem.name, 0) + n
        value = least = self.base[sem.name] - back
        for reg, deltas, first in self.loops:
            step = deltas.get(sem.name, 0)
            if step:
                value = value + reg * step
                least += step * first
        assert least >= 0 or isinstance(value, int), sem.name
        return max(value, 0) if isinstance(value, int) else value

    def once(self, body, *args):
        before = dict(self.base)
        body(*args)
        self.delta = {s: v - before.get(s, 0) for s, v in self.base.items() if v != before.get(s, 0)}

    def loop(self, first, end, body):
        start, delta = dict(self.base), self.delta
        self.alone()
        self.base = {s: v - first * delta.get(s, 0) for s, v in start.items()}
        with self.eng.Fori(first, end) as i:
            self.loops.append((i, delta, first))
            body(i)
            self.loops.pop()
        self.base = {s: v + (end - first) * delta.get(s, 0) for s, v in start.items()}

    def repeat(self, n, body):
        self.once(body, 0)
        if n > 1:
            self.loop(1, n, body)


def build(nc, x, weights, vectors, tables, keys, lru_gates, out):
    top = nc.sbuf_base + (-nc.sbuf_base) % 64
    limit = nc.sbuf_usable_end

    def place(name, shape, at, dtype=F32):
        size = int(np.prod(shape[1:])) * 4
        assert top + at + size <= limit, (name, top + at + size, limit)
        return nc.alloc_sbuf_tensor_at(name, shape, dtype, offset=top + at)

    KB = 1024
    w_raw = place("w_raw", [P, RAW, 1024], 0)
    w_hi = place("w_hi", [P, 2, 1024], 16 * KB, F32R)
    w_lo = place("w_lo", [P, 2, 1024], 24 * KB, F32R)
    h_hi = place("h_hi", [P, KT, T], 32 * KB, F32R)
    h_lo = place("h_lo", [P, KT, T], 48 * KB, F32R)
    X0 = 64 * KB
    resid = place("resid", [P, KT, T], X0)
    SMALL = 80 * KB
    rstd = place("rstd", [P, T], SMALL)
    sq = place("sq", [P, 2, T], SMALL + 2 * KB)
    tmp = place("tmp", [P, 2, T], SMALL + 6 * KB)
    normed_x = place("normed_x", [P, 4, T], SMALL + 2 * KB)
    ones = place("ones", [P, P], SMALL + 10 * KB)
    eps = place("eps", [P, 1], SMALL + 10 * KB + 512)
    tiny = place("tiny", [P, 64], SMALL + 10 * KB + 576)
    vec = place("vec", [P, N_VEC], SMALL + 10 * KB + 832)
    TAB0 = SMALL + 10 * KB + 832 + 4 * N_VEC + (-4 * N_VEC) % 64
    tab = place("tab", [P, TAB["cos"][0]], TAB0)
    A0 = TAB0 + 4 * TAB["cos"][0]
    A0 += -A0 % 32

    def v(name, i=0, n=1):
        return vec[:, VEC[name][0] + i:VEC[name][0] + i + n]

    def t_(name):
        return tab[:, TAB[name][0]:TAB[name][0] + TAB[name][1]]

    hq_ = place("hg_q_then_o", [P, HG_HEADS, T], A0)
    rq = place("ret_q", [P, 8, T], A0 + 16 * KB)
    rk = place("ret_k", [P, 8, T], A0 + 32 * KB)
    hb = place("hg_log_decay", [P, HG_HEADS, T], A0 + 48 * KB)
    hk = place("hg_k", [P, HG_HEADS, T], A0 + 64 * KB)
    hv = place("hg_v", [P, TT, HG_HEADS * 128], X0)
    W0 = A0 + 80 * KB
    att = place("hg_att", [P, TT * 640], W0)
    head_k = [place(f"head_k{p}", [P, T], W0 + (10 + 2 * p) * KB) for p in range(2)]
    head_v = [place(f"head_v{p}", [P, TT, 128], W0 + (14 + 2 * p) * KB) for p in range(2)]
    far_k = place("far_k", [P, 3, 128], W0 + 18 * KB)
    far_q = place("far_q", [P, 768], W0 + 20 * KB)
    masks = place("masks", [P, len(LEVELS), P], W0 + 23 * KB)
    skip = place("skip", [P, 1], W0 + 27 * KB)
    scan_keep = place("scan_keep", [P, T], W0 + 16 * KB)
    far_e = place("far_e", [P, 3, 128], W0 + 28 * KB)
    lev_e, lev_z = tmp, sq
    rv = place("ret_v_then_o", [P, TT, RET_HEADS * RET_DV], A0 + 48 * KB)
    rot_q = place("rot_q", [P, 2, T], W0)
    rot_k = place("rot_k", [P, 2, T], W0 + 4 * KB)
    ratt = place("ret_att", [P, TT * 512], W0 + 8 * KB)
    cos_sin = place("cos_sin", [P, 2, T], W0 + 16 * KB)
    rtmp = place("ret_tmp", [P, 2, T], W0 + 20 * KB)
    rvh = place("ret_head_v", [P, TT, RET_DV], X0)
    decay = place("decay", [P, RET_HEADS, T], X0 + 8 * KB)
    oh_hi = place("o_hg_hi", [P, 8, T], W0, F32R)
    oh_lo = place("o_hg_lo", [P, 8, T], X0, F32R)
    ga = place("gate_a", [P, 8, T], A0 + 16 * KB)
    gb = place("gate_b", [P, 8, T], A0 + 32 * KB)
    or_hi = place("o_ret_hi", [P, 16, T], W0, F32R)
    or_lo = [place("o_ret_lo0", [P, 8, T], X0, F32R), place("o_ret_lo1", [P, 8, T], A0, F32R)]
    expert_w = place("expert_w", [P, GROUP, T], A0)
    scores = place("scores", [P, TT, 16, NKEYS], A0 + 24 * KB)
    sub_keys = place("sub_keys", [P, 16, NKEYS], A0 + 56 * KB)
    hot1 = place("hot1", [P, HOTS, TOKENS_PER_BATCH, NKEYS], A0 + 56 * KB)
    peer_q = place("peer_q", [P, 16, T], A0 + 64 * KB)
    stage = place("gate_stage", [P, NKEYS, STAGED_TOKENS], A0 + 64 * KB)
    cand = place("cand", [P, PEER_HEADS, CANDS], SMALL + 2 * KB)
    place_f = place("place_f", [P, 4, CHOICES], SMALL + 6 * KB)
    low_f = place("low_f", [P, CHOICES], SMALL + 8 * KB)
    pick = place("pick", [P, CHOICES, TOPK], SMALL + 2 * KB)
    S1 = A0 + 96 * KB
    top_s = place("top_s", [P, 16, TOPK], S1)
    top_u = place("top_u", [P, 16, TOPK], S1 + KB, U32)
    top_f = place("top_f", [P, 16, TOPK], S1 + 2 * KB)
    best_s = place("best_s", [P, PEER_HEADS, TOPK], S1 + 3 * KB)
    best_u = place("best_u", [P, CHOICES], S1 + 3 * KB + 512, U32)
    place_u = place("place_u", [P, 4, CHOICES], S1, U32)
    row_f = place("row_f", [P, 2, CHOICES], S1 + 4 * KB)
    chosen = place("chosen", [P, 3, CHOICES], S1 + 5 * KB)
    denom = place("denom", [P, 2, PEER_HEADS], S1 + 6 * KB + 512)
    chosen_t = place("chosen_t", [P, 3, P], S1 + 6 * KB + 576)
    hot2 = place("hot2", [P, HOTS, TOKENS_PER_BATCH, NKEYS], S1 + 8 * KB + 64)
    g_in = place("gates_in", [P, 4, T], A0 + 64 * KB)
    ew_hi = place("ew_hi", [P, 2, T], A0 + 72 * KB, F32R)
    ew_lo = place("ew_lo", [P, 2, T], A0 + 76 * KB, F32R)
    in2 = place("in2", [P, 16, T], A0)
    val2 = place("val2", [P, TT, 512], A0 + 32 * KB)
    mix_hi = place("mix_hi", [P, 8, T], A0 + 40 * KB, F32R)
    mix_lo = place("mix_lo", [P, 8, T], A0 + 56 * KB, F32R)
    B0 = A0 + 72 * KB
    lru_w = place("lru_w", [P, 8, P], B0)
    lru = [place(f"lru{n}", [P, T], B0 + (4 + 2 * n) * KB) for n in range(6)]
    sbw = place("sb_w", [P, TT, T], A0)
    sbz = [place("sb_z0", [P, TT, T], A0 + 8 * KB), place("sb_z1", [P, TT, T], B0 + 8 * KB)]
    sbt = place("sb_t", [P, TT, T], B0 + 16 * KB)
    distance = place("distance", [P, T], B0 + 24 * KB)
    dfs = place("df_s", [P, 2, T], B0 + 26 * KB)
    dfe = [place("df_e0", [P, 2, T], B0 + 30 * KB), tmp]
    dfp = place("df_p", [P, T], B0 + 34 * KB)
    dfo = place("df_o", [P, 2, T], B0 + 36 * KB)
    dfpt = place("df_pt", [P, TT, T], B0)
    df_stat = place("df_stat", [P, 16], B0 + 40 * KB)
    ff_hi = place("ff_hi", [P, FF_TILES, T], A0, F32R)
    ff_lo = place("ff_lo", [P, FF_TILES, T], A0 + 44 * KB, F32R)
    conv = place("conv", [P, 2, T], A0 + 88 * KB)
    act_g = place("act_g", [P, 2, T], A0 + 92 * KB)
    final = place("final", [P, KT, T], A0)

    bank = [nc.alloc_psum_tensor(f"bank{n}", [P, T], F32) for n in range(8)]

    gates = nc.dram_tensor("gates", (T // STAGED_TOKENS, NKEYS, NKEYS, STAGED_TOKENS), F32, kind="Internal").ap()

    def sem(name):
        return nc.alloc_semaphore(name)

    raw_loaded = [sem(f"raw_loaded{n}") for n in range(RAW)]
    x_part = [sem(f"x_part{n}") for n in range(4)]
    gate_in = [sem(f"gate_in{n}") for n in range(4)]
    sp_passed, pool_passed, pe_passed, act_passed, dve_passed = (sem(n) for n in (
        "sp_passed", "pool_passed", "pe_passed", "act_passed", "dve_passed"))
    consts_in, x_in, masks_in, cs_in, keys_in, lru_in = (sem(n) for n in (
        "consts_in", "x_in", "masks_in", "cs_in", "keys_in", "lru_in"))
    distance_in, gates_out, out_done = (sem(n) for n in (
        "distance_in", "gates_out", "out_done"))
    hi_split, split_done, hot_gated = (sem(n) for n in (
        "hi_split", "split_done", "hot_gated"))
    choices_here, hot_distance, last_hot = (sem(n) for n in ("choices_here", "hot_distance", "last_hot"))
    tile_done, pair_used, sq_used, lev_done, far_done, o_done = (sem(n) for n in (
        "tile_done", "pair_used", "sq_used", "lev_done", "far_done", "o_done"))
    ret_s_done, ret_o_done, score_done, turned, batch_done, lru_gate_done = (sem(n) for n in (
        "ret_s_done", "ret_o_done", "score_done", "turned", "batch_done", "lru_gate_done"))
    sb_z_done, sb_tail_done, sb_o_done, df_s_done, df_pt_done, df_o_done = (sem(n) for n in (
        "sb_z_done", "sb_tail_done", "sb_o_done", "df_s_done", "df_pt_done", "df_o_done"))
    acc_read_act, acc_read_dve, tok_read = (sem(n) for n in (
        "acc_read_act", "acc_read_dve", "tok_read"))
    act_step, sq_done, root_done, bounds_exp, logf_done, head_ready = (sem(n) for n in (
        "act_step", "sq_done", "root_done", "bounds_exp", "logf_done", "head_ready"))
    far_q_exp, lev_exp, att_far, o_read, rvh_ready, ret_o_read = (sem(n) for n in (
        "far_q_exp", "lev_exp", "att_far", "o_read", "rvh_ready", "ret_o_read"))
    score_read, scores_copied, best_exp, gate_read, ew_hi_ready, lam_exp = (sem(n) for n in (
        "score_read", "scores_copied", "best_exp", "gate_read", "ew_hi_ready", "lam_exp"))
    lam_ready, lru_gate_read, lru_decays, lru_root, lru_gelu, sb_ln = (sem(n) for n in (
        "lam_ready", "lru_gate_read", "lru_decays", "lru_root", "lru_gelu", "sb_ln"))
    sb_exp, df_exp, df_pt_read, df_o_read = (sem(n) for n in (
        "sb_exp", "df_exp", "df_pt_read", "df_o_read"))
    dve_step, eps_set, ones_set, h_ready, bounds_shifted, f_done = (sem(n) for n in (
        "dve_step", "eps_set", "ones_set", "h_ready", "bounds_shifted", "f_done"))
    decay_done, far_e_ready, lev_diff, far_ready, lev_ready, lev_read = (sem(n) for n in (
        "decay_done", "far_e_ready", "lev_diff", "far_ready", "lev_ready", "lev_read"))
    halves_done, norm_scaled = sem("halves_done"), sem("norm_scaled")
    norm_hi = sem("norm_hi")
    rot_ready, ret_att, normed, gated, chosen_done, best_shifted = (sem(n) for n in (
        "rot_ready", "ret_att", "normed", "gated", "chosen_done", "best_shifted"))
    hot_ready, weighted, ew_ready, x_added, resid_ready, lam_abs = (sem(n) for n in (
        "hot_ready", "weighted", "ew_ready", "x_added", "resid_ready", "lam_abs"))
    softplus_done, conv_done, lru_var, mixed_ready, sb_z_read, sb_sp_ready = (sem(n) for n in (
        "softplus_done", "conv_done", "lru_var", "mixed_ready", "sb_z_read", "sb_sp_ready"))
    sb_tail_read, sb_w_ready, sb_o_read, df_s_read, df_max, df_p_ready = (sem(n) for n in (
        "sb_tail_read", "sb_w_ready", "sb_o_read", "df_s_read", "df_max", "df_p_ready"))
    ff_silu, ff_ready, down_read, final_done = (sem(n) for n in (
        "ff_silu", "ff_ready", "down_read", "final_done"))

    START, at = {}, 0
    for name, n in STREAM:
        START[name] = at
        at += n
    START["end"] = at

    ACT_READ, at = {}, 0
    for name, n in (("hf", 8), ("hq", 8), ("rqk", 16), ("gates", 16), ("hg", 8), ("rg", 16),
                    ("peer_q", 16), ("experts", NKEYS), ("in_2", 12), ("late_2", 4)):
        ACT_READ[name] = at
        at += n

    def one(t, i):
        return t[:, bass.ds(i, 1), :].rearrange("p a n -> p (a n)")

    def score_bank(tt, n):
        return bank[2 + n] if tt % 2 else bank[(6 + n) % 8]

    def f32(t):
        return t.bitcast(F32)

    block = nc.Block()
    block.__enter__()

    @block.sync
    def _(sp):
        c = Count(sp, sp_passed)
        for n in range(4):
            sp.dma_start(resid[:, 2 * n:2 * n + 2, :], x[:, 2 * n:2 * n + 2, :]).then_inc(x_part[n], 16)
        sp.dma_start(vec[:], vectors).then_inc(consts_in, 16)
        sp.dma_start(tab[:], tables[:, 0:TAB["cos"][0]]).then_inc(consts_in, 16)
        sp.dma_start(masks[:].rearrange("p l n -> p (l n)"), tables[:, TAB["levels"][0]:TAB["levels"][0] + len(LEVELS) * P]).then_inc(masks_in, 16)
        sp.dma_start(scan_keep[:], tables[:, TAB["scan_keep"][0]:TAB["scan_keep"][0] + T]).then_inc(masks_in, 16)

        def load(i, slot):
            sp.wait_ge(split_done, c.due(split_done, 1, back=RAW))
            sp.dma_start(w_raw[:, slot, :], weights[bass.ds(i, 1), :, :].rearrange("a p n -> (a p) n")).then_inc(raw_loaded[slot], 16)

        def load_run(first, n):
            def four(i):
                for s in range(RAW):
                    load(i * RAW + (first + s), s)
            c.repeat(n // RAW, four)

        load_run(0, START["experts"])
        load_run(START["experts"], GROUP)
        sp.wait_ge(gates_out, c.due(gates_out, 16 * (T // STAGED_TOKENS)))

        def load_gates(e, slot):
            sp.wait_ge(weighted, c.due(weighted, 1, back=4))
            sp.dma_start(g_in[:, slot, :].rearrange("p (b t) -> p b t", t=STAGED_TOKENS),
                         gates[:, :, bass.ds(e, 1), :].rearrange("b k a t -> k b (a t)")).then_inc(gate_in[slot], 16)

        def first_values(i):
            for s in range(RAW):
                load_gates(i * (2 * RAW) + s, s)
            for s in range(RAW // 2):
                load(START["experts"] + GROUP + i * RAW + s, s)
            for s in range(RAW):
                load_gates(i * (2 * RAW) + (RAW + s), s)
            for s in range(RAW // 2, RAW):
                load(START["experts"] + GROUP + i * RAW + s, s)
        c.repeat(GROUP // (2 * RAW), first_values)

        def more_values(i):
            for s in range(RAW):
                load(START["experts"] + GROUP + GROUP // 2 + i * RAW + s, s)
        c.repeat(GROUP // (2 * RAW), more_values)

        def group(g):
            first = START["experts"] + g * (2 * GROUP)

            def four(i):
                for s in range(RAW):
                    load(first + i * RAW + s, s)
                    load_gates(g * GROUP + i * RAW + s, s)
            c.repeat(GROUP // RAW, four)

            def four_values(i):
                for s in range(RAW):
                    load(first + GROUP + i * RAW + s, s)
            c.repeat(GROUP // RAW, four_values)
        c.once(group, 1)
        c.loop(2, NKEYS // GROUP, group)
        rest = N_STREAM - START["in_2"]
        load_run(START["in_2"], rest - rest % RAW)
        for s in range(rest % RAW):
            load(N_STREAM - rest % RAW + s, s)
        for k in range(0, KT, 2):
            sp.wait_ge(final_done, c.due(final_done, 2))
            sp.dma_start(out[:, k:k + 2, :], final[:, k:k + 2, :]).then_inc(out_done, 16)
        sp.wait_ge(out_done, 16 * KT // 2)

    @block.gpsimd
    def _(pool):
        c = Count(pool, pool_passed)

        one_col = ones[:, 0:1]
        pool.wait_ge(ones_set, c.due(ones_set))

        def split(slot):
            pair = slot % 2
            pool.wait_ge(raw_loaded[slot], c.due(raw_loaded[slot], 16))
            pool.wait_ge(tile_done, c.due(tile_done, 1, back=2))
            nc.gpsimd.tensor_tensor(w_hi[:, pair, :], w_raw[:, slot, :], one_col.to_broadcast((P, 1024)), ALU.mult).then_inc(hi_split, 1)
            pool.wait_ge(hi_split, c.due(hi_split))
            nc.gpsimd.tensor_tensor(w_lo[:, pair, :], w_raw[:, slot, :], f32(w_hi[:, pair, :]), ALU.subtract).then_inc(split_done, 1)
            pool.wait_ge(split_done, c.due(split_done))

        def four(i):
            for s in range(RAW):
                split(s)

        c.repeat(START["experts"] // RAW, four)

        def gate_lot(lot):
            def batches(i):
                for p in range(HOTS):
                    pool.wait_ge(hot_ready, c.due(hot_ready, 2 if p < HOTS - 1 else 1))
                    at = bass.ds((lot % LOTS) * STAGED_TOKENS + (i * HOTS + p) * TOKENS_PER_BATCH, TOKENS_PER_BATCH)
                    gate = chosen_t[:, 2, at]
                    nc.gpsimd.tensor_tensor(hot1[:, p], hot1[:, p], gate.unsqueeze(2).to_broadcast((P, TOKENS_PER_BATCH, NKEYS)),
                                            ALU.mult).then_inc(hot_gated, 1)
            c.repeat(LOT_BATCHES // HOTS, batches)
        tile = 0
        for lot in range(TT * LOTS):
            ahead = sum(FIRST_KEYS[:lot + 1]) + (2 if lot + 1 < TT * LOTS else 0)
            while tile < ahead:
                split((START["experts"] + tile) % RAW)
                tile += 1
            gate_lot(lot)
        while tile < GROUP:
            split((START["experts"] + tile) % RAW)
            tile += 1
        rest = N_STREAM - START["experts"] - GROUP
        assert (START["experts"] + tile) % RAW == 0
        c.repeat(rest // RAW, four)
        for s in range(rest % RAW):
            split(s)

    @block.tensor
    def _(pe):
        c = Count(pe, pe_passed)
        mm = nc.tensor.matmul

        def settle():
            pe.wait_ge(acc_read_act, c.due(acc_read_act, 0))
            pe.wait_ge(acc_read_dve, c.due(acc_read_dve, 0))
            pe.wait_ge(tok_read, c.due(tok_read, 0))

        def three(out_, hi, lo, rhs_hi, rhs_lo, first, last):
            mm(out_, hi, rhs_hi, start=first, stop=False)
            mm(out_, hi, rhs_lo, start=False, stop=False)
            return mm(out_, lo, rhs_hi, start=False, stop=last)

        def tile_fm(p, rhs_hi, rhs_lo, acc, first=True, last=True):
            pe.wait_ge(split_done, c.due(split_done))
            for k in range(KT):
                col = slice(k * P, (k + 1) * P)
                ins = three(acc, w_hi[:, p, col], w_lo[:, p, col], rhs_hi[:, k, :], rhs_lo[:, k, :],
                            first and k == 0, last and k == KT - 1)
            ins.then_inc(tile_done, 1)

        def tiles_fm(n, rhs_hi, rhs_lo, read):
            def two(i):
                for p in range(2):
                    pe.wait_ge(read, c.due(read, 1, back=2))
                    tile_fm(p, rhs_hi, rhs_lo, bank[p][:])
            c.repeat(n // 2, two)

        def dense_fm(n, rhs_hi, rhs_lo, read):
            settle()
            tiles_fm(n, rhs_hi, rhs_lo, read)

        def first_two(rhs_hi, rhs_lo, read, ready):
            settle()
            pe.wait_ge(read, c.due(read, 2, back=2))
            pe.wait_ge(split_done, c.due(split_done, 2))
            for k in range(KT):
                ready(k)
                col = slice(k * P, (k + 1) * P)
                for p in range(2):
                    ins = three(bank[p][:], w_hi[:, p, col], w_lo[:, p, col], rhs_hi[:, k, :], rhs_lo[:, k, :], k == 0, k == KT - 1)
                    if k == KT - 1:
                        ins.then_inc(tile_done, 1)

        def h_part(k):
            pe.wait_ge(h_ready, c.due(h_ready))

        def fresh_fm(n, read):
            first_two(h_hi, h_lo, read, h_part)
            tiles_fm(n - 2, h_hi, h_lo, read)

        def square_sum(k):
            pe.wait_ge(sq_done, c.due(sq_done))
            mm(bank[7][:], ones[:], sq[:, k % 2, :], start=k == 0, stop=k == KT - 1).then_inc(sq_used, 1)

        def residual_fm(rhs_hi, rhs_lo, ready):
            first_two(rhs_hi, rhs_lo, acc_read_dve, ready)
            for n in range(2, KT):
                pe.wait_ge(acc_read_dve, c.due(acc_read_dve, 1, back=2))
                tile_fm(n % 2, rhs_hi, rhs_lo, bank[n % 2][:])
                square_sum(n - 2)
            square_sum(KT - 2)
            square_sum(KT - 1)

        def group_tm(between=None):
            for j in range(4):
                if between and j == 2:
                    between()
                pe.wait_ge(split_done, c.due(split_done))
                for k2 in range(2):
                    k = 2 * j + k2
                    col = slice(k2 * 512, k2 * 512 + 512)
                    for tt in range(TT):
                        tok = slice(tt * P, tt * P + P)
                        o = bank[2 + tt][:]
                        if k == 0:
                            pe.wait_ge(tok_read, c.due(tok_read, 1, back=TT))
                        mm(o, h_hi[:, k, tok], w_hi[:, j % 2, col], start=k == 0, stop=False)
                        mm(o, h_hi[:, k, tok], w_lo[:, j % 2, col], start=False, stop=False)
                        ins = mm(o, h_lo[:, k, tok], w_hi[:, j % 2, col], start=False, stop=k == KT - 1)
                ins.then_inc(tile_done, 1)

        def dense_tm(groups):
            settle()
            c.repeat(groups, lambda g: group_tm())

        def norm():
            for k in range(KT):
                square_sum(k)

        pe.wait_ge(ones_set, c.due(ones_set))
        norm()
        fresh_fm(16, acc_read_act)
        dense_tm(2)
        settle()

        def tile_part(p, acc, part):
            if part == 0:
                pe.wait_ge(acc_read_act, c.due(acc_read_act, 1, back=2))
                pe.wait_ge(split_done, c.due(split_done))
            for k in (2 * part, 2 * part + 1):
                col = slice(k * P, (k + 1) * P)
                ins = three(acc, w_hi[:, p, col], w_lo[:, p, col], h_hi[:, k, :], h_lo[:, k, :], k == 0, k == KT - 1)
            if part == 3:
                ins.then_inc(tile_done, 1)

        def hgrn_head(i, p):
            def level(lhs, rhs, l):
                pe.wait_ge(lev_read, c.due(lev_read, 1, back=2))
                for j in range(TT):
                    tok = slice(j * P, j * P + P)
                    if l == 0:
                        ins = mm(bank[2][:, tok], lhs[:, tok], rhs[:, tok], start=j == 0, stop=j == TT - 1)
                    else:
                        w = LEVELS[l]
                        right = rhs[:, tok].rearrange("p (b n) -> p b n", n=2 * w)[:, :, w:2 * w]
                        ins = mm(bank[2 + l % 2][:, j * (P // 2):(j + 1) * (P // 2)], lhs[:, tok], right, start=j == 0, stop=j == TT - 1)
                ins.then_inc(lev_done, 1)

            pe.wait_ge(head_ready, c.due(head_ready, 2))
            level(head_k[p], one(hq_, i), 0)
            pe.wait_ge(far_ready, c.due(far_ready))
            pe.wait_ge(att_far, c.due(att_far, 3, back=3))
            mm(bank[4][:, 0:384], far_k[:, 0, :], far_q[:, 0:384], start=True, stop=True)
            mm(bank[5][:, 0:256], far_k[:, 1, :], far_q[:, 384:640], start=True, stop=False)
            mm(bank[5][:, 256:384], far_k[:, 2, :], far_q[:, 640:768], start=False, stop=True).then_inc(far_done, 1)
            tile_part(0, bank[0][:], 0)
            for l in range(1, len(LEVELS)):
                pe.wait_ge(lev_ready, c.due(lev_ready, 2))
                level(lev_z[:, l % 2, :], lev_z[:, l % 2, :], l)
                tile_part(l // 4, bank[l // 4][:], l % 4)
            pe.wait_ge(lev_read, c.due(lev_read, 0))
            pe.wait_ge(att_far, c.due(att_far, 0))
            pe.wait_ge(o_read, c.due(o_read, 1, back=1))
            for j in range(TT):
                ins = mm(bank[6][:, j * P:T], head_v[p][:, j, :], att[:, j * 640:j * 640 + T - j * P], start=j == 0, stop=j == TT - 1)
            ins.then_inc(o_done, 1)

        def hgrn_heads(i):
            for p in range(2):
                hgrn_head(i * 2 + p, p)
        c.repeat(HG_HEADS // 2, hgrn_heads)

        settle()

        def values(g):
            def sums():
                for p in range(2):
                    pe.wait_ge(sq_done, c.due(sq_done))
                    mm(bank[6 + p][:], ones[:], sq[:, p, :], start=True, stop=True).then_inc(sq_used, 1)
            group_tm(sums)
        c.repeat(RET_HEADS, values)
        settle()

        def ret_head(i):
            pe.wait_ge(rot_ready, c.due(rot_ready))
            pe.wait_ge(ret_o_read, c.due(ret_o_read, 0))
            for j in range(TT):
                for k in range(2):
                    ins = mm(bank[2 + j][:, 0:T - j * P], rot_k[:, k, j * P:j * P + P], rot_q[:, k, j * P:T],
                             start=k == 0, stop=k == 1)
                ins.then_inc(ret_s_done, 1)
            tiles_fm(2, h_hi, h_lo, acc_read_act)
            pe.wait_ge(ret_att, c.due(ret_att, TT))
            pe.wait_ge(rvh_ready, c.due(rvh_ready))
            for m in range(4):
                pe.wait_ge(ret_o_read, c.due(ret_o_read, 1, back=2))
                for j in range(TT):
                    ins = mm(bank[4 + m % 2][:, j * P:T], rvh[:, j, m * P:m * P + P], ratt[:, j * 512:j * 512 + T - j * P],
                             start=j == 0, stop=j == TT - 1)
                ins.then_inc(ret_o_done, 1)
            for m in range(4):
                if m == 2:
                    tiles_fm(2, h_hi, h_lo, acc_read_act)
                pe.wait_ge(sq_done, c.due(sq_done))
                mm(bank[6][:], ones[:], sq[:, m % 2, :], start=m == 0, stop=m == 3).then_inc(sq_used, 1)
        c.repeat(RET_HEADS, ret_head)
        pe.wait_ge(ret_o_read, c.due(ret_o_read, 0))

        dense_fm(8, h_hi, h_lo, acc_read_act)
        pe.wait_ge(gated, c.due(gated, 8))
        dense_fm(8, oh_hi, oh_lo, acc_read_dve)
        dense_fm(16, h_hi, h_lo, acc_read_act)
        pe.wait_ge(gated, c.due(gated, 16))
        settle()

        def two_deep(i):
            for n in range(2):
                pe.wait_ge(acc_read_dve, c.due(acc_read_dve, 1, back=2))
                tile_fm(0, or_hi[:, 0:8, :], or_lo[0], bank[n][:], last=False)
                tile_fm(1, or_hi[:, 8:16, :], or_lo[1], bank[n][:], first=False)
        c.repeat(4, two_deep)
        residual_fm(h_hi, h_lo, h_part)

        fresh_fm(16, acc_read_act)
        settle()
        pe.wait_ge(keys_in, c.due(keys_in, 16))
        for tt in range(TT):
            pe.wait_ge(score_read, c.due(score_read, 4, back=8))
            for n in range(16):
                ins = mm(score_bank(tt, n // 4)[:, n % 4 * P:n % 4 * P + P], peer_q[:, n, tt * P:tt * P + P], sub_keys[:, n, :],
                         start=n % 4 == 0, stop=n % 4 == 3)
            ins.then_inc(score_done, 1)
        pe.wait_ge(score_read, c.due(score_read, 0, back=4))

        def turn():
            pe.wait_ge(chosen_done, c.due(chosen_done))
            for n in range(3):
                ins = nc.tensor.transpose(bank[6][:, n * P:n * P + P], chosen[:, n, :], t_("identity"))
            ins.then_inc(turned, 1)

        def gate_lot():
            def batches(i):
                for p in range(HOTS):
                    pe.wait_ge(hot_gated, c.due(hot_gated))
                    if p == HOTS - 1:
                        pe.wait_ge(last_hot, c.due(last_hot))
                    pe.wait_ge(gate_read, c.due(gate_read, 1, back=HOTS))
                    for t in range(TOKENS_PER_BATCH):
                        ins = mm(bank[2 + p][:, t * P:t * P + P], hot2[:, p, t, :], hot1[:, p, t, :],
                                 start=t == 0, stop=t == TOKENS_PER_BATCH - 1)
                    ins.then_inc(batch_done, 1)
            c.repeat(LOT_BATCHES // HOTS, batches)
        for lot in range(TT * LOTS):
            if FIRST_KEYS[lot]:
                tiles_fm(FIRST_KEYS[lot], h_hi, h_lo, acc_read_act)
            if lot == 0:
                pe.wait_ge(score_read, c.due(score_read, 0))
            if lot % LOTS == 0:
                turn()
            gate_lot()
        tiles_fm(GROUP - sum(FIRST_KEYS), h_hi, h_lo, acc_read_act)
        pe.wait_ge(gate_read, c.due(gate_read, 0))

        def expert_values():
            for half in range(2):
                banks = bank[half * 4:half * 4 + 4]
                pe.wait_ge(x_added, c.due(x_added, 4, back=8))

                def values(i, first, last):
                    for p in range(2):
                        pe.wait_ge(split_done, c.due(split_done))
                        for e in range(2):
                            pe.wait_ge(ew_ready, c.due(ew_ready))
                            for m in (2, 3, 0, 1):
                                if half == 0 and first and p == 0 and e == 0 and m == 0:
                                    pe.wait_ge(acc_read_act, c.due(acc_read_act, 0))
                                col = slice(e * 512 + m * P, e * 512 + m * P + P)
                                ins = three(banks[m][:], w_hi[:, p, col], w_lo[:, p, col], ew_hi[:, e, :], ew_lo[:, e, :],
                                            first and p == 0 and e == 0, last and p == 1 and e == 1)
                            ins.then_inc(pair_used if e == 0 else tile_done, 1)
                n = GROUP // 4
                c.once(values, 0, True, False)
                c.loop(1, n - 1, lambda i: values(i, False, False))
                c.once(values, n - 1, False, True)
        expert_values()

        def group(g):
            pe.wait_ge(x_added, c.due(x_added, 0, back=4))
            tiles_fm(GROUP, h_hi, h_lo, acc_read_act)
            expert_values()
        c.once(group, 1)
        c.loop(2, NKEYS // GROUP, group)
        pe.wait_ge(x_added, c.due(x_added, 0))
        norm()

        norm()
        fresh_fm(8, acc_read_act)
        pe.wait_ge(lru_in, c.due(lru_in, 16))

        def lru_gate(n):
            pe.wait_ge(conv_done, c.due(conv_done))
            pe.wait_ge(lru_gate_read, c.due(lru_gate_read, 2, back=2))
            mm(bank[6][:], lru_w[:, n, :], lru[n % 2][:], start=True, stop=True)
            mm(bank[7][:], lru_w[:, 4 + n, :], lru[n % 2][:], start=True, stop=True).then_inc(lru_gate_done, 1)
        for n in range(2):
            lru_gate(n)
            tiles_fm(2, h_hi, h_lo, acc_read_act)
        lru_gate(2)
        settle()
        group_tm(lambda: lru_gate(3))
        settle()
        pe.wait_ge(lru_gate_read, c.due(lru_gate_read, 0))

        def head_row(h):
            return slice(64 * (h % 2), 64 * (h % 2) + 64)

        def sb_logits(h):
            pe.wait_ge(sb_tail_read, c.due(sb_tail_read, 0))
            row = head_row(h)
            for j in range(TT):
                pe.wait_ge(sb_z_read, c.due(sb_z_read, 1, back=2))
                mm(bank[j % 2][:, 0:T - j * P], in2[row, 10 + h // 2, j * P:j * P + P], in2[row, 8 + h // 2, j * P:T],
                   start=True, stop=True).then_inc(sb_z_done, 1)

        def sb_tails(h):
            pe.wait_ge(sb_sp_ready, c.due(sb_sp_ready, TT))
            for j in range(TT):
                pe.wait_ge(sb_tail_read, c.due(sb_tail_read, 1, back=2))
                acc = bank[j % 2]
                for j2 in range(j, TT):
                    ins = mm(acc[:, (j2 - j) * P:T - j * P], t_("later") if j2 == j else ones[:], sbw[:, j2, 0:T - j2 * P],
                             start=j2 == j, stop=j2 == TT - 1)
                ins.then_inc(sb_tail_done, 1)

        def sb_out(h):
            pe.wait_ge(sb_w_ready, c.due(sb_w_ready, TT))
            if h % 2 == 0:
                pe.wait_ge(sb_o_read, c.due(sb_o_read, 1, back=1))
            for j in range(TT):
                ins = mm(bank[6][head_row(h), j * P:T], val2[:, j, h * 64:h * 64 + 64], sbw[:, j, 0:T - j * P],
                         start=j == 0, stop=j == TT - 1)
            ins.then_inc(sb_o_done, 1)

        def df_logits(h, i):
            for q in range(2):
                r0 = 64 * (h % 2) + 32 * q
                pe.wait_ge(df_s_read, c.due(df_s_read, 1, back=2))
                mm(bank[2 + q][:, 0:(i + 1) * P], in2[r0:r0 + 32, 12 + h // 2, i * P:i * P + P],
                   in2[r0:r0 + 32, 14 + h // 2, 0:(i + 1) * P], start=True, stop=True).then_inc(df_s_done, 1)

        def df_turn(h, i):
            pe.wait_ge(df_p_ready, c.due(df_p_ready))
            pe.wait_ge(df_pt_read, c.due(df_pt_read, 1, back=1))
            for j in range(i + 1):
                ins = nc.tensor.transpose(bank[4][:, j * P:j * P + P], dfp[:, j * P:j * P + P], t_("identity"))
            ins.then_inc(df_pt_done, 1)

        def df_out(h):
            pe.wait_ge(df_pt_read, c.due(df_pt_read, 0))
            if h % 2 == 0:
                pe.wait_ge(df_o_read, c.due(df_o_read, 1, back=1))
            for j in range(TT):
                ins = mm(bank[7][head_row(h), j * P:T], val2[:, j, 256 + h * 64:256 + h * 64 + 64], dfpt[:, j, j * P:T],
                         start=j == 0, stop=j == TT - 1)
            ins.then_inc(df_o_done, 1)

        def df_squares(pair):
            pe.wait_ge(sq_done, c.due(sq_done))
            mm(bank[5][:], t_("halves"), sq[:, pair, :], start=True, stop=True).then_inc(sq_used, 1)
        def late_tile(p, at):
            pe.wait_ge(acc_read_act, c.due(acc_read_act, 1, back=2))
            tile_fm(p, h_hi, h_lo, bank[at][:])
        sb_logits(0)
        late_tile(0, 5)
        late_tile(1, 7)
        for h in range(SB_HEADS):
            if h == 2:
                pe.wait_ge(acc_read_act, c.due(acc_read_act, 0))
            df_logits(h, 0)
            sb_tails(h)
            if h == 2:
                df_squares(0)
            df_logits(h, 1)
            df_turn(h, 0)
            df_logits(h, 2)
            sb_out(h)
            if h < 2:
                late_tile(h, 5)
            df_turn(h, 1)
            df_logits(h, 3)
            if h + 1 < SB_HEADS:
                pe.wait_ge(acc_read_act, c.due(acc_read_act, 0))
                sb_logits(h + 1)
            df_turn(h, 2)
            df_turn(h, 3)
            df_out(h)
        df_squares(1)
        def mixed_part(k):
            if k in (4, 5):
                pe.wait_ge(sb_o_read, c.due(sb_o_read, 0) - 1 + (k - 4))
            else:
                pe.wait_ge(mixed_ready, c.due(mixed_ready))
        residual_fm(mix_hi, mix_lo, mixed_part)
        fresh_fm(2 * FF_TILES, acc_read_dve)
        settle()
        pe.wait_ge(ff_ready, c.due(ff_ready, FF_TILES))

        def down(i, first, last):
            for p in range(2):
                pe.wait_ge(split_done, c.due(split_done))
                for n in range(KT):
                    col = slice(n * P, n * P + P)
                    ins = three(bank[n][:], w_hi[:, p, col], w_lo[:, p, col], one(ff_hi, i * 2 + p), one(ff_lo, i * 2 + p),
                                first and p == 0, last and p == 1)
                ins.then_inc(tile_done, 1)
        n = FF_TILES // 2
        c.once(down, 0, True, False)
        c.loop(1, n - 1, lambda i: down(i, False, False))
        c.once(down, n - 1, False, True)
        pe.wait_ge(down_read, c.due(down_read, KT))
        norm()

    @block.scalar
    def _(act):
        c = Count(act, act_passed)
        fn = nc.scalar.activation

        def fn_at(*args, **kw):
            c.alone()
            return fn(*args, **kw)

        def evac(n, where, func=ACT.Copy, scale=1.0, first=0):
            def two(i):
                for p in range(2):
                    act.wait_ge(tile_done, c.due(tile_done))
                    fn_at(one(where, i * 2 + (first + p)), bank[p][:], func, scale=scale).then_inc(acc_read_act, 1)
            c.repeat(n // 2, two)

        def evac_tm(groups, where):
            def group(g):
                act.wait_ge(tile_done, c.due(tile_done, 4))
                for tt in range(TT):
                    fn_at(where[:, tt, bass.ds(g * 512, 512)], bank[2 + tt][:], ACT.Copy).then_inc(tok_read, 1)
                    act.wait_ge(tok_read, c.due(tok_read))
            c.repeat(groups, group)

        def norm(each):
            fn(tiny[:, 63:64], eps[:], ACT.Sqrt).then_inc(act_step, 1)
            for k in range(KT):
                if each:
                    act.wait_ge(each, c.due(each))
                elif k % 2 == 0:
                    act.wait_ge(x_part[k // 2], 16)
                act.wait_ge(sq_used, c.due(sq_used, 1, back=2))
                fn(sq[:, k % 2, :], resid[:, k, :], ACT.Square).then_inc(sq_done, 1)
            act.wait_ge(sq_used, c.due(sq_used, 0))
            act.wait_ge(act_step, c.due(act_step))
            fn(rstd[:], bank[7][:], ACT.Sqrt, scale=1.0 / D, bias=eps[:]).then_inc(root_done, 1)

        def norm_parts():
            for k in range(KT):
                act.wait_ge(norm_scaled, c.due(norm_scaled))
                fn(h_hi[:, k, :], normed_x[:, k % 4, :], ACT.Copy).then_inc(norm_hi, 1)

        act.wait_ge(eps_set, c.due(eps_set))
        norm(None)
        norm_parts()
        act.wait_ge(bounds_shifted, c.due(bounds_shifted))
        fn(tiny[:, 0:16], tiny[:, 0:16], ACT.Exp).then_inc(bounds_exp, 1)
        act.wait_ge(bounds_exp, c.due(bounds_exp))
        evac(8, hk, ACT.Sigmoid)
        evac(2, hq_, ACT.Copy, HG_DK ** -0.5)
        act.wait_ge(f_done, c.due(f_done))
        fn(hb[:], hb[:], ACT.Ln).then_inc(logf_done, 1)
        evac(6, hq_, ACT.Copy, HG_DK ** -0.5, first=2)

        def head_copies(i, p):
            fn_at(head_k[p][:], one(hk, i), ACT.Copy).then_inc(head_ready, 1)
            fn_at(head_v[p][:], hv[:, :, bass.ds(i * 128, 128)], ACT.Copy).then_inc(head_ready, 1)

        def far_decays(i):
            act.wait_ge(far_e_ready, c.due(far_e_ready, 2))
            fn(far_e[:], far_e[:], ACT.Exp).then_inc(far_q_exp, 1)
            b = one(hb, i)
            tile = [b[:, j * P:j * P + P] for j in range(TT)]
            total = [b[:, j * P + P - 1:j * P + P] for j in range(TT)]
            for n, (j, bias) in enumerate(((1, None), (2, total[1]), (3, skip[:]), (2, None), (3, total[2]), (3, None))):
                extra = {} if bias is None else {"bias": bias}
                fn_at(far_q[:, n * P:n * P + P], tile[j], ACT.Exp, **extra).then_inc(far_q_exp, 1)

        def hgrn_head(i, p, last=False):
            for l in range(1, len(LEVELS)):
                act.wait_ge(lev_diff, c.due(lev_diff, 2))
                fn(lev_e[:, l % 2, :], lev_e[:, l % 2, :], ACT.Exp).then_inc(lev_exp, 1)
                if l == 2:
                    act.wait_ge(far_done, c.due(far_done))
                    fn(att[:, 128:512], bank[4][:, 0:384], ACT.Copy).then_inc(att_far, 1)
                    fn(att[:, 768:1024], bank[5][:, 0:256], ACT.Copy).then_inc(att_far, 1)
                    fn(att[:, 1408:1536], bank[5][:, 256:384], ACT.Copy).then_inc(att_far, 1)
                if l == 4 and not last:
                    head_copies(i + 1, 1 - p)
                if l == 6:
                    act.wait_ge(tile_done, c.due(tile_done))
                    fn_at(one(rq, i), bank[0][:], ACT.Copy).then_inc(acc_read_act, 1)
            if not last:
                far_decays(i + 1)
            act.wait_ge(tile_done, c.due(tile_done))
            fn_at(one(rk, i), bank[1][:], ACT.Copy, scale=RET_DK ** -0.5).then_inc(acc_read_act, 1)
            act.wait_ge(o_done, c.due(o_done))
            fn_at(one(hq_, i), bank[6][:], ACT.Copy).then_inc(o_read, 1)

        def hgrn_heads(i, last=False):
            hgrn_head(i * 2, 0)
            hgrn_head(i * 2 + 1, 1, last)
        fn(head_k[0][:], hk[:, 0, :], ACT.Copy).then_inc(head_ready, 1)
        act.wait_ge(decay_done, c.due(decay_done, HG_HEADS))
        far_decays(0)
        evac_tm(2, hv)
        act.wait_ge(tok_read, 2 * TT)
        fn(head_v[0][:], hv[:, :, 0:128], ACT.Copy).then_inc(head_ready, 1)
        c.once(hgrn_heads, 0)
        c.loop(1, HG_HEADS // 2 - 1, hgrn_heads)
        c.once(hgrn_heads, HG_HEADS // 2 - 1, True)
        act.dma_start(cos_sin[:], tables[:, TAB["cos"][0]:TAB["cos"][0] + 1024].rearrange("p (a n) -> p a n", a=2)).then_inc(cs_in, 16)
        act.dma_start(decay[:], tables[:, TAB["decay"][0]:TAB["decay"][0] + RET_HEADS * T].rearrange("p (a n) -> p a n", a=RET_HEADS)).then_inc(cs_in, 16)

        def values(g):
            for p in range(2):
                fn_at(sq[:, p, :], one(hq_, g * 2 + p), ACT.Square).then_inc(sq_done, 1)
            for p in range(2):
                act.wait_ge(sq_used, c.due(sq_used))
                act.wait_ge(normed, c.due(normed, 1, back=2))
                fn(tmp[:, p, :], bank[6 + p][:], ACT.Sqrt, scale=1.0 / 128, bias=eps[:]).then_inc(root_done, 1)
            act.wait_ge(tile_done, c.due(tile_done, 4))
            for tt in range(TT):
                fn_at(rv[:, tt, bass.ds(g * 512, 512)], bank[2 + tt][:], ACT.Copy).then_inc(tok_read, 1)
        c.repeat(RET_HEADS, values)

        def gate_tiles(i, where):
            for p in range(2):
                act.wait_ge(tile_done, c.due(tile_done))
                fn_at(one(where, i * 2 + p), bank[p][:], ACT.Sigmoid).then_inc(acc_read_act, 1)

        def ret_head(i):
            act.wait_ge(tok_read, RET_HEADS * TT + 2 * TT)
            act.wait_ge(ret_o_read, c.due(ret_o_read, 0))
            fn_at(rvh[:], rv[:, :, bass.ds(i * RET_DV, RET_DV)], ACT.Copy).then_inc(rvh_ready, 1)
            act.wait_ge(rot_ready, c.due(rot_ready))
            gate_tiles(i, ga)
            act.wait_ge(rvh_ready, c.due(rvh_ready))
            act.wait_ge(normed, c.due(normed, 1, back=1))
            for m in range(4):
                if m < 2:
                    act.wait_ge(ret_o_done, c.due(ret_o_done))
                    fn_at(rv[:, m, bass.ds(i * RET_DV, T)], bank[4 + m % 2][:], ACT.Copy).then_inc(ret_o_read, 1)
                    act.wait_ge(ret_o_read, c.due(ret_o_read))
                    fn_at(sq[:, m % 2, :], rv[:, m, bass.ds(i * RET_DV, T)], ACT.Square).then_inc(sq_done, 1)
                else:
                    act.wait_ge(ret_o_done, c.due(ret_o_done))
                    fn_at(rv[:, m, bass.ds(i * RET_DV, T)], bank[4 + m % 2][:], ACT.Copy).then_inc(ret_o_read, 1)
                    act.wait_ge(ret_o_read, c.due(ret_o_read))
            for m in range(2, 4):
                act.wait_ge(sq_used, c.due(sq_used))
                fn_at(sq[:, m % 2, :], rv[:, m, bass.ds(i * RET_DV, T)], ACT.Square).then_inc(sq_done, 1)
            gate_tiles(i, gb)
            act.wait_ge(sq_used, c.due(sq_used, 2))
            fn(tmp[:, 0, :], bank[6][:], ACT.Sqrt, scale=1.0 / RET_DV, bias=eps[:]).then_inc(root_done, 1)
        c.repeat(RET_HEADS, ret_head)

        def silu(n):
            def two(i):
                for p in range(2):
                    act.wait_ge(tile_done, c.due(tile_done))
                    act.wait_ge(gated, c.due(gated, 1, back=2))
                    fn(sq[:, p, :], bank[p][:], ACT.Silu).then_inc(acc_read_act, 1)
            c.repeat(n // 2, two)
        silu(8)
        act.wait_ge(tile_done, c.due(tile_done, 8))
        silu(16)
        act.wait_ge(gated, c.due(gated, 0))
        act.dma_start(sub_keys[:], keys).then_inc(keys_in, 16)
        act.wait_ge(tile_done, c.due(tile_done, 16))
        act.dma_start(resid[:], x).then_inc(x_in, 16)
        act.wait_ge(acc_read_dve, c.due(acc_read_dve, 16))
        norm(acc_read_dve)
        act.wait_ge(tile_done, c.due(tile_done, 8))
        norm_parts()
        evac(16, peer_q)
        for tt in range(TT):
            act.wait_ge(score_done, c.due(score_done))
            for n in range(4):
                fn(scores[:, tt, n * 4:n * 4 + 4, :].rearrange("p a n -> p (a n)"), score_bank(tt, n)[:], ACT.Copy).then_inc(score_read, 1)

        def shares():
            act.wait_ge(best_shifted, c.due(best_shifted))
            fn(best_s[:], best_s[:], ACT.Exp).then_inc(best_exp, 1)

        def staged(lot):
            act.wait_ge(gates_out, c.due(gates_out, 16, back=16))
            if lot % LOTS == 0:
                act.wait_ge(choices_here, c.due(choices_here))

            def batches(i):
                p = HOTS - 1
                first = (lot % LOTS) * STAGED_TOKENS + (i * HOTS + p) * TOKENS_PER_BATCH
                for t in range(TOKENS_PER_BATCH):
                    fn_at(hot2[:, p, t, :], t_("iota128"), ACT.Abs, scale=-1.0,
                          bias=chosen_t[:, 1, bass.ds(first + t, 1)]).then_inc(hot_distance, 1)
                act.wait_ge(hot_distance, c.due(hot_distance, TOKENS_PER_BATCH))
                c.alone()
                fn_at(hot2[:, p], hot2[:, p], ACT.Relu, scale=-1.0, bias=ones[:, 0:1]).then_inc(last_hot, 1)
                for p in range(HOTS):
                    act.wait_ge(batch_done, c.due(batch_done))
                    t0 = (i * HOTS + p) * TOKENS_PER_BATCH
                    fn_at(stage[:, :, bass.ds(t0, TOKENS_PER_BATCH)].rearrange("p k t -> p t k"),
                          bank[2 + p][:].rearrange("p (t k) -> p t k", k=NKEYS), ACT.Copy).then_inc(gate_read, 1)
            c.repeat(LOT_BATCHES // HOTS, batches)
            act.wait_ge(gate_read, c.due(gate_read, LOT_BATCHES))
            act.dma_start(gates[lot:lot + 1, :, :, :].rearrange("b k a t -> k (b a t)"),
                          stage[:].rearrange("p a t -> p (a t)")).then_inc(gates_out, 16)
        tile = 0
        for lot in range(TT * LOTS):
            n = FIRST_KEYS[lot]
            if lot % LOTS == 0:
                act.wait_ge(halves_done, c.due(halves_done, 2))
                early = n // 4 * 2
                if early:
                    evac(early, expert_w, ACT.Gelu_apprx_tanh, first=tile)
                shares()
                evac(n - early, expert_w, ACT.Gelu_apprx_tanh, first=tile + early)
            elif n:
                evac(n, expert_w, ACT.Gelu_apprx_tanh, first=tile)
            tile += n
            staged(lot)
        evac(GROUP - tile, expert_w, ACT.Gelu_apprx_tanh, first=tile)
        act.wait_ge(gates_out, c.due(gates_out, 0))

        def expert_values():
            for half in range(2):
                def values(i):
                    if half == 0:
                        act.wait_ge(weighted, c.due(weighted, 4))
                    for p in range(2):
                        for e in range(2):
                            if e == 0:
                                act.wait_ge(pair_used, c.due(pair_used, 1, back=1))
                            else:
                                act.wait_ge(tile_done, c.due(tile_done, 1, back=1))
                            fn_at(ew_hi[:, e, :], one(expert_w, i * 4 + p * 2 + e), ACT.Copy).then_inc(ew_hi_ready, 1)
                c.repeat(GROUP // 4, values)
            act.wait_ge(ew_ready, c.due(ew_ready, 2 * GROUP))
        expert_values()

        def group(g):
            evac(GROUP, expert_w, ACT.Gelu_apprx_tanh)
            expert_values()
        c.once(group, 1)
        c.loop(2, NKEYS // GROUP, group)
        act.wait_ge(tile_done, c.due(tile_done, 0))
        act.dma_start(lru_w[:], lru_gates).then_inc(lru_in, 16)
        act.dma_start(distance[:], tables[:, TAB["distance"][0]:TAB["distance"][0] + T]).then_inc(distance_in, 16)
        act.wait_ge(x_added, c.due(x_added, KT * (NKEYS // GROUP - 1)))
        norm(x_added)

        norm(resid_ready)
        norm_parts()
        act.wait_ge(lam_abs, c.due(lam_abs))
        fn(tiny[:, 0:4], tiny[:, 4:8], ACT.Exp).then_inc(lam_exp, 1)
        act.wait_ge(lam_exp, c.due(lam_exp))
        act.wait_ge(softplus_done, c.due(softplus_done))
        fn(tiny[:, 58:60], tiny[:, 56:58], ACT.Exp).then_inc(lam_ready, 1)
        act.wait_ge(lam_ready, c.due(lam_ready))
        evac(8, in2)
        act.wait_ge(acc_read_act, ACT_READ["in_2"] + 8)
        for n in range(LRU_TILES):
            fn(in2[:, 4 + n, :], in2[:, 4 + n, :], ACT.Gelu_apprx_tanh).then_inc(lru_gelu, 1)
        for n in range(LRU_TILES):
            act.wait_ge(mixed_ready, c.due(mixed_ready, 1, back=1))
            act.wait_ge(lru_gate_done, c.due(lru_gate_done))
            fn(lru[2][:], bank[6][:], ACT.Sigmoid, bias=v("b_r", n)).then_inc(lru_gate_read, 1)
            fn(lru[3][:], bank[7][:], ACT.Sigmoid, bias=v("b_i", n)).then_inc(lru_gate_read, 1)
            act.wait_ge(lru_gate_read, c.due(lru_gate_read, 2))
            fn(lru[4][:], lru[2][:], ACT.Exp, scale=tiny[:, 52 + n:53 + n]).then_inc(lru_decays, 1)
            fn(lru[5][:], lru[2][:], ACT.Tanh, scale=tiny[:, 48 + n:49 + n]).then_inc(lru_decays, 1)
            if n < 2:
                for p in range(2):
                    act.wait_ge(tile_done, c.due(tile_done))
                    fn(in2[:, 8 + 4 * n + 2 * p, :], bank[p][:], ACT.Copy).then_inc(acc_read_act, 1)
            act.wait_ge(lru_var, c.due(lru_var))
            fn(lru[5][:], lru[5][:], ACT.Sqrt).then_inc(lru_root, 1)
        evac_tm(1, val2)

        def sb_softplus(h):
            act.wait_ge(sb_z_read, c.due(sb_z_read, TT))
            for j in range(TT):
                N = T - j * P
                fn(sbt[:, j, 0:N], sbz[h % 2][:, j, 0:N], ACT.Abs).then_inc(act_step, 1)
            act.wait_ge(act_step, c.due(act_step, TT))
            for j in range(TT):
                N = T - j * P
                fn(sbt[:, j, 0:N], sbt[:, j, 0:N], ACT.Exp, scale=-1.0).then_inc(act_step, 1)

        def sb_logarithms():
            act.wait_ge(act_step, c.due(act_step, TT))
            for j in range(TT):
                N = T - j * P
                fn(sbt[:, j, 0:N], sbt[:, j, 0:N], ACT.Ln, bias=1.0).then_inc(sb_ln, 1)

        def sb_weights(h):
            for j in range(TT):
                N = T - j * P
                act.wait_ge(sb_tail_read, c.due(sb_tail_read))
                fn(sbw[:, j, 0:N], sbz[h % 2][:, j, 0:N], ACT.Exp).then_inc(sb_exp, 1)

        def df_exps(i):
            N = (i + 1) * P
            for q in range(2):
                act.wait_ge(df_max, c.due(df_max))
                total = 4 + 2 * (i % 2) + q
                fn(dfe[i % 2][:, q, 0:N], dfs[:, q, 0:N], ACT.Exp, scale=DF_DQK ** -0.5, bias=df_stat[:, 2 + q:3 + q],
                   accum_out=df_stat[:, total:total + 1]).then_inc(df_exp, 1)

        def df_turned(i):
            N = (i + 1) * P
            act.wait_ge(df_pt_done, c.due(df_pt_done))
            if i == 0:
                act.wait_ge(df_o_done, c.due(df_o_done, 1, back=1))
            fn(dfpt[:, 0:i + 1, i * P:i * P + P], bank[4][:, 0:N].rearrange("p (j n) -> p j n", n=P), ACT.Copy).then_inc(df_pt_read, 1)

        def df_squares(pair):
            act.wait_ge(df_o_done, 2 * pair + 2)
            fn(dfo[:, pair, :], bank[7][:], ACT.Copy).then_inc(df_o_read, 1)
            act.wait_ge(df_o_read, c.due(df_o_read))
            fn(sq[:, pair, :], dfo[:, pair, :], ACT.Square).then_inc(sq_done, 1)

        def late_tile(n):
            act.wait_ge(tile_done, c.due(tile_done))
            fn(in2[:, 9 + 2 * n, :], bank[7 if n == 1 else 5][:], ACT.Copy).then_inc(acc_read_act, 1)

        def df_root():
            act.wait_ge(sq_used, c.due(sq_used))
            fn(rstd[:], bank[5][:], ACT.Sqrt, scale=1.0 / DF_DV, bias=eps[:]).then_inc(root_done, 1)
        sb_softplus(0)
        sb_logarithms()
        late_tile(0)
        late_tile(1)
        for h in range(SB_HEADS):
            if h == 2:
                df_squares(0)
            df_exps(0)
            sb_weights(h)
            if h == 2:
                df_root()
            df_exps(1)
            df_turned(0)
            if h < 2:
                late_tile(2 + h)
            df_exps(2)
            df_turned(1)
            df_exps(3)
            if h + 1 < SB_HEADS:
                sb_softplus(h + 1)
            df_turned(2)
            df_turned(3)
            if h + 1 < SB_HEADS:
                sb_logarithms()
        df_squares(1)
        df_root()
        norm(acc_read_dve)
        norm_parts()

        def ff(i):
            act.wait_ge(acc_read_dve, c.due(acc_read_dve, 2))
            act.wait_ge(ff_ready, c.due(ff_ready, 1, back=1))
            fn(act_g[:, 0, :], conv[:, 0, :], ACT.Silu).then_inc(ff_silu, 1)
            act.wait_ge(ff_silu, c.due(ff_silu))
        c.repeat(FF_TILES, ff)
        norm(down_read)

    @block.vector
    def _(dve):
        c = Count(dve, dve_passed)
        ve = nc.vector
        tt_ = ve.tensor_tensor
        ts = ve.tensor_scalar
        stt = ve.scalar_tensor_tensor

        def pair(hi, lo, value, done):
            ve.tensor_copy(hi, value).then_inc(dve_step, 1)
            dve.wait_ge(dve_step, c.due(dve_step))
            tt_(lo, value, f32(hi), ALU.subtract).then_inc(done, 1)
            dve.wait_ge(done, c.due(done))

        def inverse_root():
            dve.wait_ge(root_done, c.due(root_done))
            ve.reciprocal(rstd[:], rstd[:]).then_inc(dve_step, 1)
            dve.wait_ge(dve_step, c.due(dve_step))

        def normed_pair(gain):
            inverse_root()

            def scale(k):
                stt(normed_x[:, k % 4, :], resid[:, k, :], v(gain, k), rstd[:], ALU.mult, ALU.mult).then_inc(norm_scaled, 1)
            for k in range(3):
                scale(k)
            for k in range(KT):
                dve.wait_ge(norm_hi, c.due(norm_hi))
                tt_(h_lo[:, k, :], normed_x[:, k % 4, :], f32(h_hi[:, k, :]), ALU.subtract).then_inc(h_ready, 1)
                if k + 3 < KT:
                    if k:
                        dve.wait_ge(h_ready, c.due(h_ready))
                    scale(k + 3)
            dve.wait_ge(h_ready, c.due(h_ready, 4))

        ve.memset(eps[:], EPS).then_inc(eps_set, 1)
        dve.wait_ge(eps_set, c.due(eps_set))
        ve.memset(ones[:], 1.0).then_inc(ones_set, 1)
        dve.wait_ge(ones_set, c.due(ones_set))
        dve.wait_ge(consts_in, c.due(consts_in, 32))
        b0, b1 = v("bounds", 0, 8), v("bounds", 8, 8)
        tt_(tiny[:, 16:24], b0, b1, ALU.max).then_inc(dve_step, 1)
        dve.wait_ge(dve_step, c.due(dve_step))
        tt_(tiny[:, 0:8], b0, tiny[:, 16:24], ALU.subtract).then_inc(dve_step, 1)
        dve.wait_ge(dve_step, c.due(dve_step))
        tt_(tiny[:, 8:16], b1, tiny[:, 16:24], ALU.subtract).then_inc(bounds_shifted, 1)
        dve.wait_ge(bounds_shifted, c.due(bounds_shifted))
        for n in range(4):
            dve.wait_ge(x_part[n], 16)
        normed_pair("norm_mix")
        dve.wait_ge(bounds_exp, c.due(bounds_exp))
        tt_(tiny[:, 16:24], tiny[:, 0:8], tiny[:, 8:16], ALU.add).then_inc(dve_step, 1)
        dve.wait_ge(dve_step, c.due(dve_step))
        ve.reciprocal(tiny[:, 16:24], tiny[:, 16:24]).then_inc(dve_step, 1)
        dve.wait_ge(dve_step, c.due(dve_step))
        tt_(tiny[:, 24:32], tiny[:, 0:8], tiny[:, 16:24], ALU.mult).then_inc(dve_step, 1)
        dve.wait_ge(dve_step, c.due(dve_step))
        ts(tiny[:, 32:40], tiny[:, 24:32], -1.0, 1.0, ALU.mult, ALU.add).then_inc(dve_step, 1)
        dve.wait_ge(dve_step, c.due(dve_step))
        dve.wait_ge(acc_read_act, c.due(acc_read_act, 8))
        for h in range(HG_HEADS):
            ts(hb[:, h, :], hk[:, h, :], tiny[:, 32 + h:33 + h], tiny[:, 24 + h:25 + h], ALU.mult, ALU.add).then_inc(dve_step, 1)
            dve.wait_ge(dve_step, c.due(dve_step))
        ts(hk[:], hb[:], -1.0, 1.0, ALU.mult, ALU.add).then_inc(f_done, 1)
        dve.wait_ge(f_done, c.due(f_done))
        dve.wait_ge(logf_done, c.due(logf_done))
        dve.wait_ge(masks_in, c.due(masks_in, 32))

        def scan(h):
            ve.tensor_tensor_scan(one(hb, h), scan_keep[:], one(hb, h), 0.0, ALU.mult, ALU.add).then_inc(decay_done, 1)
            dve.wait_ge(decay_done, c.due(decay_done))
        c.repeat(HG_HEADS, scan)
        ve.memset(att[:], 0.0).then_inc(dve_step, 1)
        dve.wait_ge(dve_step, c.due(dve_step))

        def halves(t, w):
            both = t.rearrange("p (b n) -> p b n", n=2 * w)
            return both[:, :, 0:w], both[:, :, w:2 * w]

        def diff(i, l):
            w = LEVELS[l]
            left, right = halves(one(hb, i), w)
            e_left, e_right = halves(lev_e[:, l % 2, :], w)
            last = left[:, :, w - 1:w].to_broadcast((P, T // (2 * w), w))
            tt_(e_right, right, last, ALU.subtract).then_inc(lev_diff, 1)
            tt_(e_left, last, left, ALU.subtract).then_inc(lev_diff, 1)

        def scaled(i, l, p):
            w = LEVELS[l]
            dve.wait_ge(lev_exp, c.due(lev_exp))
            e_left, e_right = halves(lev_e[:, l % 2, :], w)
            z_left, z_right = halves(lev_z[:, l % 2, :], w)
            tt_(z_right, halves(one(hq_, i), w)[1], e_right, ALU.mult).then_inc(lev_ready, 1)
            tt_(z_left, halves(head_k[p][:], w)[0], e_left, ALU.mult).then_inc(lev_ready, 1)

        def select(l):
            dve.wait_ge(lev_done, c.due(lev_done))
            c.alone()
            tiles = att[:].rearrange("p (j n) -> p j n", n=640)[:, :, 0:P]
            if l == 0:
                ve.copy_predicated(tiles, masks[:, 0, :].bitcast(U32).unsqueeze(1).to_broadcast((P, TT, P)),
                                   bank[2][:].rearrange("p (j n) -> p j n", n=P)).then_inc(lev_read, 1)
            else:
                w = LEVELS[l]
                mask = masks[:, l, :].rearrange("p (b n) -> p b n", n=2 * w)[:, :, w:2 * w].bitcast(U32)
                ve.copy_predicated(tiles.rearrange("p j (b n) -> p j b n", n=2 * w)[:, :, :, w:2 * w],
                                   mask.unsqueeze(1).to_broadcast((P, TT, P // (2 * w), w)),
                                   bank[2 + l % 2][:, 0:T // 2].rearrange("p (j b n) -> p j b n", j=TT, n=w)).then_inc(lev_read, 1)
            dve.wait_ge(lev_read, c.due(lev_read))

        def far_start(i):
            tiles = one(hb, i).rearrange("p (j n) -> p j n", n=P)
            tt_(far_e[:], tiles[:, 0:3, P - 1:P].to_broadcast((P, 3, P)), tiles[:, 0:3, :], ALU.subtract).then_inc(far_e_ready, 1)
            tt_(skip[:], tiles[:, 1, P - 1:P], tiles[:, 2, P - 1:P], ALU.add).then_inc(far_e_ready, 1)
            diff(i, 1)
            diff(i, 2)

        def far_scaled(i, p):
            dve.wait_ge(head_ready, c.due(head_ready, 2))
            dve.wait_ge(far_q_exp, c.due(far_q_exp, 7))
            q = one(hq_, i)
            tt_(far_k[:], head_k[p][:, 0:384].rearrange("p (j n) -> p j n", n=P), far_e[:], ALU.mult).then_inc(dve_step, 1)
            tt_(far_q[:, 0:384], far_q[:, 0:384], q[:, 128:512], ALU.mult).then_inc(dve_step, 1)
            tt_(far_q[:, 384:640], far_q[:, 384:640], q[:, 256:512], ALU.mult).then_inc(dve_step, 1)
            tt_(far_q[:, 640:768], far_q[:, 640:768], q[:, 384:512], ALU.mult).then_inc(far_ready, 1)
            dve.wait_ge(dve_step, c.due(dve_step, 3))

        def hgrn_head(i, p, last=False):
            top = len(LEVELS) - 1
            scaled(i, 1, p)
            dve.wait_ge(o_done, c.due(o_done, 1, back=1))
            select(0)
            for l in range(2, top + 1):
                scaled(i, l, p)
                dve.wait_ge(lev_ready, c.due(lev_ready, 2))
                if l < top:
                    diff(i, l + 1)
                select(l - 1)
            dve.wait_ge(lev_ready, c.due(lev_ready, 2))
            if not last:
                far_start(i + 1)
            select(top)
            if not last:
                far_scaled(i + 1, 1 - p)

        def hgrn_heads(i, last=False):
            hgrn_head(i * 2, 0)
            hgrn_head(i * 2 + 1, 1, last)
        far_start(0)
        far_scaled(0, 0)
        c.once(hgrn_heads, 0)
        c.loop(1, HG_HEADS // 2 - 1, hgrn_heads)
        c.once(hgrn_heads, HG_HEADS // 2 - 1, True)

        dve.wait_ge(cs_in, c.due(cs_in, 32))

        def turned_by_position(i):
            dve.wait_ge(ret_s_done, c.due(ret_s_done, 0))
            cos, sin = cos_sin[:, 0, :], cos_sin[:, 1, :]
            for n, (src, dst) in enumerate(((rq, rot_q), (rk, rot_k))):
                x1, x2 = one(src, i * 2), one(src, i * 2 + 1)
                for m, (f1, f2, op) in enumerate(((cos, sin, ALU.subtract), (sin, cos, ALU.add))):
                    tt_(rtmp[:, 0, :], x1, f1, ALU.mult).then_inc(dve_step, 1)
                    tt_(rtmp[:, 1, :], x2, f2, ALU.mult).then_inc(dve_step, 1)
                    dve.wait_ge(dve_step, c.due(dve_step, 2))
                    done = rot_ready if n == m == 1 else dve_step
                    tt_(dst[:, m, :], rtmp[:, 0, :], rtmp[:, 1, :], op).then_inc(done, 1)
                    dve.wait_ge(done, c.due(done))

        def ret_head(i, last=False):
            dve.wait_ge(ret_o_done, c.due(ret_o_done, 4, back=4))
            for j in range(TT):
                N = T - j * P
                dve.wait_ge(ret_s_done, c.due(ret_s_done))
                tt_(ratt[:, j * 512:j * 512 + N], bank[2 + j][:, 0:N], decay[:, bass.ds(i, 1), 0:N].rearrange("p a n -> p (a n)"),
                    ALU.mult).then_inc(ret_att, 1)
            dve.wait_ge(ret_att, c.due(ret_att, TT))
            if not last:
                turned_by_position(i + 1)
            dve.wait_ge(root_done, c.due(root_done))
            ve.reciprocal(tmp[:, 0, :], tmp[:, 0, :]).then_inc(dve_step, 1)
            dve.wait_ge(dve_step, c.due(dve_step))
            for m in range(4):
                o = rv[:, m, bass.ds(i * RET_DV, T)]
                done = normed if m == 3 else dve_step
                tt_(o, o, tmp[:, 0, :], ALU.mult).then_inc(done, 1)
            dve.wait_ge(dve_step, c.due(dve_step, 3))
            dve.wait_ge(normed, c.due(normed))

        def hg_norm(i):
            for p in range(2):
                n = i * 2 + p
                dve.wait_ge(root_done, c.due(root_done))
                ve.reciprocal(tmp[:, p, :], tmp[:, p, :]).then_inc(dve_step, 1)
                dve.wait_ge(dve_step, c.due(dve_step))
                gain = vec[:, bass.ds(n + VEC["hg_norm"][0], 1)]
                stt(one(hq_, n), one(hq_, n), gain, tmp[:, p, :], ALU.mult, ALU.mult).then_inc(normed, 1)
                dve.wait_ge(normed, c.due(normed))
        c.repeat(HG_HEADS // 2, hg_norm)
        turned_by_position(0)
        c.once(ret_head, 0)
        c.loop(1, RET_HEADS - 1, ret_head)
        c.once(ret_head, RET_HEADS - 1, True)

        c.base[acc_read_act.name] = ACT_READ["hg"]

        def hg_gate(i):
            for p in range(2):
                n = i * 2 + p
                dve.wait_ge(acc_read_act, c.due(acc_read_act))
                tt_(tmp[:, p, :], one(hq_, n), sq[:, p, :], ALU.mult).then_inc(dve_step, 1)
                dve.wait_ge(dve_step, c.due(dve_step))
                pair(one(oh_hi, n), one(oh_lo, n), tmp[:, p, :], gated)
        c.repeat(4, hg_gate)
        c.base[tile_done.name] = START["w_hg"]

        def branch_hg(i):
            for p in range(2):
                dve.wait_ge(tile_done, c.due(tile_done))
                g = one(ga, i * 2 + p)
                tt_(g, g, bank[p][:], ALU.mult).then_inc(acc_read_dve, 1)
                dve.wait_ge(acc_read_dve, c.due(acc_read_dve))
        c.repeat(4, branch_hg)
        for half in range(2):
            def ret_gate(i):
                for m in range(4):
                    dve.wait_ge(acc_read_act, c.due(acc_read_act))
                    o = rv[:, m, bass.ds((i + half * 2) * RET_DV, T)]
                    tt_(tmp[:, m % 2, :], o, sq[:, m % 2, :], ALU.mult).then_inc(dve_step, 1)
                    dve.wait_ge(dve_step, c.due(dve_step))
                    pair(one(or_hi, (i + half * 2) * 4 + m), one(or_lo[half], i * 4 + m), tmp[:, m % 2, :], gated)
            c.repeat(2, ret_gate)
        c.base[tile_done.name] = START["w_ret"]

        def merge(i):
            for p in range(2):
                n = i * 2 + p
                dve.wait_ge(tile_done, c.due(tile_done, 2))
                tt_(one(gb, n), one(gb, n), bank[p][:], ALU.mult).then_inc(acc_read_dve, 1)
                dve.wait_ge(acc_read_dve, c.due(acc_read_dve))
                tt_(tmp[:, p, :], one(ga, n), one(gb, n), ALU.add).then_inc(dve_step, 1)
                dve.wait_ge(dve_step, c.due(dve_step))
                pair(one(h_hi, n), one(h_lo, n), tmp[:, p, :], h_ready)
        c.repeat(4, merge)
        dve.wait_ge(x_in, c.due(x_in, 16))

        def to_residual(n):
            def two(i):
                for p in range(2):
                    dve.wait_ge(tile_done, c.due(tile_done))
                    r = one(resid, i * 2 + p)
                    tt_(r, r, bank[p][:], ALU.add).then_inc(acc_read_dve, 1)
                    dve.wait_ge(acc_read_dve, c.due(acc_read_dve))
            c.repeat(n // 2, two)
        to_residual(8)
        normed_pair("norm_ffn")

        NEG = -3.0e38

        def best16(rows):
            for values, top, index in rows:
                ve.max(top[:, 0:8], values).then_inc(dve_step, 1)
            dve.wait_ge(dve_step, c.due(dve_step, len(rows)))
            for values, top, index in rows:
                ve.max_index(index[:, 0:8], top[:, 0:8], values).then_inc(dve_step, 1)
            dve.wait_ge(dve_step, c.due(dve_step, len(rows)))
            for values, top, index in rows:
                ve.match_replace(values, top[:, 0:8], values, NEG).then_inc(dve_step, 1)
            dve.wait_ge(dve_step, c.due(dve_step, len(rows)))
            for values, top, index in rows:
                ve.max(top[:, 8:16], values).then_inc(dve_step, 1)
            dve.wait_ge(dve_step, c.due(dve_step, len(rows)))
            for values, top, index in rows:
                ve.max_index(index[:, 8:16], top[:, 8:16], values).then_inc(dve_step, 1)
            dve.wait_ge(dve_step, c.due(dve_step, len(rows)))

        def choose_halves(tt):
            dve.wait_ge(score_read, c.due(score_read, 4))
            best16([(scores[:, tt, n, :], top_s[:, n, :], top_u[:, n, :]) for n in range(16)])
            ve.tensor_copy(top_f[:], top_u[:]).then_inc(dve_step, 1)
            by_half = top_s[:].rearrange("p (h two) r -> p two h r", two=2)
            n = FULL_ROWS * TOPK
            for first, rows, width, part in ((0, FULL_ROWS, TOPK, cand[:, :, 0:n]), (FULL_ROWS, TOPK - FULL_ROWS, SHORT, cand[:, :, n:CANDS])):
                shape = (P, PEER_HEADS, rows, width)
                tt_(part.rearrange("p h (a b) -> p h a b", b=width), by_half[:, 0, :, first:first + rows].unsqueeze(3).to_broadcast(shape),
                    by_half[:, 1, :, 0:width].unsqueeze(2).to_broadcast(shape), ALU.add).then_inc(halves_done, 1)
            dve.wait_ge(dve_step, c.due(dve_step))
            dve.wait_ge(halves_done, c.due(halves_done, 2))

        def choose(tt):
            best16([(cand[:, h, :], best_s[:, h, :], best_u[:, h * TOPK:h * TOPK + TOPK]) for h in range(PEER_HEADS)])
            ve.tensor_copy(denom[:, 0, :], best_s[:, :, 0]).then_inc(dve_step, 1)
            for n, (op, amount) in enumerate(((ALU.logical_shift_right, 4), (ALU.bitwise_and, TOPK - 1),
                                              (ALU.logical_shift_right, 2), (ALU.bitwise_and, SHORT - 1))):
                ts(place_u[:, n, :], best_u[:], amount, None, op).then_inc(dve_step, 1)
            dve.wait_ge(dve_step, c.due(dve_step, 5))
            ts(best_u[:], best_u[:], 6, None, ALU.logical_shift_right).then_inc(dve_step, 1)
            tt_(best_s[:], best_s[:], denom[:, 0, :].unsqueeze(2).to_broadcast((P, PEER_HEADS, TOPK)), ALU.subtract).then_inc(best_shifted, 1)
            ve.tensor_copy(place_f[:], place_u[:]).then_inc(dve_step, 1)
            dve.wait_ge(dve_step, c.due(dve_step, 2))
            ve.tensor_copy(low_f[:], best_u[:]).then_inc(dve_step, 1)
            ts(place_f[:, 2, :], place_f[:, 2, :], -(FULL_ROWS * TOPK // SHORT - FULL_ROWS), None, ALU.add).then_inc(dve_step, 1)
            dve.wait_ge(dve_step, c.due(dve_step, 2))
            tt_(place_f[:, 2:4, :], place_f[:, 2:4, :], place_f[:, 0:2, :], ALU.subtract).then_inc(dve_step, 1)
            dve.wait_ge(dve_step, c.due(dve_step))
            tt_(place_f[:, 2:4, :], place_f[:, 2:4, :], low_f[:].unsqueeze(1).to_broadcast((P, 2, CHOICES)), ALU.mult).then_inc(dve_step, 1)
            dve.wait_ge(dve_step, c.due(dve_step))
            tt_(row_f[:], place_f[:, 0:2, :], place_f[:, 2:4, :], ALU.add).then_inc(dve_step, 1)
            dve.wait_ge(dve_step, c.due(dve_step))
            keys_by_half = top_f[:].rearrange("p (h two) r -> p two h r", two=2)
            shape = (P, PEER_HEADS, TOPK, TOPK)
            for n in range(2):
                p3 = pick[:]
                p4 = pick[:].rearrange("p (h k) r -> p h k r", k=TOPK)
                tt_(p3, row_f[:, n, :].unsqueeze(2).to_broadcast((P, CHOICES, TOPK)),
                    t_("iota16").unsqueeze(1).to_broadcast((P, CHOICES, TOPK)), ALU.is_equal).then_inc(dve_step, 1)
                dve.wait_ge(dve_step, c.due(dve_step))
                tt_(p4, p4, keys_by_half[:, n].unsqueeze(2).to_broadcast(shape), ALU.mult).then_inc(dve_step, 1)
                dve.wait_ge(dve_step, c.due(dve_step))
                ve.tensor_reduce(chosen[:, n, :], p3, AX.X, ALU.add).then_inc(dve_step, 1)
                dve.wait_ge(dve_step, c.due(dve_step))
            dve.wait_ge(best_exp, c.due(best_exp))
            ve.tensor_reduce(denom[:, 0, :], best_s[:], AX.X, ALU.add).then_inc(dve_step, 1)
            dve.wait_ge(dve_step, c.due(dve_step))
            ve.reciprocal(denom[:, 1, :], denom[:, 0, :]).then_inc(dve_step, 1)
            dve.wait_ge(dve_step, c.due(dve_step))
            tt_(chosen[:, 2, :].rearrange("p (h k) -> p h k", k=TOPK), best_s[:],
                denom[:, 1, :].unsqueeze(2).to_broadcast((P, PEER_HEADS, TOPK)), ALU.mult).then_inc(chosen_done, 1)

        def one_hots(lot):
            def batches(i):
                for p in range(HOTS):
                    dve.wait_ge(batch_done, c.due(batch_done, 1, back=HOTS))
                    at = bass.ds((lot % LOTS) * STAGED_TOKENS + (i * HOTS + p) * TOKENS_PER_BATCH, TOKENS_PER_BATCH)
                    big = (P, TOKENS_PER_BATCH, NKEYS)
                    for key, hot in ((1, hot2), (0, hot1)) if p < HOTS - 1 else ((0, hot1),):
                        tt_(hot[:, p], chosen_t[:, key, at].unsqueeze(2).to_broadcast(big),
                            t_("iota128").unsqueeze(1).to_broadcast(big), ALU.is_equal).then_inc(hot_ready, 1)
            c.repeat(LOT_BATCHES // HOTS, batches)
        choose_halves(0)
        choose(0)
        for lot in range(TT * LOTS):
            tt = lot // LOTS
            if lot % LOTS == 0:
                dve.wait_ge(turned, c.due(turned))
                if tt:
                    dve.wait_ge(hot_gated, c.due(hot_gated, P // TOKENS_PER_BATCH))
                    dve.wait_ge(last_hot, c.due(last_hot, P // TOKENS_PER_BATCH // HOTS))
                else:
                    dve.wait_ge(score_read, c.due(score_read, 0) + 4 * (TT - 1))
                ve.tensor_copy(chosen_t[:], bank[6][:, 0:3 * P].rearrange("p (a n) -> p a n", n=P)).then_inc(choices_here, 1)
                dve.wait_ge(choices_here, c.due(choices_here))
            one_hots(lot)
            if tt + 1 < TT:
                if lot % LOTS == 0:
                    choose_halves(tt + 1)
                else:
                    choose(tt + 1)

        c.base[acc_read_act.name] = ACT_READ["experts"]
        c.base[tile_done.name] = START["experts"]

        def weigh(i):
            for s in range(4):
                dve.wait_ge(acc_read_act, c.due(acc_read_act))
                dve.wait_ge(gate_in[s], c.due(gate_in[s], 16))
                e = one(expert_w, i * 4 + s)
                tt_(e, e, g_in[:, s, :], ALU.mult).then_inc(weighted, 1)

        def low_parts(i):
            for e in range(4):
                dve.wait_ge(ew_hi_ready, c.due(ew_hi_ready))
                tt_(ew_lo[:, e % 2, :], one(expert_w, i * 4 + e), f32(ew_hi[:, e % 2, :]), ALU.subtract).then_inc(ew_ready, 1)

        def add_values(half):
            dve.wait_ge(tile_done, c.due(tile_done, GROUP // 2))
            for m in range(4):
                r = resid[:, half * 4 + m, :]
                tt_(r, r, bank[half * 4 + m][:], ALU.add).then_inc(x_added, 1)

        dve.wait_ge(tile_done, c.due(tile_done, GROUP))

        def weigh_and_split(i):
            weigh(i)
            dve.wait_ge(weighted, c.due(weighted, 4))
            low_parts(i)
        def second_half():
            c.once(low_parts, 0)
            add_values(0)
            c.once(low_parts, 1)
            c.loop(2, GROUP // 4, low_parts)
            add_values(1)
        c.repeat(GROUP // 4, weigh_and_split)
        second_half()

        def group(g):
            c.repeat(GROUP // 4, weigh)
            dve.wait_ge(weighted, c.due(weighted, GROUP))
            dve.wait_ge(tile_done, c.due(tile_done, GROUP))
            c.repeat(GROUP // 4, low_parts)
            second_half()
        c.once(group, 1)
        c.loop(2, NKEYS // GROUP, group)
        dve.wait_ge(x_added, c.due(x_added, 8 * (NKEYS // GROUP)))
        inverse_root()
        for k in range(KT):
            stt(resid[:, k, :], resid[:, k, :], v("final", k), rstd[:], ALU.mult, ALU.mult).then_inc(resid_ready, 1)
        dve.wait_ge(resid_ready, c.due(resid_ready, KT))

        normed_pair("norm1")
        lam, u, z, z2, s = v("lam", 0, 4), tiny[:, 0:4], tiny[:, 4:8], tiny[:, 8:12], tiny[:, 12:16]
        ts(z, lam, -1.0, None, ALU.mult).then_inc(dve_step, 1)
        dve.wait_ge(dve_step, c.due(dve_step))
        tt_(z, z, lam, ALU.min).then_inc(lam_abs, 1)
        dve.wait_ge(lam_abs, c.due(lam_abs))
        dve.wait_ge(lam_exp, c.due(lam_exp))
        ts(z2, u, 2.0, None, ALU.add).then_inc(dve_step, 1)
        dve.wait_ge(dve_step, c.due(dve_step))
        ve.reciprocal(z2, z2).then_inc(dve_step, 1)
        dve.wait_ge(dve_step, c.due(dve_step))
        tt_(z, u, z2, ALU.mult).then_inc(dve_step, 1)
        dve.wait_ge(dve_step, c.due(dve_step))
        tt_(z2, z, z, ALU.mult).then_inc(dve_step, 1)
        dve.wait_ge(dve_step, c.due(dve_step))
        ts(s, z2, 1.0 / 17, 1.0 / 15, ALU.mult, ALU.add).then_inc(dve_step, 1)
        dve.wait_ge(dve_step, c.due(dve_step))
        for odd in (13, 11, 9, 7, 5, 3, 1):
            tt_(s, s, z2, ALU.mult).then_inc(dve_step, 1)
            dve.wait_ge(dve_step, c.due(dve_step))
            ts(s, s, 1.0 / odd, None, ALU.add).then_inc(dve_step, 1)
            dve.wait_ge(dve_step, c.due(dve_step))
        tt_(s, s, z, ALU.mult).then_inc(dve_step, 1)
        dve.wait_ge(dve_step, c.due(dve_step))
        ts(u, lam, -1.0, 0.0, ALU.mult, ALU.max).then_inc(dve_step, 1)
        dve.wait_ge(dve_step, c.due(dve_step))
        stt(s, s, 2.0, u, ALU.mult, ALU.add).then_inc(dve_step, 1)
        dve.wait_ge(dve_step, c.due(dve_step))
        ts(tiny[:, 48:52], s, 8.0, None, ALU.mult).then_inc(dve_step, 1)
        dve.wait_ge(dve_step, c.due(dve_step))
        qk = v("lam_qk", 0, 128).rearrange("p (a n) -> p a n", n=32)
        tt_(tmp[:, 0, 0:64].rearrange("p (a n) -> p a n", n=32), qk[:, 0::2, :], qk[:, 1::2, :], ALU.mult).then_inc(dve_step, 1)
        dve.wait_ge(dve_step, c.due(dve_step))
        ve.tensor_reduce(tiny[:, 56:58], tmp[:, 0, 0:64].rearrange("p (a n) -> p a n", n=32), AX.X, ALU.add).then_inc(dve_step, 1)
        dve.wait_ge(dve_step, c.due(dve_step))
        ts(tiny[:, 52:56], s, -8.0, None, ALU.mult).then_inc(softplus_done, 1)
        dve.wait_ge(softplus_done, c.due(softplus_done))
        c.base[acc_read_act.name] = ACT_READ["in_2"]

        def lru_conv(n):
            xa, y = in2[:, n, :], lru[n % 2]
            dve.wait_ge(acc_read_act, c.due(acc_read_act))
            ts(y[:], xa, v("conv_a_w", 12 + n), v("conv_a_b", n), ALU.mult, ALU.add).then_inc(dve_step, 1)
            dve.wait_ge(dve_step, c.due(dve_step))
            for back in (1, 2):
                stt(y[:, back:T], xa[:, 0:T - back], v("conv_a_w", (3 - back) * 4 + n), y[:, back:T], ALU.mult, ALU.add).then_inc(dve_step, 1)
                dve.wait_ge(dve_step, c.due(dve_step))
            stt(y[:, 3:T], xa[:, 0:T - 3], v("conv_a_w", n), y[:, 3:T], ALU.mult, ALU.add).then_inc(conv_done, 1)
            dve.wait_ge(conv_done, c.due(conv_done))

        def lru_state(n):
            y = lru[n % 2]
            gate_r, u, decay_, root = lru[2], lru[3], lru[4], lru[5]
            dve.wait_ge(lru_decays, c.due(lru_decays, 2))
            tt_(gate_r[:], decay_[:], decay_[:], ALU.mult).then_inc(dve_step, 1)
            dve.wait_ge(dve_step, c.due(dve_step))
            stt(root[:], gate_r[:], 1.0, root[:], ALU.add, ALU.mult).then_inc(lru_var, 1)
            tt_(u[:], u[:], y[:], ALU.mult).then_inc(dve_step, 1)
            dve.wait_ge(dve_step, c.due(dve_step))
            if n + 2 < LRU_TILES:
                lru_conv(n + 2)
            dve.wait_ge(lru_root, c.due(lru_root))
            tt_(u[:], u[:], root[:], ALU.mult).then_inc(dve_step, 1)
            dve.wait_ge(dve_step, c.due(dve_step))
            ve.tensor_tensor_scan(gate_r[:], decay_[:], u[:], 0.0, ALU.mult, ALU.add).then_inc(dve_step, 1)
            dve.wait_ge(dve_step, c.due(dve_step))
            dve.wait_ge(lru_gelu, c.due(lru_gelu))
            tt_(gate_r[:], gate_r[:], in2[:, 4 + n, :], ALU.mult).then_inc(dve_step, 1)
            dve.wait_ge(dve_step, c.due(dve_step))
            pair(mix_hi[:, n, :], mix_lo[:, n, :], gate_r[:], mixed_ready)
        lru_conv(0)
        lru_conv(1)
        for n in range(LRU_TILES):
            lru_state(n)
        dve.wait_ge(lam_ready, c.due(lam_ready))
        dve.wait_ge(distance_in, c.due(distance_in, 16))
        tt_(tiny[:, 60:61], tiny[:, 58:59], tiny[:, 59:60], ALU.subtract).then_inc(dve_step, 1)
        dve.wait_ge(dve_step, c.due(dve_step))
        ts(tiny[:, 60:61], tiny[:, 60:61], LAM_INIT, -1.0, ALU.add, ALU.mult).then_inc(dve_step, 1)
        dve.wait_ge(dve_step, c.due(dve_step))

        def sb_logits(h):
            for j in range(TT):
                N = T - j * P
                dve.wait_ge(sb_z_done, c.due(sb_z_done))
                ts(sbz[h % 2][:, j, 0:N], bank[j % 2][:, 0:N], SB_DH ** -0.5, None, ALU.mult).then_inc(sb_z_read, 1)
            dve.wait_ge(sb_z_read, c.due(sb_z_read, TT))

        def sb_softplus(h):
            z = sbz[h % 2]
            dve.wait_ge(sb_o_done, c.due(sb_o_done, 1, back=1))
            for j in range(TT):
                N = T - j * P
                dve.wait_ge(sb_ln, c.due(sb_ln))
                stt(sbw[:, j, 0:N], z[:, j, 0:N], 0.0, sbt[:, j, 0:N], ALU.max, ALU.add).then_inc(dve_step, 1)
            dve.wait_ge(dve_step, c.due(dve_step, TT))
            for j in range(TT):
                N = T - j * P
                tt_(z[:, j, 0:N], z[:, j, 0:N], sbw[:, j, 0:N], ALU.subtract).then_inc(dve_step, 1)
            dve.wait_ge(dve_step, c.due(dve_step, TT))
            for j in range(TT):
                tt_(sbw[:, j, 0:P], sbw[:, j, 0:P], t_("earlier"), ALU.mult).then_inc(sb_sp_ready, 1)
            dve.wait_ge(sb_sp_ready, c.due(sb_sp_ready, TT))

        def sb_tails(h):
            z = sbz[h % 2]
            for j in range(TT):
                N = T - j * P
                dve.wait_ge(sb_tail_done, c.due(sb_tail_done))
                tt_(z[:, j, 0:N], z[:, j, 0:N], bank[j % 2][:, 0:N], ALU.subtract).then_inc(sb_tail_read, 1)

        def sb_weights():
            for j in range(TT):
                dve.wait_ge(sb_exp, c.due(sb_exp))
                tt_(sbw[:, j, 0:P], sbw[:, j, 0:P], t_("earlier"), ALU.mult).then_inc(sb_w_ready, 1)

        def sb_out(pair_):
            dve.wait_ge(sb_o_done, c.due(sb_o_done, 0))
            ve.tensor_copy(mix_hi[:, 4 + pair_, :], bank[6][:]).then_inc(dve_step, 1)
            dve.wait_ge(dve_step, c.due(dve_step))
            tt_(mix_lo[:, 4 + pair_, :], bank[6][:], f32(mix_hi[:, 4 + pair_, :]), ALU.subtract).then_inc(sb_o_read, 1)

        stat = [df_stat[:, k:k + 1] for k in range(16)]

        def df_logits(h, i):
            slope = 2.0 ** (-8.0 * (h + 1) / DF_HEADS) * DF_DQK ** 0.5
            N = (i + 1) * P
            if i:
                dve.wait_ge(df_exp, c.due(df_exp, 2))
            for q in range(2):
                dve.wait_ge(df_s_done, c.due(df_s_done))
                stt(dfs[:, q, 0:N], distance[:, T - N:T], -slope, bank[2 + q][:, 0:N], ALU.mult, ALU.add).then_inc(df_s_read, 1)
            dve.wait_ge(df_s_read, c.due(df_s_read, 2))
            for q in range(2):
                ve.reduce_max(stat[q], dfs[:, q, 0:N], AX.X).then_inc(dve_step, 1)
            dve.wait_ge(dve_step, c.due(dve_step, 2))
            for q in range(2):
                ts(stat[2 + q], stat[q], -(DF_DQK ** -0.5), None, ALU.mult).then_inc(df_max, 1)

        def df_maps(i):
            N = (i + 1) * P
            if i == TT - 1:
                dve.wait_ge(df_exp, c.due(df_exp, 2))
            e, total = dfe[i % 2], 4 + 2 * (i % 2)
            ve.reciprocal(df_stat[:, 8:10], df_stat[:, total:total + 2]).then_inc(dve_step, 1)
            dve.wait_ge(dve_step, c.due(dve_step))
            dve.wait_ge(df_pt_done, c.due(df_pt_done, 1, back=1))
            tt_(stat[10], stat[9], tiny[:, 60:61], ALU.mult).then_inc(dve_step, 1)
            ts(dfp[:, 0:N], e[:, 0, 0:N], stat[8], None, ALU.mult).then_inc(dve_step, 1)
            dve.wait_ge(dve_step, c.due(dve_step, 2))
            stt(dfp[:, 0:N], e[:, 1, 0:N], stat[10], dfp[:, 0:N], ALU.mult, ALU.add).then_inc(df_p_ready, 1)
            dve.wait_ge(df_p_ready, c.due(df_p_ready))

        def df_normed(pair_):
            inverse_root()
            n = 6 + pair_
            o = dfo[:, pair_, :]
            stt(o, o, v("subln"), rstd[:], ALU.mult, ALU.mult).then_inc(dve_step, 1)
            dve.wait_ge(dve_step, c.due(dve_step))
            ts(o, o, 1.0 - LAM_INIT, None, ALU.mult).then_inc(dve_step, 1)
            dve.wait_ge(dve_step, c.due(dve_step))
            pair(mix_hi[:, n, :], mix_lo[:, n, :], o, mixed_ready)
        sb_logits(0)
        for h in range(SB_HEADS):
            sb_softplus(h)
            df_logits(h, 0)
            sb_tails(h)
            df_logits(h, 1)
            df_maps(0)
            sb_weights()
            df_logits(h, 2)
            df_maps(1)
            df_logits(h, 3)
            if h + 1 < SB_HEADS:
                sb_logits(h + 1)
            df_maps(2)
            if h == 2:
                df_normed(0)
            df_maps(3)
            if h % 2:
                sb_out(h // 2)
        df_normed(1)
        c.base[tile_done.name] = START["out_2"]
        to_residual(8)
        normed_pair("norm2")

        def ff(i):
            for p in range(2):
                dve.wait_ge(tile_done, c.due(tile_done))
                n = i * 2 + p
                w = [vec[:, bass.ds(n + VEC["conv_ff_w"][0] + k * 2 * FF_TILES, 1)] for k in range(3)]
                b = vec[:, bass.ds(n + VEC["conv_ff_b"][0], 1)]
                acc, y = bank[p], conv[:, p, :]
                if p == 0:
                    dve.wait_ge(ff_silu, c.due(ff_silu, 1, back=1))
                ts(y, acc[:], w[2], b, ALU.mult, ALU.add).then_inc(dve_step, 1)
                dve.wait_ge(dve_step, c.due(dve_step))
                stt(y[:, 1:T], acc[:, 0:T - 1], w[1], y[:, 1:T], ALU.mult, ALU.add).then_inc(dve_step, 1)
                dve.wait_ge(dve_step, c.due(dve_step))
                stt(y[:, 2:T], acc[:, 0:T - 2], w[0], y[:, 2:T], ALU.mult, ALU.add).then_inc(acc_read_dve, 1)
                dve.wait_ge(acc_read_dve, c.due(acc_read_dve))
            dve.wait_ge(ff_silu, c.due(ff_silu, 0))
            tt_(tmp[:, 0, :], act_g[:, 0, :], conv[:, 1, :], ALU.mult).then_inc(dve_step, 1)
            dve.wait_ge(dve_step, c.due(dve_step))
            pair(one(ff_hi, i), one(ff_lo, i), tmp[:, 0, :], ff_ready)
        c.repeat(FF_TILES, ff)
        dve.wait_ge(tile_done, c.due(tile_done, FF_TILES))
        for n in range(KT):
            tt_(resid[:, n, :], resid[:, n, :], bank[n][:], ALU.add).then_inc(down_read, 1)
        inverse_root()
        for k in range(KT):
            stt(final[:, k, :], resid[:, k, :], v("final2", k), rstd[:], ALU.mult, ALU.mult).then_inc(final_done, 1)

    block.__exit__(None, None, None)


def tables_of_shapes():
    f = np.float32
    tab = np.zeros((P, N_TAB), f)

    def put(name, value):
        tab[:, TAB[name][0]:TAB[name][0] + TAB[name][1]] = value
    p, q = np.arange(P)[:, None], np.arange(P)[None, :]
    put("identity", p == q)
    put("later", p > q)
    put("earlier", p < q)
    put("halves", p // 64 == q // 64)
    u = np.arange(T)[None, :] - (T - P)
    put("distance", np.where((u // 64) <= (p // 64), np.abs(p - u), 1e30))
    put("iota16", np.arange(16)[None, :])
    put("iota128", q)
    put("scan_keep", np.arange(T)[None, :] % P != 0)
    half = RET_DK // 2
    inv = f(10000.0) ** (-np.arange(half, dtype=f) / f(half))
    angle = inv[:, None] * np.arange(T, dtype=f)[None, :]
    put("cos", np.cos(angle))
    put("sin", np.sin(angle))
    log_g = np.log(f(1.0) - np.exp2(f(-5.0) - np.arange(RET_HEADS, dtype=f)))
    rel = np.arange(T, dtype=f)[None, :] - np.arange(P, dtype=f)[:, None]
    put("decay", np.concatenate([np.where(rel >= 0, np.exp(log_g[h] * np.maximum(rel, 0)), 0) for h in range(RET_HEADS)], axis=1))
    masks = np.zeros((P, len(LEVELS), P), f)
    for n, w in enumerate(LEVELS):
        if w == 0:
            masks[:, n] = p == q
        else:
            masks[:, n] = (p // (2 * w) == q // (2 * w)) & (p % (2 * w) < w) & (q % (2 * w) >= w)
    put("levels", masks.reshape(P, -1))
    return tab


def kernel(**inputs):
    import concourse.bacc as bacc
    from concourse.bass_utils import run_bass_kernel_spmd

    a = {k: np.asarray(v) for k, v in inputs.items()}

    def fm(w, n=None):
        k, n = w.shape
        t = w.reshape(k // P, P, n // P, P).transpose(2, 1, 0, 3)
        return t.reshape(n // P, P, k // 1024, 1024).transpose(0, 2, 1, 3).reshape(-1, P, 1024)

    def tm(w):
        k, n = w.shape
        return w.reshape(4, 2, P, n // 512, 512).transpose(3, 0, 2, 1, 4).reshape(-1, P, 1024)

    def cols(t):
        return t.reshape(-1, P).T

    w_in = a["w_in"][0]
    at = np.cumsum([0, 1024, 1024, 1024, 1024, 1024, 1024, 2048, 2048, 1024, 1024])
    hq, hf, hi, hg, rq, rk, rv, rg, gate_a, gate_b = (w_in[:, at[n]:at[n + 1]] for n in range(10))
    w2 = a["w_in_2"][0]
    at = np.cumsum([0, 512, 512, 256, 256, 256, 256, 256, 256])
    xa, ya, sq, sk, sv, dq, dk, dv = (w2[:, at[n]:at[n + 1]] for n in range(8))
    u_tiles = a["expert_u"][0].reshape(NKEYS, P, KT, P).transpose(0, 3, 2, 1).reshape(NKEYS // GROUP, GROUP, P, 1024)
    v_tiles = a["expert_v"][0].reshape(NKEYS // GROUP, GROUP // 2, 2, P, 2, 512).transpose(0, 4, 1, 3, 2, 5).reshape(
        NKEYS // GROUP, GROUP, P, 1024)
    experts = np.concatenate([u_tiles, v_tiles], axis=1).reshape(-1, P, 1024)
    up = fm(a["w_ff_up_2"][0]).reshape(2, FF_TILES, P, 1024).transpose(1, 0, 2, 3).reshape(-1, P, 1024)
    branch_gates = np.stack([fm(gate_a).reshape(RET_HEADS, 2, P, 1024), fm(gate_b).reshape(RET_HEADS, 2, P, 1024)],
                            axis=1).reshape(-1, P, 1024)
    rqk = np.stack([fm(rq), fm(rk)], axis=1).reshape(-1, P, 1024)
    weights = np.concatenate([
        fm(hf), fm(hq), tm(hi), rqk, tm(rv), branch_gates, fm(hg), fm(a["w_branch_hg"][0]), fm(rg),
        fm(a["w_branch_ret"][0]), fm(a["w_out"][0]), fm(a["peer_w_q"][0]), experts,
        fm(np.concatenate([xa, ya] + [t[:, :P] for t in (sq, sk, dq, dk)], axis=1)), tm(np.concatenate([sv, dv], axis=1)),
        fm(np.concatenate([t[:, P:] for t in (sq, sk, dq, dk)], axis=1)), fm(a["w_out_2"][0]),
        up, a["w_ff_down_2"][0].reshape(FF_TILES, P, 1024)])
    conv_w = a["conv_ff_w_2"][0].reshape(3, 2, FF_TILES, P).transpose(3, 0, 2, 1).reshape(P, -1)
    conv_b = a["conv_ff_b_2"][0].reshape(2, FF_TILES, P).transpose(2, 1, 0).reshape(P, -1)
    lam_qk = np.concatenate([a[f"lam_{n}_2"][0] for n in ("q1", "k1", "q2", "k2")])
    vectors = np.concatenate([
        cols(a["norm_mix_w"]), cols(a["hg_lower_bounds"]), cols(a["hg_norm_w"]), cols(a["norm_ffn_w"]),
        cols(a["final_norm_w"]), cols(a["norm1_g_2"]), cols(a["conv_a_w_2"]), cols(a["conv_a_b_2"]),
        cols(a["b_rgate_2"]), cols(a["b_igate_2"]), cols(a["lru_lambda_2"]),
        np.tile(a["subln_g_2"][0], 2)[:, None], cols(a["norm2_g_2"]), conv_w, conv_b, cols(a["final_g_2"]),
        np.broadcast_to(lam_qk, (P, 128))], axis=1)
    gates_2 = np.zeros((P, 8, P), np.float32)
    for g, name in enumerate(("w_rgate_2", "w_igate_2")):
        for n in range(8):
            r = 64 * (n % 2)
            gates_2[r:r + 64, g * 4 + n // 2, r:r + 64] = a[name][0, n]
    tab = tables_of_shapes()
    arrays = {
        "x": a["x"][0].T.reshape(KT, P, T).transpose(1, 0, 2),
        "weights": weights,
        "vectors": vectors,
        "tables": tab,
        "keys": a["peer_sub_keys"][0].reshape(16, NKEYS, P).transpose(2, 0, 1),
        "lru_gates": gates_2,
    }
    nc = bacc.Bacc("TRN2", target_bir_lowering=False, num_devices=1)
    arrays = {k: np.ascontiguousarray(v) for k, v in arrays.items()}
    aps = {k: nc.dram_tensor(k, v.shape, mybir.dt.from_np(v.dtype), kind="ExternalInput").ap() for k, v in arrays.items()}
    out = nc.dram_tensor("out", (P, KT, T), F32, kind="ExternalOutput").ap()
    build(nc, **aps, out=out)
    got = run_bass_kernel_spmd(nc, [arrays], core_ids=[0]).results[0]["out"]
    return np.ascontiguousarray(got.transpose(2, 1, 0).reshape(1, T, D))
```
